# Optimizing a Trainium2 kernel written in Bass

```python
import math
import jax, jax.numpy as jnp
from jax import lax
import numpy as np

D_MODEL = 1024
BATCH = 1
SEQ = 128
DEPTH = 2
DEC_BATCH = 1
DEC_SEQ = 512
PAST_LEN = 256

GRID_W = 64
HEAD_DIM = 64
W_A = D_MODEL // 4
W_B = D_MODEL // 2
W_C = D_MODEL - W_A - W_B
H_A = W_A // HEAD_DIM
HD_A = HEAD_DIM
RWKV_DECAY_LORA = 64
RWKV_ICLR_LORA = 64
RWKV_GATE_LORA = 128
DECAY_SCALE = 0.606531
H_B = W_B // HEAD_DIM
DV = HEAD_DIM
DK = HEAD_DIM // 2
ROPE_PAIRS = DK // 4
ROPE_BASE = 10000.0
Q_BLOCK = 128
LRU_BW = HEAD_DIM
LRU_BLOCKS = W_C // LRU_BW
CONV_W = 4
CONV_LEFT = 2
LRU_C = 8.0
PEER_HEADS = 8
PEER_N_KEYS = 128
PEER_TOPK = 16
PEER_DQ = 256
N_EXPERTS = PEER_N_KEYS ** 2
PEER_BLOCK = 128
D_IN = 3 * W_A + 3 * W_B + 2 * W_C
SPLIT_POINTS = (W_A, 2 * W_A, 3 * W_A, 3 * W_A + W_B, 3 * W_A + 2 * W_B, 3 * W_A + 3 * W_B, 3 * W_A + 3 * W_B + W_C)
RMS_EPS = 1e-6
GN_EPS = 64e-5

kernel_name = 'hybrid_diffusion_rwkv7_diffattn_rglru_peer_step'

def rmsnorm(x, g, eps=RMS_EPS):
    xf = x.astype(jnp.float32)
    y = xf * lax.rsqrt(jnp.mean(xf * xf, axis=-1, keepdims=True) + eps)
    return (y * g.astype(jnp.float32)).astype(x.dtype)

def head_layernorm(x, g, eps=GN_EPS):
    xf = x.astype(jnp.float32)
    mu = jnp.mean(xf, axis=-1, keepdims=True)
    var = jnp.mean(jnp.square(xf - mu), axis=-1, keepdims=True)
    return ((xf - mu) * lax.rsqrt(var + eps) * g.astype(jnp.float32)).astype(x.dtype)

def l2_normalize(x):
    xf = x.astype(jnp.float32)
    return (xf * lax.rsqrt(jnp.maximum(jnp.sum(xf * xf, axis=-1, keepdims=True), 1e-12))).astype(x.dtype)

def adaln_params(cond, w, b):
    m = jax.nn.silu(cond) @ w + b
    return jnp.split(m[:, None, :], 6, axis=-1)

def axial_rope_tables(T):
    rows = T // GRID_W
    row = jnp.repeat(jnp.arange(rows), GRID_W).astype(jnp.float32)
    col = jnp.tile(jnp.arange(GRID_W), rows).astype(jnp.float32)
    inv = ROPE_BASE ** (-jnp.arange(ROPE_PAIRS, dtype=jnp.float32) / ROPE_PAIRS)
    ang = jnp.concatenate([row[:, None] * inv, col[:, None] * inv], axis=-1)
    return jnp.cos(ang), jnp.sin(ang)

def apply_axial_rope(x, cos, sin):
    x1 = x[..., 0::2]
    x2 = x[..., 1::2]
    c = cos[None, :, None, None, :].astype(x.dtype)
    s = sin[None, :, None, None, :].astype(x.dtype)
    return jnp.stack([x1 * c - x2 * s, x1 * s + x2 * c], axis=-1).reshape(x.shape)

def blocked_diff_attention(q, k, v, lam):
    B, H, Sq = q.shape[:3]
    nb = Sq // Q_BLOCK
    qb = jnp.moveaxis(q.reshape(B, H, nb, Q_BLOCK, 2, DK), 2, 0)
    scale = DK ** -0.5

    def one_block(qi):
        s = jnp.einsum('bhqcd,bhkcd->bhcqk', qi, k).astype(jnp.float32) * scale
        p = jax.nn.softmax(s, axis=-1)
        p = p[:, :, 0] - lam * p[:, :, 1]
        return jnp.einsum('bhqk,bhkd->bhqd', p.astype(v.dtype), v)

    o = lax.map(one_block, qb)
    return jnp.moveaxis(o, 0, 2).reshape(B, H, Sq, DV)

def rwkv7_scan(r, w, k, v, kk, a, s0, reverse):
    xs = (jnp.swapaxes(r, 0, 1), jnp.swapaxes(w, 0, 1), jnp.swapaxes(k, 0, 1),
          jnp.swapaxes(v, 0, 1), jnp.swapaxes(kk, 0, 1), jnp.swapaxes(a, 0, 1))

    def step(S, inp):
        r_t, w_t, k_t, v_t, kk_t, a_t = inp
        sa = jnp.einsum('bhij,bhj->bhi', S, -kk_t)
        S = (S * w_t[:, :, None, :] + sa[..., None] * (kk_t * a_t)[:, :, None, :]
             + v_t[..., None] * k_t[:, :, None, :])
        return S, jnp.einsum('bhij,bhj->bhi', S, r_t)

    s_last, o = lax.scan(step, s0, xs, reverse=reverse)
    return jnp.swapaxes(o, 0, 1), s_last

def rwkv7_mixer(h, r, k, v, lp, s0):
    B, T, _ = h.shape
    shp = (B, T, H_A, HD_A)
    rh = r.reshape(shp)
    kh = k.reshape(shp)
    vh = v.reshape(shp)
    kk = l2_normalize((k * lp['rwkv_kk']).reshape(shp))
    o_sum = None
    states = []
    for d in range(2):
        w = jnp.exp(-DECAY_SCALE * jax.nn.sigmoid(lp['rwkv_w0'][d] + jnp.tanh(h @ lp['rwkv_wA'][d]) @ lp['rwkv_wB'][d]))
        a = jax.nn.sigmoid(lp['rwkv_a0'][d] + (h @ lp['rwkv_aA'][d]) @ lp['rwkv_aB'][d])
        kd = k * (1.0 + (a - 1.0) * lp['rwkv_ka'])
        o, s_last = rwkv7_scan(rh, w.reshape(shp), kd.reshape(shp), vh, kk, a.reshape(shp), s0[:, d], reverse=(d == 1))
        o_sum = o if o_sum is None else o_sum + o
        states.append(s_last)
    o = head_layernorm(o_sum, lp['rwkv_ln_g'].reshape(H_A, HD_A))
    bonus = jnp.sum(rh * kh * lp['rwkv_rk'], axis=-1, keepdims=True) * vh
    g = jax.nn.sigmoid(h @ lp['rwkv_gA']) @ lp['rwkv_gB']
    out = (o + bonus).reshape(B, T, W_A) * g
    return out, jnp.stack(states, axis=1)

def diff_attention_mixer(q, k, v, lp, lam_init, rope, ctx_k, ctx_v):
    B, T, _ = q.shape
    qh = q.reshape(B, T, H_B, 2, DK)
    kh = k.reshape(B, T, H_B, 2, DK)
    vh = v.reshape(B, T, H_B, DV)
    if rope is not None:
        cos, sin = rope
        qh = apply_axial_rope(qh, cos, sin)
        kh = apply_axial_rope(kh, cos, sin)
    k_new = jnp.transpose(kh.reshape(B, T, H_B, 2 * DK), (0, 2, 1, 3))
    v_new = jnp.transpose(vh, (0, 2, 1, 3))
    if ctx_k is None:
        k_all, v_all = k_new, v_new
    else:
        k_all = jnp.concatenate([ctx_k, k_new], axis=2)
        v_all = jnp.concatenate([ctx_v, v_new], axis=2)
    Sk = k_all.shape[2]
    f32 = jnp.float32
    lam = (jnp.exp(jnp.sum(lp['diff_lq1'].astype(f32) * lp['diff_lk1'].astype(f32)))
           - jnp.exp(jnp.sum(lp['diff_lq2'].astype(f32) * lp['diff_lk2'].astype(f32))) + lam_init)
    o = blocked_diff_attention(jnp.transpose(qh, (0, 2, 1, 3, 4)), k_all.reshape(B, H_B, Sk, 2, DK), v_all, lam)
    o = rmsnorm(o, lp['diff_subln_g'], eps=1e-5) * (1.0 - lam_init)
    out = jnp.transpose(o, (0, 2, 1, 3)).reshape(B, T, W_B)
    return out, k_new, v_new

def centred_depthwise_conv(x, w, b):
    T = x.shape[1]
    xp = jnp.pad(x, ((0, 0), (CONV_LEFT, CONV_W - 1 - CONV_LEFT), (0, 0)))
    y = b
    for j in range(CONV_W):
        y = y + xp[:, j:j + T] * w[j]
    return y

def linear_scan(a, b, h0, reverse):
    def step(h, ab):
        h = ab[0] * h + ab[1]
        return h, h
    h_last, hs = lax.scan(step, h0, (jnp.swapaxes(a, 0, 1), jnp.swapaxes(b, 0, 1)), reverse=reverse)
    return jnp.swapaxes(hs, 0, 1), h_last

def rglru_mixer(xc, gc, lp, s0):
    B, T, _ = xc.shape
    xconv = centred_depthwise_conv(xc, lp['lru_conv_w'], lp['lru_conv_b'])
    xg = xconv.reshape(B, T, LRU_BLOCKS, LRU_BW)
    h_sum = None
    states = []
    for d in range(2):
        gate_r = jax.nn.sigmoid(jnp.einsum('btgi,gij->btgj', xg, lp['lru_wa'][d]).reshape(B, T, W_C) + lp['lru_ba'][d])
        gate_i = jax.nn.sigmoid(jnp.einsum('btgi,gij->btgj', xg, lp['lru_wx'][d]).reshape(B, T, W_C) + lp['lru_bx'][d])
        log_a = -LRU_C * gate_r.astype(jnp.float32) * jax.nn.softplus(-lp['lru_lambda'][d].astype(jnp.float32))
        a = jnp.exp(log_a).astype(xc.dtype)
        bterm = (jnp.sqrt(-jnp.expm1(2.0 * log_a)) * (gate_i * xconv).astype(jnp.float32)).astype(xc.dtype)
        hs, h_last = linear_scan(a, bterm, s0[:, d], reverse=(d == 1))
        h_sum = hs if h_sum is None else h_sum + hs
        states.append(h_last)
    y = h_sum * jax.nn.gelu(gc, approximate=False)
    return y, jnp.stack(states, axis=1)

def token_mixers(h, lp, lam_init, rope, ctx_k, ctx_v, s_rwkv0, s_lru0):
    proj = h @ lp['w_in']
    r_a, k_a, v_a, q_b, k_b, v_b, x_c, g_c = jnp.split(proj, SPLIT_POINTS, axis=-1)
    out_a, s_rwkv = rwkv7_mixer(h, r_a, k_a, v_a, lp, s_rwkv0)
    out_b, k_new, v_new = diff_attention_mixer(q_b, k_b, v_b, lp, lam_init, rope, ctx_k, ctx_v)
    out_c, s_lru = rglru_mixer(x_c, g_c, lp, s_lru0)
    y = jnp.concatenate([out_a, out_b, out_c], axis=-1) @ lp['w_out']
    return y, k_new, v_new, s_rwkv, s_lru

def peer_ffn(h, wq, sub_keys, u_tab, v_tab):
    B, T, D = h.shape
    n = B * T
    x = h.reshape(n, D)
    q = (x @ wq).reshape(n, PEER_HEADS, 2, PEER_DQ // 2)
    s = jnp.einsum('nhcd,hckd->nhck', q, sub_keys).astype(jnp.float32)
    s1, i1 = lax.top_k(s[:, :, 0], PEER_TOPK)
    s2, i2 = lax.top_k(s[:, :, 1], PEER_TOPK)
    cand = (s1[..., :, None] + s2[..., None, :]).reshape(n, PEER_HEADS, PEER_TOPK * PEER_TOPK)
    cidx = (i1[..., :, None] * PEER_N_KEYS + i2[..., None, :]).reshape(n, PEER_HEADS, PEER_TOPK * PEER_TOPK)
    top, pos = lax.top_k(cand, PEER_TOPK)
    idx = jnp.take_along_axis(cidx, pos, axis=-1)
    gate = jax.nn.softmax(top, axis=-1).astype(h.dtype)
    nb = n // PEER_BLOCK

    def one_block(args):
        xb, ib, gb = args
        act = jax.nn.gelu(jnp.einsum('nd,nhkd->nhk', xb, u_tab[ib]), approximate=False)
        return jnp.einsum('nhk,nhkd->nd', gb * act, v_tab[ib])

    y = lax.map(one_block, (x.reshape(nb, PEER_BLOCK, D),
                            idx.reshape(nb, PEER_BLOCK, PEER_HEADS, PEER_TOPK),
                            gate.reshape(nb, PEER_BLOCK, PEER_HEADS, PEER_TOPK)))
    return y.reshape(B, T, D)

def trunk_layer(x, mod, lp, lam_init, rope, ctx_k, ctx_v, s_rwkv0, s_lru0):
    sh1, sc1, g1, sh2, sc2, g2 = mod
    h = rmsnorm(x, lp['norm1_g']) * (1.0 + sc1) + sh1
    y, k_new, v_new, s_rwkv, s_lru = token_mixers(h, lp, lam_init, rope, ctx_k, ctx_v, s_rwkv0, s_lru0)
    x = x + g1 * y
    h2 = rmsnorm(x, lp['norm2_g']) * (1.0 + sc2) + sh2
    x = x + g2 * peer_ffn(h2, lp['peer_wq'], lp['peer_keys'], lp['peer_u'], lp['peer_v'])
    return x, k_new, v_new, s_rwkv, s_lru

def setup_inputs(seed: int = 0) -> dict:
    key = jax.random.key(seed)
    ks = iter(jax.random.split(key, 64))
    f32 = jnp.float32

    def nrm(shape, scale):
        return jax.random.normal(next(ks), shape, f32) * scale

    def gain(shape):
        return 1.0 + nrm(shape, 0.02)

    u_lam = jax.random.uniform(next(ks), (DEPTH, 2, W_C), f32, 0.9, 0.999)
    p_lam = u_lam ** (1.0 / LRU_C)
    lru_lambda = jnp.log(p_lam) - jnp.log1p(-p_lam)
    return {
        'x_prompt': nrm((BATCH, SEQ, D_MODEL), 1.0),
        'x_sample': nrm((DEC_BATCH, DEC_SEQ, D_MODEL), 1.0),
        'c': nrm((DEC_BATCH, D_MODEL), 1.0),
        'cache_k': nrm((DEC_BATCH, DEPTH, H_B, PAST_LEN, 2 * DK), 1.0),
        'cache_v': nrm((DEC_BATCH, DEPTH, H_B, PAST_LEN, DV), 1.0),
        'state_rwkv': nrm((DEC_BATCH, DEPTH, 2, H_A, HD_A, HD_A), 0.3),
        'state_lru': nrm((DEC_BATCH, DEPTH, 2, W_C), 0.5),
        'c_ctx': nrm((D_MODEL,), 1.0),
        'mod_w': nrm((DEPTH, D_MODEL, 6 * D_MODEL), 0.5 * D_MODEL ** -0.5),
        'mod_b': nrm((DEPTH, 6 * D_MODEL), 0.02),
        'norm1_g': gain((DEPTH, D_MODEL)),
        'norm2_g': gain((DEPTH, D_MODEL)),
        'w_in': nrm((DEPTH, D_MODEL, D_IN), D_MODEL ** -0.5),
        'w_out': nrm((DEPTH, W_A + W_B + W_C, D_MODEL), (W_A + W_B + W_C) ** -0.5),
        'rwkv_w0': nrm((DEPTH, 2, W_A), 0.5),
        'rwkv_wA': nrm((DEPTH, 2, D_MODEL, RWKV_DECAY_LORA), D_MODEL ** -0.5),
        'rwkv_wB': nrm((DEPTH, 2, RWKV_DECAY_LORA, W_A), 0.5 * RWKV_DECAY_LORA ** -0.5),
        'rwkv_a0': nrm((DEPTH, 2, W_A), 0.5),
        'rwkv_aA': nrm((DEPTH, 2, D_MODEL, RWKV_ICLR_LORA), D_MODEL ** -0.5),
        'rwkv_aB': nrm((DEPTH, 2, RWKV_ICLR_LORA, W_A), 0.5 * RWKV_ICLR_LORA ** -0.5),
        'rwkv_gA': nrm((DEPTH, D_MODEL, RWKV_GATE_LORA), D_MODEL ** -0.5),
        'rwkv_gB': nrm((DEPTH, RWKV_GATE_LORA, W_A), RWKV_GATE_LORA ** -0.5),
        'rwkv_kk': 0.85 + nrm((DEPTH, W_A), 0.05),
        'rwkv_ka': 1.0 + nrm((DEPTH, W_A), 0.05),
        'rwkv_rk': nrm((DEPTH, H_A, HD_A), 0.1),
        'rwkv_ln_g': gain((DEPTH, W_A)),
        'diff_lq1': nrm((DEPTH, DK), 0.1),
        'diff_lk1': nrm((DEPTH, DK), 0.1),
        'diff_lq2': nrm((DEPTH, DK), 0.1),
        'diff_lk2': nrm((DEPTH, DK), 0.1),
        'diff_subln_g': gain((DEPTH, DV)),
        'lru_conv_w': nrm((DEPTH, CONV_W, W_C), 0.5),
        'lru_conv_b': nrm((DEPTH, W_C), 0.02),
        'lru_wa': nrm((DEPTH, 2, LRU_BLOCKS, LRU_BW, LRU_BW), LRU_BW ** -0.5),
        'lru_ba': nrm((DEPTH, 2, W_C), 0.02),
        'lru_wx': nrm((DEPTH, 2, LRU_BLOCKS, LRU_BW, LRU_BW), LRU_BW ** -0.5),
        'lru_bx': nrm((DEPTH, 2, W_C), 0.02),
        'lru_lambda': lru_lambda,
        'peer_wq': nrm((DEPTH, D_MODEL, PEER_HEADS * PEER_DQ), D_MODEL ** -0.5),
        'peer_keys': nrm((DEPTH, PEER_HEADS, 2, PEER_N_KEYS, PEER_DQ // 2), (PEER_DQ // 2) ** -0.5),
        'peer_u': nrm((DEPTH, N_EXPERTS, D_MODEL), D_MODEL ** -0.5),
        'peer_v': nrm((DEPTH, N_EXPERTS, D_MODEL), 0.25),
        'final_norm_g': gain((D_MODEL,)),
    }

def reference(x_prompt, x_sample, c, cache_k, cache_v, state_rwkv, state_lru, c_ctx,
              mod_w, mod_b, norm1_g, norm2_g, w_in, w_out,
              rwkv_w0, rwkv_wA, rwkv_wB, rwkv_a0, rwkv_aA, rwkv_aB, rwkv_gA, rwkv_gB,
              rwkv_kk, rwkv_ka, rwkv_rk, rwkv_ln_g,
              diff_lq1, diff_lk1, diff_lq2, diff_lk2, diff_subln_g,
              lru_conv_w, lru_conv_b, lru_wa, lru_ba, lru_wx, lru_bx, lru_lambda,
              peer_wq, peer_keys, peer_u, peer_v, final_norm_g):
    Bp = x_prompt.shape[0]
    Ts = x_sample.shape[1]
    rope = axial_rope_tables(Ts)
    zero_rwkv = jnp.zeros((Bp, 2, H_A, HD_A, HD_A), x_prompt.dtype)
    zero_lru = jnp.zeros((Bp, 2, W_C), x_prompt.dtype)
    xp = x_prompt
    xs = x_sample
    ks_list, vs_list, sr_list, sl_list = [], [], [], []
    for l in range(DEPTH):
        lp = {
            'w_in': w_in[l], 'w_out': w_out[l], 'norm1_g': norm1_g[l], 'norm2_g': norm2_g[l],
            'rwkv_w0': rwkv_w0[l], 'rwkv_wA': rwkv_wA[l], 'rwkv_wB': rwkv_wB[l],
            'rwkv_a0': rwkv_a0[l], 'rwkv_aA': rwkv_aA[l], 'rwkv_aB': rwkv_aB[l],
            'rwkv_gA': rwkv_gA[l], 'rwkv_gB': rwkv_gB[l], 'rwkv_kk': rwkv_kk[l], 'rwkv_ka': rwkv_ka[l],
            'rwkv_rk': rwkv_rk[l], 'rwkv_ln_g': rwkv_ln_g[l],
            'diff_lq1': diff_lq1[l], 'diff_lk1': diff_lk1[l], 'diff_lq2': diff_lq2[l], 'diff_lk2': diff_lk2[l],
            'diff_subln_g': diff_subln_g[l],
            'lru_conv_w': lru_conv_w[l], 'lru_conv_b': lru_conv_b[l], 'lru_wa': lru_wa[l], 'lru_ba': lru_ba[l],
            'lru_wx': lru_wx[l], 'lru_bx': lru_bx[l], 'lru_lambda': lru_lambda[l],
            'peer_wq': peer_wq[l], 'peer_keys': peer_keys[l], 'peer_u': peer_u[l], 'peer_v': peer_v[l],
        }
        lam_init = 0.8 - 0.6 * math.exp(-0.3 * l)
        mod_p = adaln_params(c_ctx[None, :], mod_w[l], mod_b[l])
        mod_s = adaln_params(c, mod_w[l], mod_b[l])
        xp, k_l, v_l, sr_l, sl_l = trunk_layer(xp, mod_p, lp, lam_init, None, None, None, zero_rwkv, zero_lru)
        xs, _, _, _, _ = trunk_layer(xs, mod_s, lp, lam_init, rope, cache_k[:, l], cache_v[:, l],
                                     state_rwkv[:, l], state_lru[:, l])
        ks_list.append(k_l)
        vs_list.append(v_l)
        sr_list.append(sr_l)
        sl_list.append(sl_l)
    y_prompt = rmsnorm(xp, final_norm_g)
    y_sample = rmsnorm(xs, final_norm_g)
    new_cache_k = jnp.stack(ks_list, axis=1)
    new_cache_v = jnp.stack(vs_list, axis=1)
    new_state_rwkv = jnp.stack(sr_list, axis=1)
    new_state_lru = jnp.stack(sl_list, axis=1)
    return (y_prompt, y_sample, new_cache_k, new_cache_v, new_state_rwkv, new_state_lru)


_drawn_inputs = setup_inputs


def setup_inputs(seed=0):
    import zlib

    import numpy as np

    out = dict(_drawn_inputs(seed))
    spreads = {}
    factors = {'state_rwkv': 8.0,
     'norm2_g': 6.572,
     'rwkv_kk': 5.88,
     'rwkv_ln_g': 23.499,
     'diff_lq1': 3.801,
     'diff_lk1': 4.35,
     'diff_lq2': 5.001,
     'diff_lk2': 5.413,
     'diff_subln_g': 8.0,
     'lru_ba': 8.0,
     'lru_bx': 6.411,
     'final_norm_g': 21.549,
     'state_lru': 3.153}
    for name, (base, spread) in spreads.items():
        noise = np.random.default_rng([zlib.crc32(name.encode()), seed]).standard_normal(out[name].shape)
        drawn = base * np.exp(spread * noise) if base else spread * noise
        out[name] = __import__('jax').numpy.asarray(drawn.astype(out[name].dtype))
    for name, factor in factors.items():
        out[name] = (out[name] * factor).astype(out[name].dtype)
    return out
```

```python
from contextlib import ExitStack

import numpy as np

import concourse.bass as bass
from concourse import mybir

F32 = mybir.dt.float32
U32 = mybir.dt.uint32
ALU = mybir.AluOpType
ACT = mybir.ActivationFunctionType
AX = mybir.AxisListType

P = 128
D = 1024
DEPTH = 2
NS = 512
NPR = 128
NT = NS + NPR
TILES = NT // P
PAST = 256
GRID_W = 64
KC = D // P
HD = 64
CA = 2
HA = 4
HB = 8
CB = 4
DK = 32
CC = 2
DECAY_SCALE = 0.606531
CH = 64
PH = 8
TOPK = 16
NKEY = 128
LRU_C = 8.0
RMS_EPS = 1e-6
SUB_EPS = 1e-5
GN_EPS = 64e-5
NEG = -3.0e38

R0, K0, V0, Q0, B0, X0, G0, LW, LA, LG = 0, 2, 4, 6, 10, 14, 16, 18, 19, 20
NPROJ = 21
VTOK = 768

CI = {}
_at = 0
for _n, _w in (("ident", P), ("ones", P), ("bones", P), ("iota", P), ("perm", P), ("maskF", 2 * P), ("maskB", 2 * P),
               ("lowF", P), ("lowB", P), ("scanF", NT), ("scanB", NT), ("cos", NS), ("sin", NS)):
    CI[_n] = (_at, _w)
    _at += _w
NCONST = _at
NKEEP = 4 * P

VI = {}
_at = 0
for _n, _w in (("mod_b", 48), ("n1", 8), ("n2", 8), ("w0", 4), ("a0", 4), ("kk", 2), ("ka", 2), ("rk", 2),
               ("lng", 2), ("sub", 1), ("convw", 8), ("convb", 2), ("ba", 4), ("bx", 4), ("lam", 4),
               ("lq", 4 * DK), ("laminit", 1), ("final", 8), ("h0", 4)):
    VI[_n] = (_at, _w)
    _at += _w
NVEC = _at


class Counter:

    def __init__(self, eng, sem):
        self.eng, self.sem, self.n = eng, sem, 0

    def did(self, inst):
        inst.then_inc(self.sem, 1)
        self.n += 1

    def wait(self):
        self.eng.wait_ge(self.sem, self.n)

    def then(self, inst):
        self.did(inst)
        self.wait()


class Program:
    def __init__(self, nc, ctx, dram):
        self.nc, self.ctx, self.dram = nc, ctx, dram
        self.sems = []
        self.n = 0

    def sem(self, name):
        s = self.ctx.enter_context(self.nc.semaphore(name))
        self.sems.append(s)
        return s

    def sb(self, st, name, shape, dt=F32):
        self.n += 1
        return st.enter_context(self.nc.sbuf_tensor(f"{name}_{self.n}", shape, dt))


def load_stage(g, l):
    nc, d = g.nc, g.dram
    loaded, done, ex = g.sem("vectors_loaded"), g.sem("lambda_steps"), g.sem("lambda_exps")
    silu, sp = g.sem("cond_silu"), g.sem("softplus_steps")
    vec = g.vec

    def v(name, a=0, b=None):
        at, w = VI[name]
        return vec[:, at + a:at + (w if b is None else b)]

    g.v = v
    with nc.Block() as block:
        @block.sync
        def _(sync):
            sync.dma_start(vec[:, :], d["vecs"][l]).then_inc(loaded, 16)
            sync.dma_start(g.cond[:, :, :], d["cond"]).then_inc(loaded, 16)
            sync.dma_start(g.keep[:, :], d["consts"][:, 0:NKEEP]).then_inc(loaded, 16)

        @block.vector
        def _(ve):
            c = Counter(ve, done)
            ve.wait_ge(loaded, 48)
            lq = v("lq").rearrange("p (a k) -> p a k", a=4)
            for i in range(2):
                c.then(ve.tensor_tensor(g.tiny[:, 8:8 + DK], lq[:, 2 * i, :], lq[:, 2 * i + 1, :], ALU.mult))
                c.then(ve.tensor_reduce(g.tiny[:, i:i + 1], g.tiny[:, 8:8 + DK], AX.X, ALU.add))
            ve.wait_ge(ex, 1)
            c.then(ve.tensor_tensor(g.lam[:, 0:1], g.tiny[:, 2:3], g.tiny[:, 3:4], ALU.subtract))
            c.then(ve.tensor_tensor(g.lam[:, 0:1], g.lam[:, 0:1], v("laminit"), ALU.add))
            c.then(ve.tensor_scalar(g.lam[:, 1:2], g.lam[:, 0:1], -1.0, None, ALU.mult))
            c.then(ve.tensor_scalar(g.lam[:, 2:3], v("laminit"), -1.0, 1.0, ALU.mult, ALU.add))
            c.then(ve.tensor_tensor(g.lam[:, 3:4], g.lam[:, 2:3], v("sub"), ALU.mult))
            c.then(ve.tensor_scalar(g.omka[:, :], v("ka"), -1.0, 1.0, ALU.mult, ALU.add))
            ve.wait_ge(sp, 1)
            c.then(ve.tensor_scalar(g.nsp[:, :], g.nsp[:, :], -LRU_C, None, ALU.mult))

        @block.scalar
        def _(act):
            c = Counter(act, sp)
            act.wait_ge(loaded, 48)
            nc.scalar.activation(g.scond[:, :, :], g.cond[:, :, :], ACT.Silu).then_inc(silu, 1)
            act.wait_ge(done, 4)
            nc.scalar.activation(g.tiny[:, 2:4], g.tiny[:, 0:2], ACT.Exp).then_inc(ex, 1)
            nc.scalar.activation(g.nsp2[:, :], v("lam"), ACT.Exp, scale=-1.0).then_inc(silu, 1)
            act.wait_ge(silu, 2)
            c.did(nc.scalar.activation(g.nsp[:, :], g.nsp2[:, :], ACT.Ln, bias=1.0))


def gemm(g, name, weights, n_out, R, rhs, take, n=NT, wring=None, extra=None):
    nc = g.nc
    w_in = [g.sem(f"{name}_w_loaded{i}") for i in range(R)]
    w_free, ready, taken = g.sem(f"{name}_w_used"), g.sem(f"{name}_sums_ready"), g.sem(f"{name}_sums_taken")
    with ExitStack() as st, nc.Block() as block:
        ring = wring if wring is not None else g.sb(st, f"{name}_w", [P, R, KC, P])

        @block.sync
        def _(sync):
            sync.sem_inc(w_free, R)
            with sync.Fori(0, n_out // R) as i:
                for j in range(R):
                    sync.wait_ge(w_free, i * R + (j + 1))
                    sync.dma_start(ring[:, j, :, :], weights(i * R + j)).then_inc(w_in[j], 16)
            if extra and "sync" in extra:
                extra["sync"](sync)

        @block.tensor
        def _(pe):
            with pe.Fori(0, n_out // R) as i:
                for j in range(R):
                    pe.wait_ge(w_in[j], i * 16 + 16)
                    pe.wait_ge(taken, i * R + (j + 1))
                    for a, b in ((0, min(n, NS)), (NS, n)) if n > NS else ((0, n),):
                        for kc in range(KC):
                            mm = pe.matmul(g.ps[:, 2 * j + (a == NS), 0:b - a], ring[:, j, kc, :], rhs[:, kc, a:b],
                                           start=(kc == 0), stop=(kc == KC - 1))
                    mm.then_inc(ready, 1)
                    pe.wait_ge(ready, i * R + (j + 1))
                    pe.sem_inc(w_free, 1)
            if extra and "tensor" in extra:
                extra["tensor"](pe)

        @block.vector
        def _(ve):
            ve.sem_inc(taken, R)
            with ve.Fori(0, n_out // R) as i:
                for j in range(R):
                    ve.wait_ge(ready, i * R + (j + 1))
                    take(ve, i * R + j, g.flat[:, 1024 * j:1024 * j + n]).then_inc(taken, 1)
            if extra and "vector" in extra:
                extra["vector"](ve)

        if extra and "scalar" in extra:
            @block.scalar
            def _(act):
                extra["scalar"](act)


def mod_stage(g, l):
    nc, d, v = g.nc, g.dram, g.v
    gemm(g, "mod", lambda oc: d["mod_w"][l, oc], 6 * KC, 4, g.scond,
         lambda ve, oc, sums: ve.tensor_copy(g.modT[:, bass.ds(oc, 1), :], sums), n=2)
    steps = g.sem("mod_steps")
    with nc.Block() as block:
        @block.vector
        def _(ve):
            c = Counter(ve, steps)
            c.then(ve.tensor_tensor(g.modT[:, :, :], g.modT[:, :, :],
                                    v("mod_b").unsqueeze(2).broadcast_to([P, 6 * KC, 2]), ALU.add))
            for i, (name, part) in enumerate((("n1", 1), ("n2", 4))):
                c.then(ve.tensor_scalar(g.gain[:, i, :, :], g.modT[:, part * KC:(part + 1) * KC, :], 1.0, None, ALU.add))
                c.then(ve.tensor_tensor(g.gain[:, i, :, :], g.gain[:, i, :, :],
                                        v(name).unsqueeze(2).broadcast_to([P, KC, 2]), ALU.mult))


def norm_stage(g, name, out, gain, shift):
    nc = g.nc
    sq_ready, sum_ready, r_ready, steps = (g.sem(f"{name}_{x}") for x in ("squared", "summed", "root", "steps"))
    scaled = g.sem(f"{name}_scaled")
    with ExitStack() as st, nc.Block() as block:
        sq = g.sb(st, "sq", [P, 2, NT])
        rs = g.sb(st, "rs", [P, 2, NT])
        used = g.sem(f"{name}_square_used")

        @block.scalar
        def _(act):
            for kc in range(KC):
                if kc >= 2:
                    act.wait_ge(used, kc - 1)
                nc.scalar.activation(sq[:, kc % 2, :], g.xT[:, kc, :], ACT.Square).then_inc(sq_ready, 1)
            act.wait_ge(steps, 1)
            nc.scalar.activation(rs[:, 1, :], rs[:, 0, :], ACT.Sqrt).then_inc(r_ready, 1)
            for kc in range(KC):
                act.wait_ge(scaled, kc + 1)
                for c, (a, b) in enumerate(((0, NS), (NS, NT))):
                    nc.scalar.activation(out[:, kc, a:b], out[:, kc, a:b], ACT.Identity,
                                         scale=gain(kc, c), bias=shift(kc, c) if shift else 0.0)

        @block.tensor
        def _(pe):
            for kc in range(KC):
                pe.wait_ge(sq_ready, kc + 1)
                for bank, (a, b) in enumerate(((0, NS), (NS, NT))):
                    mm = pe.matmul(g.ps[:, bank, 0:b - a], g.ones, sq[:, kc % 2, a:b], start=(kc == 0), stop=(kc == KC - 1))
                mm.then_inc(used, 1)

        @block.vector
        def _(ve):
            c = Counter(ve, steps)
            ve.wait_ge(used, KC)
            c.did(ve.tensor_scalar(rs[:, 0, :], g.flat[:, 0:NT], 1.0 / D, RMS_EPS, ALU.mult, ALU.add))
            ve.wait_ge(r_ready, 1)
            c.then(ve.reciprocal(rs[:, 0, :], rs[:, 1, :]))
            for kc in range(KC):
                ve.tensor_tensor(out[:, kc, :], g.xT[:, kc, :], rs[:, 0, :], ALU.mult).then_inc(scaled, 1)


def proj_stage(g, l):
    nc, d = g.nc, g.dram
    gemm(g, "proj", lambda oc: d["w_proj"][l, oc], NPROJ, 3, g.hT,
         lambda ve, oc, sums: ve.tensor_copy(g.proj[:, bass.ds(oc, 1), :], sums))
    w_in, ready, taken = g.sem("vtok_w_loaded"), g.sem("vtok_ready"), g.sem("vtok_taken")
    with ExitStack() as st, nc.Block() as block:
        wv = g.sb(st, "wv", [P, KC, VTOK])

        @block.sync
        def _(sync):
            sync.dma_start(wv[:, :, :], d["w_v"][l]).then_inc(w_in, 16)

        @block.tensor
        def _(pe):
            pe.wait_ge(w_in, 16)
            for t in range(TILES):
                if t >= 4:
                    pe.wait_ge(taken, t - 3)
                s = t % 4
                for bank, (a, b) in enumerate(((0, 512), (512, VTOK))):
                    for kc in range(KC):
                        mm = pe.matmul(g.ps[:, 2 * s + bank, 0:b - a], g.hT[:, kc, t * P:(t + 1) * P], wv[:, kc, a:b],
                                       start=(kc == 0), stop=(kc == KC - 1))
                mm.then_inc(ready, 1)

        @block.vector
        def _(ve):
            for t in range(TILES):
                ve.wait_ge(ready, t + 1)
                ve.tensor_copy(g.vtok[:, t, :], g.flat[:, 1024 * (t % 4):1024 * (t % 4) + VTOK]).then_inc(taken, 1)


def rope_stage(g, l):
    nc, d = g.nc, g.dram
    loaded, out_done = g.sem("rope_consts_loaded"), g.sem("cache_stored")
    rot, cosd, sind = g.sem("rotated"), g.sem("cos_done"), g.sem("sin_done")
    added = g.sem("rope_added")
    with ExitStack() as st, nc.Block() as block:
        cs = g.sb(st, "ropecs", [P, 2, NS])
        perm = g.sb(st, "perm", [P, P])
        tmp = g.sb(st, "ropetmp", [P, 2, 2, NS])
        at = CI["cos"][0]

        @block.sync
        def _(sync):
            sync.dma_start(cs[:, :, :], d["consts"][:, at:at + 2 * NS]).then_inc(loaded, 16)
            sync.dma_start(perm[:, :], d["consts"][:, CI["perm"][0]:CI["perm"][0] + P]).then_inc(loaded, 16)
            sync.dma_start(g.kctx[:, :, :], d["cache_k"][l]).then_inc(loaded, 16)
            sync.dma_start(g.vctx[:, :, :], d["cache_v"][l]).then_inc(loaded, 16)
            sync.dma_start(d["new_k"][l], g.proj[:, B0:B0 + CB, NS:NT]).then_inc(out_done, 16)
            sync.dma_start(d["new_v"][l], g.vtok[:, TILES - 1, 256:VTOK]).then_inc(out_done, 16)
            sync.wait_ge(out_done, 32)
            sync.wait_ge(loaded, 64)

        @block.tensor
        def _(pe):
            pe.wait_ge(loaded, 64)
            for c in range(8):
                if c >= 2:
                    pe.wait_ge(sind, c - 1)
                pe.matmul(g.ps[:, c % 2, :], perm[:, :], g.proj[:, Q0 + c, 0:NS], start=True, stop=True).then_inc(rot, 1)

        @block.gpsimd
        def _(pool):
            pool.wait_ge(loaded, 64)
            for c in range(8):
                if c >= 2:
                    pool.wait_ge(added, c - 1)
                pool.tensor_tensor(tmp[:, 0, c % 2, :], g.proj[:, Q0 + c, 0:NS], cs[:, 0, :], ALU.mult).then_inc(cosd, 1)

        @block.vector
        def _(ve):
            for c in range(8):
                ve.wait_ge(rot, c + 1)
                ve.tensor_tensor(tmp[:, 1, c % 2, :], g.ps[:, c % 2, :], cs[:, 1, :], ALU.mult).then_inc(sind, 1)
                ve.wait_ge(sind, c + 1)
                ve.wait_ge(cosd, c + 1)
                ve.tensor_tensor(g.proj[:, Q0 + c, 0:NS], tmp[:, 0, c % 2, :], tmp[:, 1, c % 2, :], ALU.add).then_inc(added, 1)


def attention_stage(g, l):
    nc = g.nc
    units = [(h, t) for t in range(TILES) for h in range(HB)]
    scale = DK ** -0.5
    s_ready, m_ready, e_done = g.sem("scores_ready"), g.sem("row_max_ready"), g.sem("exps_ready")
    steps, comb, t_ready = g.sem("attn_steps"), g.sem("probs_combined"), g.sem("probs_transposed")
    pt_ready, o_ready, o_taken = g.sem("probsT_ready"), g.sem("attn_out_ready"), g.sem("attn_out_taken")
    with ExitStack() as st, nc.Block() as block:
        p = g.sb(st, "p", [P, 2, 2, 768])
        pt = g.sb(st, "pt", [P, 2, 768])
        mx = g.sb(st, "mx", [P, 2, 4])
        sm = g.sb(st, "sm", [P, 2, 4])

        def keys(t):
            if t == TILES - 1:
                return [(lambda c, a, b: g.proj[a:b, B0 + c, NS:NT], 0, P)]
            return [(lambda c, a, b: g.proj[a:b, B0 + c, 0:NS], 0, NS), (lambda c, a, b: g.kctx[a:b, c, :], NS, PAST)]

        def values(t, h):
            col = slice(256 + h * HD, 256 + (h + 1) * HD)
            if t == TILES - 1:
                return [g.vtok[:, t, col]]
            return [g.vtok[:, k, col] for k in range(NS // P)] + \
                   [g.vctx[:, k, h * HD:(h + 1) * HD] for k in range(PAST // P)]

        def nk(t):
            return P if t == TILES - 1 else NS + PAST

        @block.tensor
        def _(pe):
            for u in range(len(units) + 2):
                if u < len(units):
                    h, t = units[u]
                    if u >= 1:
                        pe.wait_ge(e_done, u)
                    for c in range(2):
                        base = (h % 2) * HD + c * DK
                        for key, col, n in keys(t):
                            mm = pe.matmul(g.flat[:, 1024 * c + col:1024 * c + col + n],
                                           g.proj[base:base + DK, Q0 + h // 2, t * P:(t + 1) * P],
                                           key(h // 2, base, base + DK), start=True, stop=True)
                    mm.then_inc(s_ready, 1)
                if 1 <= u <= len(units):
                    w = u - 1
                    h, t = units[w]
                    pe.wait_ge(comb, w + 1)
                    if w >= 1:
                        pe.wait_ge(pt_ready, w)
                    for k in range(nk(t) // P):
                        mm = pe.transpose(g.flat[:, 2048 + k * P:2048 + (k + 1) * P], p[:, w % 2, 0, k * P:(k + 1) * P], g.ident)
                    mm.then_inc(t_ready, 1)
                if u >= 2:
                    w = u - 2
                    h, t = units[w]
                    pe.wait_ge(pt_ready, w + 1)
                    if w >= 2:
                        pe.wait_ge(o_taken, w - 1)
                    base = (h % 2) * HD
                    vs = values(t, h)
                    for k, vk in enumerate(vs):
                        mm = pe.matmul(g.ps[base:base + HD, 6 + w % 2, 0:P], vk, pt[:, w % 2, k * P:(k + 1) * P],
                                       start=(k == 0), stop=(k == len(vs) - 1))
                    mm.then_inc(o_ready, 1)

        @block.vector
        def _(ve):
            c = Counter(ve, steps)

            def out(w):
                h, t = units[w]
                base = (h % 2) * HD
                ve.wait_ge(o_ready, w + 1)
                ve.tensor_copy(g.outT[base:base + HD, CA + h // 2, t * P:(t + 1) * P],
                               g.ps[base:base + HD, 6 + w % 2, 0:P]).then_inc(o_taken, 1)

            def row_max(u):
                _, t = units[u]
                ve.wait_ge(s_ready, u + 1)
                c.then(ve.tensor_reduce(mx[:, u % 2, 0:2], g.flat[:, 0:2048].rearrange("p (c k) -> p c k", c=2)[:, :, 0:nk(t)],
                                        AX.X, ALU.max, negate=True))
                ve.tensor_scalar(mx[:, u % 2, 2:4], mx[:, u % 2, 0:2], scale, None, ALU.mult).then_inc(m_ready, 1)

            row_max(0)
            for u in range(len(units)):
                _, t = units[u]
                ve.wait_ge(e_done, u + 1)
                if u + 1 < len(units):
                    row_max(u + 1)
                c.then(ve.reciprocal(sm[:, u % 2, 2:4], sm[:, u % 2, 0:2]))
                c.then(ve.tensor_scalar(p[:, u % 2, 1, 0:nk(t)], p[:, u % 2, 1, 0:nk(t)], sm[:, u % 2, 3:4], g.lam[:, 1:2],
                                        ALU.mult, ALU.mult))
                ve.scalar_tensor_tensor(p[:, u % 2, 0, 0:nk(t)], p[:, u % 2, 0, 0:nk(t)], sm[:, u % 2, 2:3],
                                        p[:, u % 2, 1, 0:nk(t)], ALU.mult, ALU.add).then_inc(comb, 1)
                if u >= 2:
                    out(u - 2)
            out(len(units) - 2)
            out(len(units) - 1)

        @block.scalar
        def _(act):
            def evac(w):
                _, t = units[w]
                act.wait_ge(t_ready, w + 1)
                if w >= 2:
                    act.wait_ge(o_ready, w - 1)
                nc.scalar.activation(pt[:, w % 2, 0:nk(t)], g.flat[:, 2048:2048 + nk(t)], ACT.Copy).then_inc(pt_ready, 1)

            ones = []
            for u in range(len(units)):
                _, t = units[u]
                act.wait_ge(m_ready, u + 1)
                if u >= 2:
                    act.wait_ge(t_ready, u - 1)
                for c in range(2):
                    e = nc.scalar.activation(p[:, u % 2, c, 0:nk(t)], g.flat[:, 1024 * c:1024 * c + nk(t)], ACT.Exp,
                                             bias=mx[:, u % 2, 2 + c:3 + c], scale=scale, accum_out=sm[:, u % 2, c:c + 1])
                e.then_inc(e_done, 1)
                if u >= 1:
                    evac(u - 1)
            evac(len(units) - 1)


def head_sums(g, pe, src, ready, done, n_chunks=CA, first_bank=0):
    for c in range(n_chunks):
        pe.wait_ge(ready, c + 1)
        for bank, (a, b) in enumerate(((0, NS), (NS, NT))):
            mm = pe.matmul(g.ps[:, first_bank + 2 * c + bank, 0:b - a], g.bones, src(c)[:, a:b], start=True, stop=True)
        mm.then_inc(done, 1)


def subln_stage(g):
    nc = g.nc
    sq, sums, steps, roots = (g.sem(f"subln_{x}") for x in ("squared", "summed", "steps", "roots"))
    with ExitStack() as st, nc.Block() as block:
        s = g.sb(st, "s", [P, CB, NT])

        @block.scalar
        def _(act):
            for c in range(CB):
                nc.scalar.activation(s[:, c, :], g.outT[:, CA + c, :], ACT.Square).then_inc(sq, 1)
            for c in range(CB):
                act.wait_ge(steps, c + 1)
                nc.scalar.activation(s[:, c, :], s[:, c, :], ACT.Sqrt).then_inc(roots, 1)

        @block.tensor
        def _(pe):
            head_sums(g, pe, lambda c: s[:, c, :], sq, sums, n_chunks=CB)

        @block.vector
        def _(ve):
            k = Counter(ve, steps)
            for c in range(CB):
                ve.wait_ge(sums, c + 1)
                k.did(ve.tensor_scalar(s[:, c, :], g.flat[:, 1024 * c:1024 * c + NT], 1.0 / HD, SUB_EPS, ALU.mult, ALU.add))
            for c in range(CB):
                ve.wait_ge(roots, c + 1)
                k.then(ve.reciprocal(s[:, c, :], s[:, c, :]))
                k.did(ve.scalar_tensor_tensor(g.outT[:, CA + c, :], g.outT[:, CA + c, :], g.lam[:, 3:4], s[:, c, :],
                                              ALU.mult, ALU.mult))


def lru_stage(g, l):
    nc, d, v = g.nc, g.dram, g.v
    wl, zero, conv, gate_mm, gate_tk = (g.sem(f"lru_{x}") for x in ("w_loaded", "w_zero", "conv", "gates_summed", "gates_taken"))
    steps, agates, scans, out_st, gel = (g.sem(f"lru_{x}") for x in ("steps", "a_steps", "scans", "stored", "gelu"))
    SEQS = ((0, NS), (NS, NT))
    with ExitStack() as st, nc.Block() as block:
        w = g.sb(st, "lruw", [P, 2, 2, CC, P])
        xp = g.sb(st, "xpad", [P, CC, NT + 6])
        xc = g.sb(st, "xconv", [P, CC, NT])
        ga = g.sb(st, "ga", [P, NT])
        gi = g.sb(st, "gi", [P, NT])
        a = g.sb(st, "a", [P, NT])
        th = g.sb(st, "th", [P, NT])
        bt = g.sb(st, "bt", [P, NT])
        hs = g.sb(st, "hs", [P, CC, 2, NT])
        last = g.sb(st, "last", [P, 2, CC])

        @block.gpsimd
        def _(pool):
            pool.memset(w[:, :, :, :, :], 0.0).then_inc(zero, 1)

        @block.sync
        def _(sync):
            sync.wait_ge(zero, 1)
            for q in range(2):
                for half in range(2):
                    sync.dma_start(w[half * HD:(half + 1) * HD, q, :, :, half * HD:(half + 1) * HD],
                                   d["lru_w"][l, q, half]).then_inc(wl, 16)
            sync.wait_ge(steps, 3 * 2 * CC)
            sync.dma_start(d["new_lru"][l], last[:, :, :]).then_inc(out_st, 16)
            sync.wait_ge(out_st, 16)

        @block.tensor
        def _(pe):
            pe.wait_ge(wl, 64)
            pe.wait_ge(conv, CC)
            n = 0
            for c in range(CC):
                for dr in range(2):
                    for q in range(2):
                        if n >= 4:
                            pe.wait_ge(gate_tk, n - 3)
                        for bank, (x, y) in enumerate(SEQS):
                            mm = pe.matmul(g.ps[:, 2 * (n % 4) + bank, 0:y - x], w[:, q, dr, c, :], xc[:, c, x:y], start=True, stop=True)
                        mm.then_inc(gate_mm, 1)
                        n += 1

        @block.scalar
        def _(act):
            s = Counter(act, agates)
            for c in range(CC):
                nc.scalar.activation(g.outT[:, CA + CB + c, :], g.proj[:, G0 + c, :], ACT.Gelu).then_inc(gel, 1)
            n = 0
            for c in range(CC):
                for dr in range(2):
                    col = 2 * dr + c
                    i = 2 * c + dr
                    if i >= 1:
                        act.wait_ge(steps, 3 * i)
                    for q, dst, bias in ((0, ga, "ba"), (1, gi, "bx")):
                        act.wait_ge(gate_mm, n + 1)
                        nc.scalar.activation(dst[:, :], g.flat[:, 1024 * (n % 4):1024 * (n % 4) + NT], ACT.Sigmoid,
                                             bias=v(bias, col, col + 1)).then_inc(gate_tk, 1)
                        n += 1
                    act.wait_ge(gate_tk, n)
                    s.did(nc.scalar.activation(a[:, :], ga[:, :], ACT.Exp, scale=g.nsp[:, col:col + 1]))
                    s.then(nc.scalar.activation(th[:, :], ga[:, :], ACT.Tanh, scale=g.nsp[:, col:col + 1]))
                    act.wait_ge(steps, 3 * i + 2)
                    s.did(nc.scalar.activation(ga[:, :], ga[:, :], ACT.Sqrt))

        @block.vector
        def _(ve):
            k = Counter(ve, scans)
            s = Counter(ve, steps)
            cv = Counter(ve, g.sem("lru_conv_steps"))
            cv.then(ve.memset(xp[:, :, :], 0.0))
            for c in range(CC):
                cv.did(ve.tensor_copy(xp[:, c, 2:2 + NS], g.proj[:, X0 + c, 0:NS]))
                cv.did(ve.tensor_copy(xp[:, c, NS + 5:NS + 5 + NPR], g.proj[:, X0 + c, NS:NT]))
            cv.wait()
            for c in range(CC):
                for (x, y), at in zip(SEQS, (0, NS + 3)):
                    for j in range(4):
                        src = xp[:, c, at + j:at + j + y - x]
                        if j == 0:
                            i = ve.tensor_scalar(xc[:, c, x:y], src, v("convw", 2 * j + c, 2 * j + c + 1), v("convb", c, c + 1), ALU.mult, ALU.add)
                        else:
                            i = ve.scalar_tensor_tensor(xc[:, c, x:y], src, v("convw", 2 * j + c, 2 * j + c + 1), xc[:, c, x:y], ALU.mult, ALU.add)
                        if j < 3 or y == NS:
                            cv.then(i)
                        else:
                            i.then_inc(conv, 1)
            ve.wait_ge(conv, CC)
            for c in range(CC):
                for dr in range(2):
                    i = 2 * c + dr
                    col = 2 * dr + c
                    ve.wait_ge(agates, 3 * i + 2)
                    s.then(ve.tensor_tensor(bt[:, :], a[:, :], a[:, :], ALU.mult))
                    k.then(ve.scalar_tensor_tensor(bt[:, :], bt[:, :], 1.0, th[:, :], ALU.add, ALU.mult))
                    s.did(ve.tensor_scalar(ga[:, :], bt[:, :], -1.0, None, ALU.mult))
                    k.then(ve.tensor_tensor(gi[:, :], gi[:, :], xc[:, c, :], ALU.mult))
                    ve.wait_ge(agates, 3 * i + 3)
                    k.then(ve.tensor_tensor(bt[:, :], ga[:, :], gi[:, :], ALU.mult))
                    for j, (x, y) in enumerate(SEQS):
                        init = v("h0", col, col + 1) if j == 0 else 0.0
                        o, aa, bb = hs[:, c, dr, x:y], a[:, x:y], bt[:, x:y]
                        if dr:
                            o, aa, bb = o[:, ::-1], aa[:, ::-1], bb[:, ::-1]
                        k.did(ve.tensor_tensor_scan(o, aa, bb, init, ALU.mult, ALU.add))
                    k.wait()
                    e = NT - 1 if dr == 0 else NS
                    s.did(ve.tensor_copy(last[:, dr, c:c + 1], hs[:, c, dr, e:e + 1]))
                    s.wait()
                k.then(ve.tensor_tensor(hs[:, c, 0, :], hs[:, c, 0, :], hs[:, c, 1, :], ALU.add))
                ve.wait_ge(gel, c + 1)
                k.did(ve.tensor_tensor(g.outT[:, CA + CB + c, :], g.outT[:, CA + CB + c, :], hs[:, c, 0, :], ALU.mult))


def rwkv_prepare(g, l, keep):
    nc, d, v = g.nc, g.dram, g.v
    ar, gt, pc = keep
    loaded, first, zs, z_tk = (g.sem(f"rwkv_{x}") for x in ("lora_loaded", "lora_in", "lora_summed", "lora_taken"))
    sq, kks, roots = (g.sem(f"rwkv_{x}") for x in ("key_squared", "prep_steps", "key_roots"))
    logs, exps, kk_tk = (g.sem(f"rwkv_{x}") for x in ("logs_ready", "exps_ready", "key_sums_taken"))
    with ExitStack() as st, nc.Block() as block:
        wb = g.sb(st, "wB", [P, 2, CA * P])
        gb = g.sb(st, "gB", [P, CA * P])
        t1 = g.sb(st, "t1", [P, 2, NT])
        lw = g.sb(st, "lw", [P, 4, NT])
        aa = g.sb(st, "aa", [P, 4, NT])
        kk = g.sb(st, "kk", [P, CA, NT])
        e = g.sb(st, "e", [P, 2, 3, NT])
        sc = g.sb(st, "scan", [P, 2, NT])

        @block.sync
        def _(sync):
            sync.dma_start(wb[:, :, :], d["rwkv_B"][l]).then_inc(loaded, 16)
            sync.dma_start(gb[:, :], d["rwkv_gB"][l]).then_inc(loaded, 16)
            sync.dma_start(sc[:, :, :], d["consts"][:, CI["scanF"][0]:CI["scanF"][0] + 2 * NT]).then_inc(loaded, 16)

        @block.tensor
        def _(pe):
            pe.wait_ge(loaded, 48)
            n = 0

            def sums(lhs, rhs):
                nonlocal n
                if n >= 4:
                    pe.wait_ge(z_tk, n - 3)
                for bank, (x, y) in enumerate(((0, NS), (NS, NT))):
                    mm = pe.matmul(g.ps[:, 2 * (n % 4) + bank, 0:y - x], lhs, rhs[:, x:y], start=True, stop=True)
                mm.then_inc(zs, 1)
                n += 1

            pe.wait_ge(first, 2)
            for q in range(2):
                for dr in range(2):
                    rows = slice(dr * HD, (dr + 1) * HD)
                    for c in range(CA):
                        sums(wb[rows, q, c * P:(c + 1) * P], t1[rows, 0, :] if q == 0 else g.proj[rows, LA, :])
            for c in range(CA):
                sums(gb[:, c * P:(c + 1) * P], t1[:, 1, :])
            for c in range(CA):
                pe.wait_ge(sq, c + 1)
                sums(g.bones, e[:, c, 0, :])

        @block.scalar
        def _(act):
            nc.scalar.activation(t1[:, 0, :], g.proj[:, LW, :], ACT.Tanh).then_inc(first, 1)
            nc.scalar.activation(t1[:, 1, :], g.proj[:, LG, :], ACT.Sigmoid).then_inc(first, 1)
            n = 0
            for q, dst, bias in ((0, lw, "w0"), (1, aa, "a0")):
                for i in range(4):
                    act.wait_ge(zs, n + 1)
                    nc.scalar.activation(dst[:, i, :], g.flat[:, 1024 * (n % 4):1024 * (n % 4) + NT], ACT.Sigmoid,
                                         bias=v(bias, i, i + 1)).then_inc(z_tk, 1)
                    n += 1
            for c in range(CA):
                act.wait_ge(zs, n + 1)
                nc.scalar.activation(gt[:, c, :], g.flat[:, 1024 * (n % 4):1024 * (n % 4) + NT], ACT.Copy).then_inc(z_tk, 1)
                n += 1
            for c in range(CA):
                act.wait_ge(kk_tk, c + 1)
                nc.scalar.activation(e[:, c, 0, :], e[:, c, 1, :], ACT.Sqrt).then_inc(roots, 1)
            for i in range(4):
                act.wait_ge(logs, 2 * i + 2)
                nc.scalar.activation(e[:, i % 2, 2, :], e[:, i % 2, 0, :], ACT.Exp, scale=-1.0).then_inc(exps, 1)
                act.wait_ge(exps, 3 * i + 1)
                nc.scalar.activation(e[:, i % 2, 0, :], e[:, i % 2, 0, :], ACT.Exp).then_inc(exps, 1)
                nc.scalar.activation(e[:, i % 2, 1, :], e[:, i % 2, 1, :], ACT.Exp).then_inc(exps, 1)

        @block.vector
        def _(ve):
            k = Counter(ve, kks)
            ve.wait_ge(loaded, 48)
            for c in range(CA):
                k.then(ve.tensor_scalar(kk[:, c, :], g.proj[:, K0 + c, :], v("kk", c, c + 1), None, ALU.mult))
                ve.tensor_tensor(e[:, c, 0, :], kk[:, c, :], kk[:, c, :], ALU.mult).then_inc(sq, 1)
            for c in range(CA):
                n = 10 + c
                ve.wait_ge(zs, n + 1)
                ve.tensor_scalar(e[:, c, 1, :], g.flat[:, 1024 * (n % 4):1024 * (n % 4) + NT], 1e-12, None, ALU.max).then_inc(kk_tk, 1)
            for c in range(CA):
                ve.wait_ge(roots, c + 1)
                k.then(ve.reciprocal(e[:, c, 1, :], e[:, c, 0, :]))
                k.then(ve.tensor_tensor(kk[:, c, :], kk[:, c, :], e[:, c, 1, :], ALU.mult))
            k.then(ve.tensor_scalar(lw[:, :, :], lw[:, :, :], -DECAY_SCALE, None, ALU.mult))

            def log_sums(i):
                dr = i // 2
                o, m, x = e[:, i % 2, 0, :], sc[:, dr, :], lw[:, i, :]
                if dr:
                    o, m, x = o[:, ::-1], m[:, ::-1], x[:, ::-1]
                if i >= 2:
                    ve.wait_ge(kks, k.n)
                ve.tensor_tensor_scan(o, m, x, 0.0, ALU.mult, ALU.add).then_inc(logs, 1)
                ve.wait_ge(logs, 2 * i + 1)
                ve.tensor_tensor(e[:, i % 2, 1, :], e[:, i % 2, 0, :], lw[:, i, :], ALU.subtract).then_inc(logs, 1)

            def tiled(x):
                return x.rearrange("p (t n) -> p t n", n=P)

            log_sums(0)
            for i in range(4):
                dr, c = divmod(i, 2)
                if i < 3:
                    log_sums(i + 1)
                ve.wait_ge(exps, 3 * i + 3)
                ep, em, en = (e[:, i % 2, j, :] for j in range(3))
                k.did(ve.tensor_tensor(ar[:, dr, c, :, 1, :], tiled(g.proj[:, R0 + c, :]), tiled(ep), ALU.mult))
                k.did(ve.scalar_tensor_tensor(ar[:, dr, c, :, 0, :], tiled(kk[:, c, :]), -1.0, tiled(em), ALU.mult, ALU.mult))
                k.did(ve.tensor_copy(pc[:, dr, c, :], ep.rearrange("p (n t) -> p n t", t=CH)[:, :, 0 if dr else CH - 1]))
                b, kh = g.proj[:, Q0 + i, :], g.proj[:, B0 + i, :]
                k.then(ve.tensor_tensor(b, kk[:, c, :], aa[:, i, :], ALU.mult))
                k.did(ve.tensor_tensor(b, b, en, ALU.mult))
                k.then(ve.tensor_scalar(kh, aa[:, i, :], v("ka", c, c + 1), g.omka[:, c:c + 1], ALU.mult, ALU.add))
                k.then(ve.tensor_tensor(kh, kh, g.proj[:, K0 + c, :], ALU.mult))
                k.then(ve.tensor_tensor(kh, kh, en, ALU.mult))


HOPS = [("pairs", "V"), ("lower", "VA"), ("square1", "VA"), ("square2", "VA"), ("square3", "VA"), ("square4", "VA"),
        ("square5", "V"), ("inverse", "V")] + [(x + str(i), "V") for i in range(2) for x in ("rhs", "sa", "state")]


def rwkv_scan(g, l, keep):
    nc, d = g.nc, g.dram
    ar, gt, pc = keep
    ready = [g.sem(f"products_ready{i}") for i in range(2)]
    byv = [g.sem(f"by_vector{i}") for i in range(2)]
    bya = [g.sem(f"by_scalar{i}") for i in range(2)]
    loaded, zeroed, stored, own, final = (g.sem(f"scan_{x}") for x in ("loaded", "zeroed", "stored", "steps", "final_states"))
    with ExitStack() as st, nc.Block() as block:
        mask = g.sb(st, "mask", [P, 2, 2 * P])
        low = g.sb(st, "low", [P, 2, P])
        mb = g.sb(st, "mb", [P, 2, CA, 2, 2, P])
        mk = g.sb(st, "mk", [P, 2, CA, 2, 2, P])
        pw = g.sb(st, "pw", [P, 2, HA, P])
        pwt = g.sb(st, "pwt", [P, 2, HA, P])
        x = g.sb(st, "x", [P, 2, HA, P])
        bt = g.sb(st, "bt", [P, 2, 2, CA * P])
        sz = g.sb(st, "sz", [P, 2, CA, P])
        szt = g.sb(st, "szt", [P, 2, CA, P])
        rh = g.sb(st, "rh", [P, 2, CA * P])
        sa = g.sb(st, "sa", [P, 2, CA * P])

        def tile(step, dr):
            return TILES - 1 if step == TILES - 1 else (step if dr == 0 else NS // P - 1 - step)

        def half(i, dr):
            return i if dr == 0 else 1 - i

        @block.sync
        def _(sync):
            sync.dma_start(mask[:, :, :], d["consts"][:, CI["maskF"][0]:CI["maskF"][0] + 4 * P]).then_inc(loaded, 16)
            sync.dma_start(low[:, :, :], d["consts"][:, CI["lowF"][0]:CI["lowF"][0] + 2 * P]).then_inc(loaded, 16)
            sync.wait_ge(zeroed, 1)
            for h in range(2):
                rows = slice(h * HD, (h + 1) * HD)
                sync.dma_start(sz[rows, :, :, h * HD:(h + 1) * HD], d["state_rwkv"][l, h]).then_inc(loaded, 16)
            sync.wait_ge(final, 4)
            for h in range(2):
                rows = slice(h * HD, (h + 1) * HD)
                sync.dma_start(d["new_rwkv"][l, h], sz[rows, :, :, h * HD:(h + 1) * HD]).then_inc(stored, 16)
            sync.wait_ge(stored, 32)

        @block.tensor
        def _(pe):
            pe.wait_ge(loaded, 64)
            nv, na = [0, 0], [0, 0]

            def hop(name, dr, t):
                bh = lambda c: g.proj[:, Q0 + 2 * dr + c, t * P:(t + 1) * P]
                kh = lambda c: g.proj[:, B0 + 2 * dr + c, t * P:(t + 1) * P]
                A, B, C, O = 3 * dr, 3 * dr + 1, 3 * dr + 2, 6 + dr
                heads = [(c, h, slice(h * HD, (h + 1) * HD)) for c in range(CA) for h in range(2)]
                if name == "pairs":
                    for src, banks in ((bh, (A, B)), (kh, (C, O))):
                        for c, h, rows in heads:
                            mm = pe.matmul(g.ps[:, banks[h], c * 2 * P:(c + 1) * 2 * P], src(c)[rows, :],
                                           ar[rows, dr, c, t, :, :], start=True, stop=True)
                elif name == "lower":
                    for c, h, rows in heads:
                        pe.matmul(g.ps[:, (A, B)[h], c * P:(c + 1) * P], ar[rows, dr, c, t, 0, :], bh(c)[rows, :],
                                  start=True, stop=True)
                    for i, src in enumerate((bh, kh)):
                        for c in range(CA):
                            mm = pe.transpose(g.ps[:, C, (2 * i + c) * P:(2 * i + c + 1) * P], src(c), g.ident)
                elif name.startswith("square") or name == "inverse":
                    n = 6 if name == "inverse" else int(name[6:])
                    for h in range(HA):
                        cols = slice(h * P, (h + 1) * P)
                        p0 = mb[:, dr, h // 2, h % 2, 0, :] if n == 1 else pw[:, dr, h, :]
                        pt = pwt[:, dr, h, :]
                        if n >= 2:
                            mm = pe.matmul(g.ps[:, C, cols], pt, x[:, dr, h, :], start=True, stop=True)
                        if n <= 4:
                            mm = pe.matmul(g.ps[:, A, cols], pt, p0, start=True, stop=True)
                        if n <= 5:
                            mm = pe.matmul(g.ps[:, B, cols], p0, pt, start=True, stop=True)
                else:
                    i = int(name[-1])
                    hf = half(i, dr)
                    hs = slice(hf * HD, (hf + 1) * HD)
                    if name.startswith("rhs"):
                        for c in range(CA):
                            pe.matmul(g.ps[hs, A, c * P:(c + 1) * P], ar[:, dr, c, t, 0, hs], sz[:, dr, c, :],
                                      start=(c == 0), stop=False, skip_group_check=True)
                        for c, h, rows in heads:
                            at = c * P + h * HD
                            mm = pe.matmul(g.ps[hs, A, at:at + HD], mk[:, dr, c, h, 0, hs], g.vtok[:, t, at:at + HD],
                                           start=False, stop=(c == CA - 1 and h == 1), skip_group_check=True)
                    elif name.startswith("sa"):
                        for c, h, rows in heads:
                            at = c * P + h * HD
                            mm = pe.matmul(g.ps[hs, B, at:at + HD], x[:, dr, 2 * c + h, hs], rh[:, dr, at:at + HD],
                                           start=(at == 0), stop=(c == CA - 1 and h == 1), skip_group_check=True)
                    else:
                        for c in range(CA):
                            cols = slice(c * P, (c + 1) * P)
                            pe.matmul(g.ps[:, C, cols], bt[hs, dr, 0, cols], sa[hs, dr, cols],
                                      start=(c == 0), stop=False, skip_group_check=True)
                            pe.matmul(g.ps[:, C, cols], bt[hs, dr, 1, cols], g.vtok[hs, t, cols],
                                      start=False, stop=(c == CA - 1), skip_group_check=True)
                        for c in range(CA):
                            at = c * P + hf * HD
                            mm = pe.matmul(g.ps[:, O, at:at + HD], sz[:, dr, c, :], ar[:, dr, c, t, 1, hs],
                                           start=(i == 0 and c == 0), stop=False, skip_group_check=True)
                        if i == 1:
                            for c, h, rows in heads:
                                at = c * P + h * HD
                                for j, (lhs, m) in enumerate(((sa[:, dr, at:at + HD], mb), (g.vtok[:, t, at:at + HD], mk))):
                                    mm = pe.matmul(g.ps[rows, O, c * P:(c + 1) * P], lhs, m[:, dr, c, h, 1, :],
                                                   start=False, stop=(c == CA - 1 and j == 1), skip_group_check=True)
                mm.then_inc(ready[dr], 1)

            for step in range(TILES):
                for name, by in HOPS:
                    for dr in range(2):
                        if nv[dr]:
                            pe.wait_ge(byv[dr], nv[dr])
                        if na[dr]:
                            pe.wait_ge(bya[dr], na[dr])
                        hop(name, dr, tile(step, dr))
                        nv[dr] += "V" in by
                        na[dr] += "A" in by

        @block.scalar
        def _(act):
            k = 0
            for step in range(TILES):
                for name, by in HOPS:
                    k += 1
                    if "A" not in by:
                        continue
                    for dr in range(2):
                        act.wait_ge(ready[dr], k)
                        if name == "lower":
                            dst, src = bt[:, dr, :, :], g.ps[:, 3 * dr + 2, :]
                        else:
                            dst, src = pw[:, dr, :, :], g.ps[:, 3 * dr, :]
                        nc.scalar.activation(dst, src, ACT.Copy).then_inc(bya[dr], 1)

        @block.vector
        def _(ve):
            o = Counter(ve, own)
            ve.memset(sz[:, :, :, :], 0.0).then_inc(zeroed, 1)
            o.did(ve.memset(rh[:, :, :], 0.0))
            o.did(ve.memset(sa[:, :, :], 0.0))
            o.then(ve.memset(g.outT[:, 0:CA, :], 0.0))
            ve.wait_ge(loaded, 64)
            k = 0
            for step in range(TILES):
                for name, by in HOPS:
                    k += 1
                    for dr in range(2):
                        t = tile(step, dr)
                        A, B, C, O = 3 * dr, 3 * dr + 1, 3 * dr + 2, 6 + dr
                        ve.wait_ge(ready[dr], k)
                        if name == "pairs":
                            for dst, banks in ((mb, (A, B)), (mk, (C, O))):
                                for h in range(2):
                                    last = ve.tensor_tensor(dst[:, dr, :, h, :, :].rearrange("p c a t -> p c (a t)"),
                                                            g.ps[:, banks[h], :].rearrange("p (c n) -> p c n", c=CA),
                                                            mask[:, dr, :].unsqueeze(1).broadcast_to([P, CA, 2 * P]), ALU.mult)
                            if step == TILES - 1:
                                last = ve.memset(sz[:, dr, :, :], 0.0)
                        elif name == "lower":
                            for h in range(2):
                                ve.tensor_tensor(pwt[:, dr, h::2, :], g.ps[:, (A, B)[h], 0:2 * P].rearrange("p (c n) -> p c n", c=CA),
                                                 low[:, dr, :].unsqueeze(1).broadcast_to([P, CA, P]), ALU.mult)
                            last = ve.tensor_tensor(x[:, dr, :, :], mb[:, dr, :, :, 0, :].rearrange("p c h t -> p (c h) t"),
                                                    g.ident.unsqueeze(1).broadcast_to([P, HA, P]), ALU.add)
                        elif name.startswith("square") or name == "inverse":
                            if name != "square1":
                                last = ve.tensor_tensor(x[:, dr, :, :], x[:, dr, :, :],
                                                        g.ps[:, C, :].rearrange("p (h n) -> p h n", h=HA), ALU.add)
                            if name != "inverse":
                                last = ve.tensor_copy(pwt[:, dr, :, :], g.ps[:, B, :])
                        else:
                            i = int(name[-1])
                            hf = half(i, dr)
                            hs = slice(hf * HD, (hf + 1) * HD)
                            if name.startswith("rhs"):
                                last = ve.tensor_copy(rh[hs, dr, :], g.ps[hs, A, 0:CA * P])
                            elif name.startswith("sa"):
                                last = ve.tensor_copy(sa[hs, dr, :], g.ps[hs, B, 0:CA * P])
                            else:
                                o.then(ve.tensor_tensor(szt[:, dr, :, :], sz[:, dr, :, :],
                                                        g.ps[:, C, 0:CA * P].rearrange("p (c n) -> p c n", c=CA), ALU.add))
                                if i == 1:
                                    out = g.outT[:, 0:CA, t * P:(t + 1) * P]
                                    o.did(ve.tensor_tensor(out, out, g.ps[:, O, 0:CA * P].rearrange("p (c n) -> p c n", c=CA), ALU.add))
                                ch = 2 * t + hf
                                for c in range(CA):
                                    last = ve.scalar_tensor_tensor(sz[:, dr, c, :], szt[:, dr, c, :], pc[:, dr, c, ch:ch + 1],
                                                                   g.bones, ALU.mult, ALU.mult)
                                    if step == TILES - 1 and i == 1:
                                        last.then_inc(final, 1)
                                        last = None
                        if last is not None:
                            last.then_inc(byv[dr], 1)


def rwkv_finish(g, keep):
    nc, v = g.nc, g.v
    ar, gt, pc = keep
    sb_, ss, steps, sq, roots = (g.sem(f"rwkv_out_{x}") for x in ("bonus_in", "summed", "steps", "squared", "roots"))
    taken = g.sem("rwkv_out_taken")
    with ExitStack() as st, nc.Block() as block:
        bo = g.sb(st, "bo", [P, CA, NT])
        s2 = g.sb(st, "s2", [P, CA, NT])

        @block.tensor
        def _(pe):
            n = 0
            for src, sem in ((lambda c: bo[:, c, :], sb_), (lambda c: g.outT[:, c, :], None), (lambda c: s2[:, c, :], sq)):
                for c in range(CA):
                    if sem is not None:
                        pe.wait_ge(sem, c + 1)
                    if n >= 4:
                        pe.wait_ge(taken, n - 3)
                    for bank, (a, b) in enumerate(((0, NS), (NS, NT))):
                        mm = pe.matmul(g.ps[:, 2 * (n % 4) + bank, 0:b - a], g.bones, src(c)[:, a:b], start=True, stop=True)
                    mm.then_inc(ss, 1)
                    n += 1

        @block.scalar
        def _(act):
            for c in range(CA):
                act.wait_ge(taken, 3 + c)
                nc.scalar.activation(s2[:, c, :], g.outT[:, c, :], ACT.Square).then_inc(sq, 1)
            for c in range(CA):
                act.wait_ge(taken, 5 + c)
                nc.scalar.activation(s2[:, c, :], s2[:, c, :], ACT.Sqrt).then_inc(roots, 1)

        @block.vector
        def _(ve):
            k = Counter(ve, steps)
            flat = lambda n: g.flat[:, 1024 * (n % 4):1024 * (n % 4) + NT]
            for c in range(CA):
                ve.scalar_tensor_tensor(bo[:, c, :], g.proj[:, R0 + c, :], v("rk", c, c + 1), g.proj[:, K0 + c, :],
                                        ALU.mult, ALU.mult).then_inc(sb_, 1)
            for c in range(CA):
                ve.wait_ge(ss, c + 1)
                ve.tensor_tensor(bo[:, c, :], flat(c), g.proj[:, V0 + c, :], ALU.mult).then_inc(taken, 1)
            for c in range(CA):
                ve.wait_ge(ss, 3 + c)
                ve.scalar_tensor_tensor(g.outT[:, c, :], flat(2 + c), -1.0 / HD, g.outT[:, c, :], ALU.mult, ALU.add).then_inc(taken, 1)
            for c in range(CA):
                ve.wait_ge(ss, 5 + c)
                ve.tensor_scalar(s2[:, c, :], flat(4 + c), 1.0 / HD, GN_EPS, ALU.mult, ALU.add).then_inc(taken, 1)
            for c in range(CA):
                ve.wait_ge(roots, c + 1)
                k.then(ve.reciprocal(s2[:, c, :], s2[:, c, :]))
                k.then(ve.scalar_tensor_tensor(g.outT[:, c, :], g.outT[:, c, :], v("lng", c, c + 1), s2[:, c, :], ALU.mult, ALU.mult))
                k.then(ve.tensor_tensor(g.outT[:, c, :], g.outT[:, c, :], bo[:, c, :], ALU.add))
                k.did(ve.tensor_tensor(g.outT[:, c, :], g.outT[:, c, :], gt[:, c, :], ALU.mult))


def residual_take(g, part):
    def take(ve, oc, sums):
        for c, (a, b) in enumerate(((0, NS), (NS, NT))):
            x = g.xT[:, bass.ds(oc, 1), a:b]
            i = ve.scalar_tensor_tensor(x, sums[:, a:b].unsqueeze(1), g.modT[:, bass.ds(part * KC + oc, 1), c], x, ALU.mult, ALU.add)
        return i
    return take


def select_stage(g, l, qT, sel):
    nc, d = g.nc, g.dram
    loaded, sc_ready, sc_taken, steps = (g.sem(f"sel_{x}") for x in ("keys_loaded", "scores_ready", "scores_taken", "steps"))
    dif, ex, out_ready, tr, tr_tk = (g.sem(f"sel_{x}") for x in ("differences", "exps", "selected", "transposed", "transposes_taken"))
    NC = 2 * PH
    with ExitStack() as st, nc.Block() as block:
        kt = g.sb(st, "kt", [P, NC, P])
        s = g.sb(st, "s", [P, NC, NKEY])
        s2 = g.sb(st, "s2", [P, NKEY])
        v16 = g.sb(st, "v16", [P, NC, TOPK])
        i16 = g.sb(st, "i16", [P, NC, TOPK], U32)
        if16 = g.sb(st, "if16", [P, NC, TOPK])
        cand = g.sb(st, "cand", [P, PH, TOPK * TOPK])
        c2 = g.sb(st, "c2", [P, TOPK * TOPK])
        top = g.sb(st, "top", [P, PH, TOPK])
        pos = g.sb(st, "pos", [P, PH, TOPK], U32)
        hi = g.sb(st, "hi", [P, 2, PH, TOPK], U32)
        hif = g.sb(st, "hif", [P, 2, PH, TOPK])
        oh = g.sb(st, "oh", [P, PH, TOPK, TOPK])
        res = g.sb(st, "res", [P, 3, PH, TOPK])
        sm = g.sb(st, "sm", [P, 2, PH])

        @block.sync
        def _(sync):
            sync.dma_start(kt[:, :, :], d["peer_keys"][l]).then_inc(loaded, 16)

        @block.tensor
        def _(pe):
            pe.wait_ge(loaded, 16)
            for t in range(TILES + 1):
                if t < TILES:
                    if t >= 1:
                        pe.wait_ge(sc_taken, t)
                    for i in range(NC):
                        mm = pe.matmul(g.flat[:, i * P:(i + 1) * P], qT[:, i, t * P:(t + 1) * P], kt[:, i, :], start=True, stop=True)
                    mm.then_inc(sc_ready, 1)
                if t >= 1:
                    pe.wait_ge(out_ready, t)
                    if t >= 2:
                        pe.wait_ge(tr_tk, t - 1)
                    for j in range(3):
                        mm = pe.transpose(g.ps[:, 4, j * P:(j + 1) * P], res[:, j, :, :].rearrange("p h k -> p (h k)"), g.ident)
                    mm.then_inc(tr, 1)

        @block.scalar
        def _(act):
            for t in range(TILES):
                act.wait_ge(sc_ready, t + 1)
                if t >= 1:
                    act.wait_ge(dif, t)
                nc.scalar.activation(s[:, :, :], g.flat[:, 0:NC * P], ACT.Copy).then_inc(sc_taken, 1)
                act.wait_ge(dif, t + 1)
                nc.scalar.activation(res[:, 2, :, :], res[:, 2, :, :], ACT.Exp).then_inc(ex, 1)
                act.wait_ge(tr, t + 1)
                nc.scalar.activation(sel[:, :, t * P:(t + 1) * P], g.ps[:, 4, 0:3 * P], ACT.Copy).then_inc(tr_tk, 1)

        @block.vector
        def _(ve):
            k = Counter(ve, steps)

            def top16(values, scratch, best, index):
                k.then(ve.max(best[:, 0:8], values))
                k.did(ve.max_index(index[:, 0:8], best[:, 0:8], values))
                k.then(ve.match_replace(scratch, best[:, 0:8], values, NEG))
                k.then(ve.max(best[:, 8:16], scratch))
                k.then(ve.max_index(index[:, 8:16], best[:, 8:16], scratch))

            iota16 = g.iota[:, 0:TOPK].unsqueeze(1).broadcast_to([P, PH * TOPK, TOPK])
            for t in range(TILES):
                ve.wait_ge(sc_taken, t + 1)
                for i in range(NC):
                    top16(s[:, i, :], s2[:, :], v16[:, i, :], i16[:, i, :])
                k.then(ve.tensor_copy(if16[:, :, :], i16[:, :, :]))
                both = v16[:, :, :].rearrange("p (h c) k -> p h c k", c=2)
                for h in range(PH):
                    k.did(ve.tensor_tensor(cand[:, h, :].rearrange("p (a b) -> p a b", b=TOPK),
                                           both[:, h, 0, :].unsqueeze(2).broadcast_to([P, TOPK, TOPK]),
                                           both[:, h, 1, :].unsqueeze(1).broadcast_to([P, TOPK, TOPK]), ALU.add))
                k.wait()
                for h in range(PH):
                    top16(cand[:, h, :], c2[:, :], top[:, h, :], pos[:, h, :])
                k.did(ve.tensor_scalar(hi[:, 0, :, :], pos[:, :, :], 4, None, ALU.logical_shift_right))
                k.then(ve.tensor_scalar(hi[:, 1, :, :], pos[:, :, :], TOPK - 1, None, ALU.bitwise_and))
                k.then(ve.tensor_copy(hif[:, :, :, :], hi[:, :, :, :]))
                if t >= 1:
                    ve.wait_ge(tr, t)
                ids = if16[:, :, :].rearrange("p (h c) k -> p h c k", c=2)
                for c in range(2):
                    rank = hif[:, c, :, :].rearrange("p h k -> p (h k)").unsqueeze(2).broadcast_to([P, PH * TOPK, TOPK])
                    flat = oh[:, :, :, :].rearrange("p h k m -> p (h k) m")
                    k.then(ve.tensor_tensor(flat, rank, iota16, ALU.is_equal))
                    k.then(ve.tensor_tensor(oh[:, :, :, :], oh[:, :, :, :],
                                            ids[:, :, c, :].unsqueeze(2).broadcast_to([P, PH, TOPK, TOPK]), ALU.mult))
                    k.then(ve.tensor_reduce(res[:, c, :, :], oh[:, :, :, :], AX.X, ALU.add))
                ve.tensor_tensor(res[:, 2, :, :], top[:, :, :], top[:, :, 0:1].broadcast_to([P, PH, TOPK]), ALU.subtract).then_inc(dif, 1)
                ve.wait_ge(ex, t + 1)
                k.then(ve.tensor_reduce(sm[:, 0, :], res[:, 2, :, :], AX.X, ALU.add))
                k.then(ve.reciprocal(sm[:, 1, :], sm[:, 0, :]))
                ve.tensor_tensor(res[:, 2, :, :], res[:, 2, :, :], sm[:, 1, :].unsqueeze(2).broadcast_to([P, PH, TOPK]),
                                 ALU.mult).then_inc(out_ready, 1)


GT_N = P
GB = 8
NG = NKEY // GB
OCT = 8


def gates_stage(g, l, sel):
    nc, d = g.nc, g.dram
    b_ready, a_ready, mm_ready, taken = (g.sem(f"gate_{x}") for x in ("b_onehots", "a_onehots", "products", "taken"))
    a_eq = g.sem("gate_a_equal")
    store = [g.sem(f"gate_stored{i}") for i in range(2)]
    with ExitStack() as st, nc.Block() as block:
        oa = g.sb(st, "oa", [P, 2, OCT, P])
        ob = g.sb(st, "ob", [P, 2, OCT, P])
        stage = g.sb(st, "stage", [P, 2, NKEY, GT_N])
        NO = GT_N // OCT
        iota = g.iota.unsqueeze(1).broadcast_to([P, OCT, P])

        def turns(eng, body):
            with eng.Fori(0, TILES // 2) as i:
                for q in range(2):
                    body(i * 2 + q, q, i)
            body(TILES - 1, 0, TILES // 2)

        @block.vector
        def _(ve):
            ve.sem_inc(mm_ready, 2)

            def tile(t, q, i):
                def col(j, o):
                    return sel[:, j, bass.ds(t * P + o * OCT, OCT)].unsqueeze(2).broadcast_to([P, OCT, P])

                for o in range(NO):
                    ve.wait_ge(mm_ready, t * NO + (o + 1))
                    ve.tensor_tensor(ob[:, o % 2, :, :], iota, col(1, o), ALU.is_equal).then_inc(b_ready, 1)
                    ve.tensor_tensor(oa[:, o % 2, :, :], iota, col(0, o), ALU.is_equal).then_inc(a_eq, 1)
                    ve.wait_ge(a_eq, t * NO + (o + 1))
                    ve.tensor_tensor(oa[:, o % 2, :, :], oa[:, o % 2, :, :], col(2, o), ALU.mult).then_inc(a_ready, 1)

            turns(ve, tile)

        @block.tensor
        def _(pe):
            def tile(t, q, i):
                for o in range(NO):
                    pe.wait_ge(a_ready, t * NO + (o + 1))
                    pe.wait_ge(b_ready, t * NO + (o + 1))
                    pe.wait_ge(taken, t * NO + (o + 1))
                    for n in range(OCT):
                        at = 1024 * (o % 4) + n * P
                        mm = pe.matmul(g.flat[:, at:at + P], oa[:, o % 2, n, :], ob[:, o % 2, n, :], start=True, stop=True)
                    mm.then_inc(mm_ready, 1)

            turns(pe, tile)

        @block.scalar
        def _(act):
            act.sem_inc(taken, 4)
            act.sem_inc(store[0], 16)
            act.sem_inc(store[1], 16)

            def tile(t, q, i):
                act.wait_ge(store[q], i * 16 + 16)
                for o in range(NO):
                    act.wait_ge(mm_ready, t * NO + (o + 3))
                    at = 1024 * (o % 4)
                    dst = stage[:, q, :, o * OCT:(o + 1) * OCT].rearrange("p b n -> p n b")
                    nc.scalar.activation(dst, g.flat[:, at:at + 1024].rearrange("p (n b) -> p n b", n=OCT), ACT.Copy).then_inc(taken, 1)

            turns(act, tile)

        @block.sync
        def _(sync):
            def tile(t, q, i):
                sync.wait_ge(taken, t * NO + (NO + 4))
                sync.dma_start(d["gates"][:, :, bass.ds(t, 1), :],
                               stage[:, q, :, :].rearrange("p (g b) n -> p g (b n)", b=GB).unsqueeze(2)).then_inc(store[q], 16)

            turns(sync, tile)
            sync.wait_ge(store[0], 16 * (TILES // 2 + 2))
            sync.wait_ge(store[1], 16 * (TILES // 2 + 1))


def experts_stage(g, l, acc):
    nc, d = g.nc, g.dram
    UR = 4
    u_in = [g.sem(f"u_loaded{i}") for i in range(UR)]
    g_in = [g.sem(f"g_loaded{i}") for i in range(2)]
    v_in = [g.sem(f"v_loaded{i}") for i in range(2)]
    h_ready, h_taken, w_ready, y_ready, y_taken = (g.sem(f"exp_{x}") for x in ("h_ready", "h_taken", "weights_ready", "y_ready", "y_taken"))
    with ExitStack() as st, nc.Block() as block:
        u = g.sb(st, "u", [P, UR, KC, P])
        gw = g.sb(st, "gw", [P, 2, NT // GT_N, GB, GT_N])
        vv = g.sb(st, "vv", [P, 2, GB, D])
        hh = g.sb(st, "hh", [P, 2, NT])

        @block.sync
        def _(sync):
            sync.sem_inc(h_ready, UR)
            sync.sem_inc(y_ready, 4 * TILES)
            with sync.Fori(0, NG // 2) as i:
                for q in range(2):
                    sync.wait_ge(y_ready, i * (4 * TILES) + (q + 1) * 2 * TILES)
                    sync.dma_start(gw[:, q, :, :, :].rearrange("p t b n -> p (t b n)"),
                                   d["gates"][:, bass.ds(i * 2 + q, 1), :, :].rearrange("p g t m -> p (g t m)")).then_inc(g_in[q], 16)
                    for b in range(GB):
                        j = q * GB + b
                        sync.wait_ge(h_ready, i * (2 * GB) + (j + 1))
                        sync.dma_start(u[:, j % UR, :, :], d["peer_u"][l, i * (2 * GB) + j]).then_inc(u_in[j % UR], 16)
                        if b == 1:
                            sync.dma_start(vv[:, q, :, :].rearrange("p b n -> p (b n)"),
                                           d["peer_v"][l, :, bass.ds((i * 2 + q) * (GB * D), GB * D)]).then_inc(v_in[q], 16)

        @block.tensor
        def _(pe):
            def hidden(i, q, count):
                for b in range(GB):
                    j = q * GB + b
                    pe.wait_ge(u_in[j % UR], count(i, 2 * GB // UR, j // UR + 1) * 16)
                    pe.wait_ge(h_taken, count(i, 2 * GB, j + 1))
                    for bank, (x, y) in enumerate(((0, NS), (NS, NT))):
                        for kc in range(KC):
                            mm = pe.matmul(g.ps[:, 2 * (j % 2) + bank, 0:y - x], u[:, j % UR, kc, :], g.hT[:, kc, x:y],
                                           start=(kc == 0), stop=(kc == KC - 1))
                    mm.then_inc(h_ready, 1)

            def output(i, q, count):
                pe.wait_ge(v_in[q], count(i, 1, 1) * 16)
                pe.wait_ge(w_ready, count(i, 2 * GB, (q + 1) * GB + 2))
                for n in range(2 * TILES):
                    t, half = divmod(n, 2)
                    pe.wait_ge(y_taken, count(i, 4 * TILES, q * 2 * TILES + n + 1))
                    bank = 4 + (q * 2 * TILES + n) % 4
                    for b in range(GB):
                        mm = pe.matmul(g.ps[:, bank, :], gw[:, q, t, b, :], vv[:, q, b, half * 512:(half + 1) * 512],
                                       start=(b == 0), stop=(b == GB - 1))
                    mm.then_inc(y_ready, 1)

            count = lambda i, per, n: i * per + n
            hidden(0, 0, count)
            with pe.Fori(0, NG // 2 - 1) as i:
                hidden(i, 1, count)
                output(i, 0, count)
                hidden(i + 1, 0, count)
                output(i, 1, count)
            last = NG // 2 - 1
            hidden(last, 1, count)
            output(last, 0, count)
            output(last, 1, count)

        @block.scalar
        def _(act):
            act.sem_inc(h_taken, 2)
            with act.Fori(0, NG // 2) as i:
                for j in range(2 * GB):
                    act.wait_ge(h_ready, i * (2 * GB) + (j + 1 + UR))
                    act.wait_ge(w_ready, i * (2 * GB) + (j + 1))
                    nc.scalar.activation(hh[:, j % 2, :], g.flat[:, 1024 * (j % 2):1024 * (j % 2) + NT], ACT.Gelu).then_inc(h_taken, 1)

        @block.vector
        def _(ve):
            def weights(i, q, count):
                ve.wait_ge(g_in[q], count(i, 1, 1) * 16)
                for b in range(GB):
                    j = q * GB + b
                    ve.wait_ge(h_taken, count(i, 2 * GB, j + 1 + 2))
                    ve.tensor_tensor(gw[:, q, :, b, :], gw[:, q, :, b, :], hh[:, j % 2, :].rearrange("p (t n) -> p t n", n=GT_N),
                                     ALU.mult).then_inc(w_ready, 1)

            def take(i, q, count):
                for n in range(2 * TILES):
                    t, half = divmod(n, 2)
                    m = q * 2 * TILES + n
                    ve.wait_ge(y_ready, count(i, 4 * TILES, m + 1 + 4 * TILES))
                    a = acc[:, t, half * 512:(half + 1) * 512]
                    ve.tensor_tensor(a, a, g.ps[:, 4 + m % 4, :], ALU.add).then_inc(y_taken, 1)

            count = lambda i, per, n: i * per + n
            ve.memset(acc[:, :, :], 0.0).then_inc(y_taken, 4)
            ve.wait_ge(y_taken, 4)
            ve.sem_inc(w_ready, 2)
            weights(0, 0, count)
            with ve.Fori(0, NG // 2 - 1) as i:
                weights(i, 1, count)
                take(i, 0, count)
                weights(i + 1, 0, count)
                take(i, 1, count)
            last = NG // 2 - 1
            weights(last, 1, count)
            take(last, 0, count)
            take(last, 1, count)


def fold_stage(g, acc):
    nc = g.nc
    tr, tk = g.sem("fold_transposed"), g.sem("fold_taken")
    with nc.Block() as block:
        @block.tensor
        def _(pe):
            for t in range(TILES):
                if t >= 4:
                    pe.wait_ge(tk, t - 3)
                for kc in range(KC):
                    at = 1024 * (t % 4) + kc * P
                    mm = pe.transpose(g.flat[:, at:at + P], acc[:, t, kc * P:(kc + 1) * P], g.ident)
                mm.then_inc(tr, 1)

        @block.vector
        def _(ve):
            for t in range(TILES):
                ve.wait_ge(tr, t + 1)
                c = int(t == TILES - 1)
                for kc in range(KC):
                    at = 1024 * (t % 4) + kc * P
                    x = g.xT[:, kc, t * P:(t + 1) * P]
                    i = ve.scalar_tensor_tensor(x, g.flat[:, at:at + P], g.modT[:, 5 * KC + kc, c:c + 1], x, ALU.mult, ALU.add)
                i.then_inc(tk, 1)


def build(nc, dram, upto=99):
    ctx = ExitStack()
    with ctx:
        g = Program(nc, ctx, dram)
        g.ps = ctx.enter_context(nc.psum_tensor("ps", [P, 8, 512], F32))
        g.flat = g.ps[:, :, :].rearrange("p b n -> p (b n)")
        g.xT = g.sb(ctx, "xT", [P, KC, NT])
        g.keep = g.sb(ctx, "keep", [P, NKEEP])
        g.ident, g.ones, g.bones, g.iota = (g.keep[:, i * P:(i + 1) * P] for i in range(4))
        g.vec = g.sb(ctx, "vec", [P, NVEC])
        g.cond = g.sb(ctx, "cond", [P, KC, 2])
        g.scond = g.sb(ctx, "scond", [P, KC, 2])
        g.tiny = g.sb(ctx, "tiny", [P, 8 + DK])
        g.lam = g.sb(ctx, "lam", [P, 4])
        g.omka = g.sb(ctx, "omka", [P, 2])
        g.nsp = g.sb(ctx, "nsp", [P, 4])
        g.nsp2 = g.sb(ctx, "nsp2", [P, 4])
        g.modT = g.sb(ctx, "modT", [P, 6 * KC, 2])
        g.gain = g.sb(ctx, "gain", [P, 2, KC, 2])
        x_in = ctx.enter_context(nc.semaphore("x_loaded"))
        y_out = ctx.enter_context(nc.semaphore("y_stored"))

        with nc.Block() as block:
            @block.sync
            def _(sync):
                sync.dma_start(g.xT[:, :, :], dram["x"]).then_inc(x_in, 16)
                sync.wait_ge(x_in, 16)

        with nc.Fori(0, DEPTH) as l:
            load_stage(g, l)
            mod_stage(g, l)
            with ExitStack() as s1:
                g.outT = g.sb(s1, "outT", [P, KC, NT])
                g.proj = g.sb(s1, "proj", [P, NPROJ, NT])
                g.vtok = g.sb(s1, "vtok", [P, TILES, VTOK])
                with ExitStack() as s2:
                    g.hT = g.sb(s2, "hT", [P, KC, NT])
                    norm_stage(g, "norm1", g.hT, lambda kc, c: g.gain[:, 0, kc, c:c + 1], lambda kc, c: g.modT[:, kc, c:c + 1])
                    proj_stage(g, l)
                with ExitStack() as s2:
                    g.kctx = g.sb(s2, "kctx", [P, CB, PAST])
                    g.vctx = g.sb(s2, "vctx", [P, PAST // P, 512])
                    rope_stage(g, l)
                    attention_stage(g, l)
                subln_stage(g)
                lru_stage(g, l)
                with ExitStack() as s2:
                    keep = (g.sb(s2, "ar", [P, 2, CA, TILES, 2, P]), g.sb(s2, "gt", [P, CA, NT]), g.sb(s2, "pc", [P, 2, CA, NT // CH]))
                    rwkv_prepare(g, l, keep)
                    rwkv_scan(g, l, keep)
                    rwkv_finish(g, keep)
                gemm(g, "wout", lambda oc: dram["w_out"][l, oc], KC, 4, g.outT, residual_take(g, 2))
            with ExitStack() as s1:
                g.hT = g.sb(s1, "hT", [P, KC, NT])
                norm_stage(g, "norm2", g.hT, lambda kc, c: g.gain[:, 1, kc, c:c + 1], lambda kc, c: g.modT[:, 3 * KC + kc, c:c + 1])
                with ExitStack() as s2:
                    sel = g.sb(s2, "sel", [P, 3, NT])
                    with ExitStack() as s3:
                        qT = g.sb(s3, "qT", [P, 2 * PH, NT])
                        gemm(g, "query", lambda oc: dram["peer_wq"][l, oc], 2 * PH, 4, g.hT,
                             lambda ve, oc, sums: ve.tensor_copy(qT[:, bass.ds(oc, 1), :], sums))
                        select_stage(g, l, qT, sel)
                    gates_stage(g, l, sel)
                acc = g.sb(s1, "acc", [P, TILES, D])
                experts_stage(g, l, acc)
                fold_stage(g, acc)
            nums = sorted(s.num for s in g.sems)
            assert nums == list(range(nums[0], nums[-1] + 1))
            with nc.Block() as block:
                @block.gpsimd
                def _(pool):
                    pool.sem_clear(range(nums[0], nums[-1] + 1))

        with ExitStack() as s1:
            out = g.sb(s1, "out", [P, KC, NT])
            norm_stage(g, "final", out, lambda kc, c: g.v("final", kc, kc + 1), None)
            with nc.Block() as block:
                @block.sync
                def _(sync):
                    sync.dma_start(dram["y"], out[:, :, :]).then_inc(y_out, 16)
                    sync.wait_ge(y_out, 16)


def constants():
    i = np.arange(P)
    same = (i[:, None] // CH) == (i[None, :] // CH)
    s, t = i[:, None], i[None, :]
    perm = np.zeros((P, P))
    for m in range(0, P, 2):
        perm[m + 1, m] = -1.0
        perm[m, m + 1] = 1.0
    tok = np.arange(NS)
    row, col = (tok // GRID_W).astype(np.float32), (tok % GRID_W).astype(np.float32)
    pairs = DK // 4
    inv = (np.float32(10000.0) ** (-np.arange(pairs, dtype=np.float32) / np.float32(pairs))).astype(np.float32)
    ang = np.concatenate([row[:, None] * inv, col[:, None] * inv], axis=-1).astype(np.float32)
    pair = (i % DK) // 2
    n = np.arange(NT)
    parts = {
        "ident": np.eye(P), "ones": np.ones((P, P)), "bones": same, "iota": np.broadcast_to(i, (P, P)), "perm": perm,
        "maskF": np.concatenate([same & (s < t), same & (s <= t)], 1),
        "maskB": np.concatenate([same & (s > t), same & (s >= t)], 1),
        "lowF": same & (t < s), "lowB": same & (t > s),
        "scanF": np.broadcast_to(n % CH != 0, (P, NT)), "scanB": np.broadcast_to(n % CH != CH - 1, (P, NT)),
        "cos": np.cos(ang).T[pair], "sin": np.sin(ang).T[pair],
    }
    return np.concatenate([np.asarray(parts[k], np.float32) for k in CI], axis=1)


def kernel(**inputs):
    import concourse.bacc as bacc
    from concourse.bass_utils import run_bass_kernel_spmd

    w = {k: np.asarray(x) for k, x in inputs.items()}
    L = DEPTH

    def chunks(x):
        n = x.shape[-1] // P
        return x.reshape(L, x.shape[1] // P, P, n, P).transpose(0, 3, 2, 1, 4)

    def vec(x):
        return x.reshape(L, -1, P).transpose(0, 2, 1)

    wi = w["w_in"]
    va, vb = wi[:, :, 512:768], wi[:, :, 768 + 1024:768 + 1536]
    lora = [w[k].transpose(0, 2, 1, 3).reshape(L, D, P) for k in ("rwkv_wA", "rwkv_aA")]
    w_proj = np.concatenate([wi[:, :, 0:768 + 1024], wi[:, :, 768 + 1536:], *lora, w["rwkv_gA"]], axis=2)
    lam_init = np.array([0.8 - 0.6 * np.exp(-0.3 * l) for l in range(L)], np.float32)
    cols = {
        "mod_b": vec(w["mod_b"]), "n1": vec(w["norm1_g"]), "n2": vec(w["norm2_g"]),
        "w0": vec(w["rwkv_w0"].reshape(L, -1)), "a0": vec(w["rwkv_a0"].reshape(L, -1)),
        "kk": vec(w["rwkv_kk"]), "ka": vec(w["rwkv_ka"]), "rk": vec(w["rwkv_rk"].reshape(L, -1)),
        "lng": vec(w["rwkv_ln_g"]), "sub": np.concatenate([w["diff_subln_g"]] * 2, 1)[:, :, None],
        "convw": vec(w["lru_conv_w"].reshape(L, -1)), "convb": vec(w["lru_conv_b"]),
        "ba": vec(w["lru_ba"].reshape(L, -1)), "bx": vec(w["lru_bx"].reshape(L, -1)), "lam": vec(w["lru_lambda"].reshape(L, -1)),
        "lq": np.broadcast_to(np.concatenate([w[f"diff_{n}"] for n in ("lq1", "lk1", "lq2", "lk2")], 1)[:, None, :], (L, P, 4 * DK)),
        "laminit": np.broadcast_to(lam_init[:, None, None], (L, P, 1)),
        "final": np.broadcast_to(w["final_norm_g"].reshape(1, KC, P).transpose(0, 2, 1), (L, P, KC)),
        "h0": vec(w["state_lru"][0].reshape(L, -1)),
    }
    x = np.concatenate([w["x_sample"][0], w["x_prompt"][0]], 0)
    lru = np.stack([w["lru_wa"], w["lru_wx"]], 1).reshape(L, 2, 2, CC, 2, HD, HD)
    arrays = {
        "consts": constants(),
        "vecs": np.concatenate([cols[k] for k in VI], axis=2),
        "x": x.T.reshape(KC, P, NT).transpose(1, 0, 2),
        "cond": np.stack([w["c"][0], w["c_ctx"]], 1).reshape(KC, P, 2).transpose(1, 0, 2),
        "mod_w": chunks(w["mod_w"]),
        "w_proj": chunks(w_proj),
        "w_v": np.concatenate([va, vb], 2).reshape(L, KC, P, VTOK).transpose(0, 2, 1, 3),
        "w_out": chunks(w["w_out"]),
        "cache_k": w["cache_k"][0].transpose(0, 1, 3, 2).reshape(L, CB, P, PAST).transpose(0, 2, 1, 3),
        "cache_v": w["cache_v"][0].transpose(0, 2, 1, 3).reshape(L, PAST // P, P, HB * HD).transpose(0, 2, 1, 3),
        "state_rwkv": w["state_rwkv"][0].reshape(L, 2, CA, 2, HD, HD).transpose(0, 3, 5, 1, 2, 4),
        "rwkv_B": np.stack([w["rwkv_wB"].reshape(L, P, CA * P), w["rwkv_aB"].reshape(L, P, CA * P)], 2),
        "rwkv_gB": w["rwkv_gB"],
        "lru_w": lru.transpose(0, 1, 4, 5, 2, 3, 6),
        "peer_wq": chunks(w["peer_wq"]),
        "peer_keys": w["peer_keys"].reshape(L, 2 * PH, NKEY, P).transpose(0, 3, 1, 2),
        "peer_u": w["peer_u"].reshape(L, NKEY, NKEY, KC, P).transpose(0, 2, 4, 3, 1),
        "peer_v": w["peer_v"].reshape(L, NKEY, NKEY * D),
    }
    arrays = {k: np.ascontiguousarray(a) for k, a in arrays.items()}
    nc = bacc.Bacc("TRN2", target_bir_lowering=False, num_devices=1)
    dram = {k: nc.dram_tensor(k, a.shape, F32, kind="ExternalInput").ap() for k, a in arrays.items()}
    outs = {
        "y": (P, KC, NT), "new_k": (L, P, CB, NPR), "new_v": (L, P, 512),
        "new_rwkv": (L, 2, HD, 2, CA, HD), "new_lru": (L, P, 2, CC),
    }
    for k, s in outs.items():
        dram[k] = nc.dram_tensor(k, s, F32, kind="ExternalOutput").ap()
    dram["gates"] = nc.dram_tensor("gates", (P, NG, NT // GT_N, GB * GT_N), F32, kind="Internal").ap()
    build(nc, dram)
    r = run_bass_kernel_spmd(nc, [arrays], core_ids=[0]).results[0]
    y = r["y"].transpose(2, 1, 0).reshape(NT, D)
    return (
        y[None, NS:], y[None, :NS],
        r["new_k"].transpose(0, 2, 1, 3).reshape(L, HB, HD, NPR).transpose(0, 1, 3, 2)[None],
        r["new_v"].reshape(L, NPR, HB, HD).transpose(0, 2, 1, 3)[None],
        r["new_rwkv"].transpose(0, 3, 4, 1, 5, 2).reshape(L, 2, HA, HD, HD)[None],
        r["new_lru"].transpose(0, 2, 3, 1).reshape(L, 2, CC * P)[None],
    )
```

```python
from contextlib import ExitStack

import numpy as np

import concourse.bass as bass
from concourse import mybir

F32 = mybir.dt.float32
U32 = mybir.dt.uint32
F32R = mybir.dt.float32r
ALU = mybir.AluOpType
ACT = mybir.ActivationFunctionType
AX = mybir.AxisListType

P = 128
D = 1024
DEPTH = 2
NS = 512
NPR = 128
NT = NS + NPR
TILES = NT // P
PAST = 256
GRID_W = 64
KC = D // P
HD = 64
CA = 2
HA = 4
HB = 8
CB = 4
DK = 32
CC = 2
DECAY_SCALE = 0.606531
CH = 64
PH = 8
TOPK = 16
NKEY = 128
LRU_C = 8.0
RMS_EPS = 1e-6
SUB_EPS = 1e-5
GN_EPS = 64e-5
NEG = -3.0e38

R0, K0, V0, Q0, B0, X0, G0, LW, LA, LG = 0, 2, 4, 6, 10, 14, 16, 18, 19, 20
NPROJ = 21
VTOK = 768

CI = {}
_at = 0
for _n, _w in (("ident", P), ("ones", P), ("bones", P), ("iota", P), ("perm", P), ("maskF", 2 * P), ("maskB", 2 * P),
               ("lowF", P), ("lowB", P), ("scanF", NT), ("scanB", NT), ("cos", NS), ("sin", NS)):
    CI[_n] = (_at, _w)
    _at += _w
NCONST = _at
NKEEP = 4 * P

VI = {}
_at = 0
for _n, _w in (("mod_b", 48), ("n1", 8), ("n2", 8), ("w0", 4), ("a0", 4), ("kk", 2), ("ka", 2), ("rk", 2),
               ("lng", 2), ("sub", 1), ("convw", 8), ("convb", 2), ("ba", 4), ("bx", 4), ("lam", 4),
               ("lq", 4 * DK), ("laminit", 1), ("final", 8), ("h0", 4)):
    VI[_n] = (_at, _w)
    _at += _w
NVEC = _at


class Counter:

    def __init__(self, eng, sem):
        self.eng, self.sem, self.n = eng, sem, 0

    def did(self, inst):
        inst.then_inc(self.sem, 1)
        self.n += 1

    def wait(self):
        self.eng.wait_ge(self.sem, self.n)

    def then(self, inst):
        self.did(inst)
        self.wait()


class Program:
    def __init__(self, nc, ctx, dram):
        self.nc, self.ctx, self.dram = nc, ctx, dram
        self.sems = []
        self.n = 0

    def sem(self, name):
        s = self.phase.enter_context(self.nc.semaphore(name))
        self.sems.append(s)
        return s

    def begin(self):
        self.phase, self.sems = ExitStack(), []

    def end(self):
        nums = sorted(s.num for s in self.sems)
        runs = [n for n in nums if n - 1 not in nums]
        with self.nc.Block() as block:
            @block.gpsimd
            def _(pool):
                for a in runs:
                    b = a
                    while b in nums:
                        b += 1
                    pool.sem_clear(range(a, b))
        self.phase.close()

    def sb(self, st, name, shape, dt=F32):
        self.n += 1
        return st.enter_context(self.nc.sbuf_tensor(f"{name}_{self.n}", shape, dt))


def load_stage(g, l):
    nc, d = g.nc, g.dram
    loaded, done, ex = g.sem("vectors_loaded"), g.sem("lambda_steps"), g.sem("lambda_exps")
    silu, sp = g.sem("cond_silu"), g.sem("softplus_steps")
    vec = g.vec

    def v(name, a=0, b=None):
        at, w = VI[name]
        return vec[:, at + a:at + (w if b is None else b)]

    g.v = v
    with nc.Block() as block:
        @block.sync
        def _(sync):
            sync.dma_start(vec[:, :], d["vecs"][l]).then_inc(loaded, 16)
            sync.dma_start(g.cond[:, :, :], d["cond"]).then_inc(loaded, 16)
            sync.dma_start(g.keep[:, :], d["consts"][:, 0:NKEEP]).then_inc(loaded, 16)

        @block.vector
        def _(ve):
            c = Counter(ve, done)
            ve.wait_ge(loaded, 48)
            lq = v("lq").rearrange("p (a k) -> p a k", a=4)
            for i in range(2):
                c.then(ve.tensor_tensor(g.tiny[:, 8:8 + DK], lq[:, 2 * i, :], lq[:, 2 * i + 1, :], ALU.mult))
                c.then(ve.tensor_reduce(g.tiny[:, i:i + 1], g.tiny[:, 8:8 + DK], AX.X, ALU.add))
            ve.wait_ge(ex, 1)
            c.then(ve.tensor_tensor(g.lam[:, 0:1], g.tiny[:, 2:3], g.tiny[:, 3:4], ALU.subtract))
            c.then(ve.tensor_tensor(g.lam[:, 0:1], g.lam[:, 0:1], v("laminit"), ALU.add))
            c.then(ve.tensor_scalar(g.lam[:, 1:2], g.lam[:, 0:1], -1.0, None, ALU.mult))
            c.then(ve.tensor_scalar(g.lam[:, 2:3], v("laminit"), -1.0, 1.0, ALU.mult, ALU.add))
            c.then(ve.tensor_tensor(g.lam[:, 3:4], g.lam[:, 2:3], v("sub"), ALU.mult))
            c.then(ve.tensor_scalar(g.omka[:, :], v("ka"), -1.0, 1.0, ALU.mult, ALU.add))
            ve.wait_ge(sp, 1)
            c.then(ve.tensor_scalar(g.nsp[:, :], g.nsp[:, :], -LRU_C, None, ALU.mult))

        @block.scalar
        def _(act):
            c = Counter(act, sp)
            act.wait_ge(loaded, 48)
            nc.scalar.activation(g.scond[:, :, :], g.cond[:, :, :], ACT.Silu).then_inc(silu, 1)
            act.wait_ge(done, 4)
            nc.scalar.activation(g.tiny[:, 2:4], g.tiny[:, 0:2], ACT.Exp).then_inc(ex, 1)
            nc.scalar.activation(g.nsp2[:, :], v("lam"), ACT.Exp, scale=-1.0).then_inc(silu, 1)
            act.wait_ge(silu, 2)
            c.did(nc.scalar.activation(g.nsp[:, :], g.nsp2[:, :], ACT.Ln, bias=1.0))


def gemm_plain(g, name, weights, n_out, R, rhs, take, n=NT, wring=None, extra=None):
    nc = g.nc
    w_in = [g.sem(f"{name}_w_loaded{i}") for i in range(R)]
    w_free, ready, taken = g.sem(f"{name}_w_used"), g.sem(f"{name}_sums_ready"), g.sem(f"{name}_sums_taken")
    with ExitStack() as st, nc.Block() as block:
        ring = wring if wring is not None else g.sb(st, f"{name}_w", [P, R, KC, P])

        @block.sync
        def _(sync):
            sync.sem_inc(w_free, R)
            with sync.Fori(0, n_out // R) as i:
                for j in range(R):
                    sync.wait_ge(w_free, i * R + (j + 1))
                    sync.dma_start(ring[:, j, :, :], weights(i * R + j)).then_inc(w_in[j], 16)
            if extra and "sync" in extra:
                extra["sync"](sync)

        @block.tensor
        def _(pe):
            with pe.Fori(0, n_out // R) as i:
                for j in range(R):
                    pe.wait_ge(w_in[j], i * 16 + 16)
                    pe.wait_ge(taken, i * R + (j + 1))
                    for a, b in ((0, min(n, NS)), (NS, n)) if n > NS else ((0, n),):
                        for kc in range(KC):
                            mm = pe.matmul(g.ps[:, 2 * j + (a == NS), 0:b - a], ring[:, j, kc, :], rhs[:, kc, a:b],
                                           start=(kc == 0), stop=(kc == KC - 1))
                    mm.then_inc(ready, 1)
                    pe.wait_ge(ready, i * R + (j + 1))
                    pe.sem_inc(w_free, 1)
            if extra and "tensor" in extra:
                extra["tensor"](pe)

        @block.vector
        def _(ve):
            ve.sem_inc(taken, R)
            with ve.Fori(0, n_out // R) as i:
                for j in range(R):
                    ve.wait_ge(ready, i * R + (j + 1))
                    take(ve, i * R + j, g.flat[:, 1024 * j:1024 * j + n]).then_inc(taken, 1)
            if extra and "vector" in extra:
                extra["vector"](ve)

        if extra and "scalar" in extra:
            @block.scalar
            def _(act):
                extra["scalar"](act)


def split3(pe, out, lhs, rhs, start=True, stop=True):
    pe.matmul(out, lhs[1], rhs[0], start=start, stop=False)
    pe.matmul(out, lhs[0], rhs[1], start=False, stop=False)
    return pe.matmul(out, lhs[0], rhs[0], start=False, stop=stop)


def halves(ap):
    return ap.rearrange("p (h n) -> p h n", n=H2)


def gemm(g, name, weights, n_out, R, SR, rhs, take):
    nc = g.nc
    w_in = [g.sem(f"{name}_w_loaded{i}") for i in range(R)]
    w_hi, w_lo, ready, taken = (g.sem(f"{name}_{x}") for x in ("w_high", "w_low", "sums_ready", "sums_taken"))
    with ExitStack() as st, nc.Block() as block:
        raw = g.sb(st, f"{name}_raw", [P, R, KC, P])
        hi = g.sb(st, f"{name}_hi", [P, SR, KC, P], F32R)
        lo = g.sb(st, f"{name}_lo", [P, SR, KC, P], F32R)

        @block.sync
        def _(sync):
            sync.sem_inc(w_lo, R)
            with sync.Fori(0, n_out // R) as i:
                for j in range(R):
                    sync.wait_ge(w_lo, i * R + (j + 1))
                    sync.dma_start(raw[:, j, :, :], weights(i * R + j)).then_inc(w_in[j], 16)

        @block.scalar
        def _(act):
            act.sem_inc(ready, SR)
            with act.Fori(0, n_out // R) as i:
                for j in range(R):
                    act.wait_ge(w_in[j], i * 16 + 16)
                    act.wait_ge(ready, i * R + (j + 1))
                    nc.scalar.activation(hi[:, j % SR, :, :], raw[:, j, :, :], ACT.Copy).then_inc(w_hi, 1)

        @block.tensor
        def _(pe):
            with pe.Fori(0, n_out // R) as i:
                for j in range(R):
                    pe.wait_ge(w_lo, i * R + (j + 1 + R))
                    pe.wait_ge(taken, i * R + (j + 1))
                    w = (hi[:, j % SR, :, :], lo[:, j % SR, :, :])
                    for h in range(2):
                        cols = slice(h * H2, (h + 1) * H2)
                        for kc in range(KC):
                            mm = split3(pe, g.ps[:, 2 * j + h, 0:H2], [x[:, kc, :] for x in w], [x[:, kc, cols] for x in rhs],
                                        start=(kc == 0), stop=(kc == KC - 1))
                    mm.then_inc(ready, 1)

        @block.vector
        def _(ve):
            ve.sem_inc(taken, R)

            def low(i, j):
                ve.wait_ge(w_hi, i * R + (j + 1))
                s = (j % R) % SR
                ve.tensor_tensor(lo[:, s, :, :], raw[:, j % R, :, :], hi[:, s, :, :].bitcast(F32), ALU.subtract).then_inc(w_lo, 1)

            def turn(i, last):
                for j in range(R):
                    if not (last and j == R - 1):
                        low(i, j + 1)
                    ve.wait_ge(ready, i * R + (j + 1 + SR))
                    take(ve, i * R + j, g.ps[:, 2 * j:2 * j + 2, 0:H2]).then_inc(taken, 1)

            low(0, 0)
            with ve.Fori(0, n_out // R - 1) as i:
                turn(i, False)
            turn(n_out // R - 1, True)


def mod_stage(g, l):
    nc, d, v = g.nc, g.dram, g.v
    gemm_plain(g, "mod", lambda oc: d["mod_w"][l, oc], 6 * KC, 4, g.scond,
         lambda ve, oc, sums: ve.tensor_copy(g.modT[:, bass.ds(oc, 1), :], sums), n=2)
    steps = g.sem("mod_steps")
    with nc.Block() as block:
        @block.vector
        def _(ve):
            c = Counter(ve, steps)
            c.then(ve.tensor_tensor(g.modT[:, :, :], g.modT[:, :, :],
                                    v("mod_b").unsqueeze(2).broadcast_to([P, 6 * KC, 2]), ALU.add))
            for i, (name, part) in enumerate((("n1", 1), ("n2", 4))):
                c.then(ve.tensor_scalar(g.gain[:, i, :, :], g.modT[:, part * KC:(part + 1) * KC, :], 1.0, None, ALU.add))
                c.then(ve.tensor_tensor(g.gain[:, i, :, :], g.gain[:, i, :, :],
                                        v(name).unsqueeze(2).broadcast_to([P, KC, 2]), ALU.mult))


def norm_stage(g, name, out, gain, shift, low=None):
    nc = g.nc
    sq_ready, sum_ready, r_ready, steps = (g.sem(f"{name}_{x}") for x in ("squared", "summed", "root", "steps"))
    scaled, normed, lowed = g.sem(f"{name}_scaled"), g.sem(f"{name}_normed"), g.sem(f"{name}_low")
    with ExitStack() as st, nc.Block() as block:
        sq = g.sb(st, "sq", [P, 2, NT])
        rs = g.sb(st, "rs", [P, 2, NT])
        t = g.sb(st, "t", [P, 3, NT])
        raw = (lambda kc: out[:, kc, :]) if low is None else (lambda kc: t[:, kc % 3, :])

        @block.scalar
        def _(act):
            for kc in range(KC):
                if kc >= 2:
                    act.wait_ge(sum_ready, kc - 1)
                nc.scalar.activation(sq[:, kc % 2, :], g.xT[:, kc, :], ACT.Square).then_inc(sq_ready, 1)
            act.wait_ge(steps, 1)
            nc.scalar.activation(rs[:, 1, :], rs[:, 0, :], ACT.Sqrt).then_inc(r_ready, 1)
            for kc in range(KC):
                act.wait_ge(scaled, kc + 1)
                for c, (a, b) in enumerate(((0, NS), (NS, NT))):
                    last = nc.scalar.activation(raw(kc)[:, a:b], raw(kc)[:, a:b], ACT.Identity,
                                                scale=gain(kc, c), bias=shift(kc, c) if shift else 0.0)
                last.then_inc(normed, 1)
                if low is not None:
                    act.wait_ge(normed, 2 * kc + 1)
                    nc.scalar.activation(out[:, kc, :], raw(kc), ACT.Copy).then_inc(normed, 1)

        @block.tensor
        def _(pe):
            for kc in range(KC):
                pe.wait_ge(sq_ready, kc + 1)
                for bank, (a, b) in enumerate(((0, NS), (NS, NT))):
                    mm = pe.matmul(g.ps[:, bank, 0:b - a], g.ones, sq[:, kc % 2, a:b], start=(kc == 0), stop=(kc == KC - 1))
                mm.then_inc(sum_ready, 1)

        @block.vector
        def _(ve):
            c = Counter(ve, steps)
            ve.wait_ge(sum_ready, KC)
            c.did(ve.tensor_scalar(rs[:, 0, :], g.flat[:, 0:NT], 1.0 / D, RMS_EPS, ALU.mult, ALU.add))
            ve.wait_ge(r_ready, 1)
            c.then(ve.reciprocal(rs[:, 0, :], rs[:, 1, :]))

            def lower(kc):
                ve.wait_ge(normed, 2 * kc + 2)
                ve.tensor_tensor(low[:, kc, :], raw(kc), out[:, kc, :].bitcast(F32), ALU.subtract).then_inc(lowed, 1)

            for kc in range(KC):
                if low is not None and kc >= 3:
                    ve.wait_ge(lowed, kc - 2)
                ve.tensor_tensor(raw(kc), g.xT[:, kc, :], rs[:, 0, :], ALU.mult).then_inc(scaled, 1)
                if low is not None and kc >= 1:
                    lower(kc - 1)
            if low is not None:
                lower(KC - 1)


def split_stage(g, name, src, hi, lo):
    nc = g.nc
    high = g.sem(f"{name}_high")
    with nc.Block() as block:
        @block.scalar
        def _(act):
            for kc in range(KC):
                nc.scalar.activation(hi[:, kc, :], src[:, kc, :], ACT.Copy).then_inc(high, 1)

        @block.vector
        def _(ve):
            for kc in range(KC):
                ve.wait_ge(high, kc + 1)
                ve.tensor_tensor(lo[:, kc, :], src[:, kc, :], hi[:, kc, :].bitcast(F32), ALU.subtract)


VP = 256


def proj_stage(g, l):
    nc, d = g.nc, g.dram
    gemm(g, "proj", lambda oc: d["w_proj"][l, oc], NPROJ, 3, 3, g.h2,
         lambda ve, oc, sums: ve.tensor_copy(g.proj[:, bass.ds(oc, 1), :].rearrange("p o (h n) -> p (o h) n", n=H2), sums))
    w_in, w_hi, w_lo, ready, taken = (g.sem(f"vtok_{x}") for x in ("w_loaded", "w_high", "w_low", "ready", "taken"))
    NP = VTOK // VP
    with ExitStack() as st, nc.Block() as block:
        raw = g.sb(st, "wv", [P, KC, VP])
        hi = g.sb(st, "wvh", [P, 2, KC, VP], F32R)
        lo = g.sb(st, "wvl", [P, 2, KC, VP], F32R)

        @block.sync
        def _(sync):
            for c in range(NP):
                if c:
                    sync.wait_ge(w_lo, c)
                sync.dma_start(raw[:, :, :], d["w_v"][l, :, :, c * VP:(c + 1) * VP]).then_inc(w_in, 16)

        @block.scalar
        def _(act):
            for c in range(NP):
                act.wait_ge(w_in, 16 * (c + 1))
                if c >= 2:
                    act.wait_ge(ready, TILES * (c - 1))
                nc.scalar.activation(hi[:, c % 2, :, :], raw[:, :, :], ACT.Copy).then_inc(w_hi, 1)

        @block.tensor
        def _(pe):
            for c in range(NP):
                pe.wait_ge(w_lo, c + 1)
                for t in range(TILES):
                    n = c * TILES + t
                    if n >= 8:
                        pe.wait_ge(taken, n - 7)
                    for kc in range(KC):
                        mm = split3(pe, g.ps[:, n % 8, 0:VP], [x[:, kc, t * P:(t + 1) * P] for x in g.h2],
                                    [x[:, c % 2, kc, :] for x in (hi, lo)], start=(kc == 0), stop=(kc == KC - 1))
                    mm.then_inc(ready, 1)

        @block.vector
        def _(ve):
            def low(c):
                ve.wait_ge(w_hi, c + 1)
                ve.tensor_tensor(lo[:, c % 2, :, :], raw[:, :, :], hi[:, c % 2, :, :].bitcast(F32), ALU.subtract).then_inc(w_lo, 1)

            low(0)
            low(1)
            for c in range(NP):
                for t in range(TILES):
                    n = c * TILES + t
                    ve.wait_ge(ready, n + 1)
                    ve.tensor_copy(g.vtok[:, t, c * VP:(c + 1) * VP], g.ps[:, n % 8, 0:VP]).then_inc(taken, 1)
                if c + 2 < NP:
                    low(c + 2)


def rope_stage(g, l):
    nc, d = g.nc, g.dram
    loaded, out_done = g.sem("rope_consts_loaded"), g.sem("cache_stored")
    rot, cosd, sind = g.sem("rotated"), g.sem("cos_done"), g.sem("sin_done")
    added = g.sem("rope_added")
    with ExitStack() as st, nc.Block() as block:
        cs = g.sb(st, "ropecs", [P, 2, NS])
        perm = g.sb(st, "perm", [P, P])
        tmp = g.sb(st, "ropetmp", [P, 2, 2, NS])
        at = CI["cos"][0]

        @block.sync
        def _(sync):
            sync.dma_start(cs[:, :, :], d["consts"][:, at:at + 2 * NS]).then_inc(loaded, 16)
            sync.dma_start(perm[:, :], d["consts"][:, CI["perm"][0]:CI["perm"][0] + P]).then_inc(loaded, 16)
            sync.dma_start(g.kctx[:, :, :], d["cache_k"][l]).then_inc(loaded, 16)
            sync.dma_start(g.vctx[:, :, :], d["cache_v"][l]).then_inc(loaded, 16)
            sync.dma_start(d["new_k"][l], g.proj[:, B0:B0 + CB, NS:NT]).then_inc(out_done, 16)
            sync.dma_start(d["new_v"][l], g.vtok[:, TILES - 1, 256:VTOK]).then_inc(out_done, 16)
            sync.wait_ge(out_done, 32)
            sync.wait_ge(loaded, 64)

        @block.tensor
        def _(pe):
            pe.wait_ge(loaded, 64)
            for c in range(8):
                if c >= 2:
                    pe.wait_ge(sind, c - 1)
                pe.matmul(g.ps[:, c % 2, :], perm[:, :], g.proj[:, Q0 + c, 0:NS], start=True, stop=True).then_inc(rot, 1)

        @block.gpsimd
        def _(pool):
            pool.wait_ge(loaded, 64)
            for c in range(8):
                if c >= 2:
                    pool.wait_ge(added, c - 1)
                pool.tensor_tensor(tmp[:, 0, c % 2, :], g.proj[:, Q0 + c, 0:NS], cs[:, 0, :], ALU.mult).then_inc(cosd, 1)

        @block.vector
        def _(ve):
            for c in range(8):
                ve.wait_ge(rot, c + 1)
                ve.tensor_tensor(tmp[:, 1, c % 2, :], g.ps[:, c % 2, :], cs[:, 1, :], ALU.mult).then_inc(sind, 1)
                ve.wait_ge(sind, c + 1)
                ve.wait_ge(cosd, c + 1)
                ve.tensor_tensor(g.proj[:, Q0 + c, 0:NS], tmp[:, 0, c % 2, :], tmp[:, 1, c % 2, :], ALU.add).then_inc(added, 1)


def attention_stage(g, l):
    nc = g.nc
    units = [(h, t) for t in range(TILES) for h in range(HB)]
    scale = DK ** -0.5
    s_ready, m_ready, e_done = g.sem("scores_ready"), g.sem("row_max_ready"), g.sem("exps_ready")
    steps, comb, t_ready = g.sem("attn_steps"), g.sem("probs_combined"), g.sem("probs_transposed")
    pt_ready, o_ready, o_taken = g.sem("probsT_ready"), g.sem("attn_out_ready"), g.sem("attn_out_taken")
    with ExitStack() as st, nc.Block() as block:
        p = g.sb(st, "p", [P, 2, 2, 768])
        pt = g.sb(st, "pt", [P, 2, 768])
        mx = g.sb(st, "mx", [P, 2, 4])
        sm = g.sb(st, "sm", [P, 2, 4])

        def keys(t):
            if t == TILES - 1:
                return [(lambda c, a, b: g.proj[a:b, B0 + c, NS:NT], 0, P)]
            return [(lambda c, a, b: g.proj[a:b, B0 + c, 0:NS], 0, NS), (lambda c, a, b: g.kctx[a:b, c, :], NS, PAST)]

        def values(t, h):
            col = slice(256 + h * HD, 256 + (h + 1) * HD)
            if t == TILES - 1:
                return [g.vtok[:, t, col]]
            return [g.vtok[:, k, col] for k in range(NS // P)] + \
                   [g.vctx[:, k, h * HD:(h + 1) * HD] for k in range(PAST // P)]

        def nk(t):
            return P if t == TILES - 1 else NS + PAST

        @block.tensor
        def _(pe):
            for u in range(len(units) + 2):
                if u < len(units):
                    h, t = units[u]
                    if u >= 1:
                        pe.wait_ge(e_done, u)
                    for c in range(2):
                        base = (h % 2) * HD + c * DK
                        for key, col, n in keys(t):
                            mm = pe.matmul(g.flat[:, 1024 * c + col:1024 * c + col + n],
                                           g.proj[base:base + DK, Q0 + h // 2, t * P:(t + 1) * P],
                                           key(h // 2, base, base + DK), start=True, stop=True)
                    mm.then_inc(s_ready, 1)
                if 1 <= u <= len(units):
                    w = u - 1
                    h, t = units[w]
                    pe.wait_ge(comb, w + 1)
                    if w >= 1:
                        pe.wait_ge(pt_ready, w)
                    for k in range(nk(t) // P):
                        mm = pe.transpose(g.flat[:, 2048 + k * P:2048 + (k + 1) * P], p[:, w % 2, 0, k * P:(k + 1) * P], g.ident)
                    mm.then_inc(t_ready, 1)
                if u >= 2:
                    w = u - 2
                    h, t = units[w]
                    pe.wait_ge(pt_ready, w + 1)
                    if w >= 2:
                        pe.wait_ge(o_taken, w - 1)
                    base = (h % 2) * HD
                    vs = values(t, h)
                    for k, vk in enumerate(vs):
                        mm = pe.matmul(g.ps[base:base + HD, 6 + w % 2, 0:P], vk, pt[:, w % 2, k * P:(k + 1) * P],
                                       start=(k == 0), stop=(k == len(vs) - 1))
                    mm.then_inc(o_ready, 1)

        @block.vector
        def _(ve):
            c = Counter(ve, steps)

            def out(w):
                h, t = units[w]
                base = (h % 2) * HD
                ve.wait_ge(o_ready, w + 1)
                ve.tensor_copy(g.outT[base:base + HD, CA + h // 2, t * P:(t + 1) * P],
                               g.ps[base:base + HD, 6 + w % 2, 0:P]).then_inc(o_taken, 1)

            def row_max(u):
                _, t = units[u]
                ve.wait_ge(s_ready, u + 1)
                c.then(ve.tensor_reduce(mx[:, u % 2, 0:2], g.flat[:, 0:2048].rearrange("p (c k) -> p c k", c=2)[:, :, 0:nk(t)],
                                        AX.X, ALU.max, negate=True))
                ve.tensor_scalar(mx[:, u % 2, 2:4], mx[:, u % 2, 0:2], scale, None, ALU.mult).then_inc(m_ready, 1)

            row_max(0)
            for u in range(len(units)):
                _, t = units[u]
                ve.wait_ge(e_done, u + 1)
                if u + 1 < len(units):
                    row_max(u + 1)
                c.then(ve.reciprocal(sm[:, u % 2, 2:4], sm[:, u % 2, 0:2]))
                c.then(ve.tensor_scalar(p[:, u % 2, 1, 0:nk(t)], p[:, u % 2, 1, 0:nk(t)], sm[:, u % 2, 3:4], g.lam[:, 1:2],
                                        ALU.mult, ALU.mult))
                ve.scalar_tensor_tensor(p[:, u % 2, 0, 0:nk(t)], p[:, u % 2, 0, 0:nk(t)], sm[:, u % 2, 2:3],
                                        p[:, u % 2, 1, 0:nk(t)], ALU.mult, ALU.add).then_inc(comb, 1)
                if u >= 2:
                    out(u - 2)
            out(len(units) - 2)
            out(len(units) - 1)

        @block.scalar
        def _(act):
            def evac(w):
                _, t = units[w]
                act.wait_ge(t_ready, w + 1)
                if w >= 2:
                    act.wait_ge(o_ready, w - 1)
                nc.scalar.activation(pt[:, w % 2, 0:nk(t)], g.flat[:, 2048:2048 + nk(t)], ACT.Copy).then_inc(pt_ready, 1)

            ones = []
            for u in range(len(units)):
                _, t = units[u]
                act.wait_ge(m_ready, u + 1)
                if u >= 2:
                    act.wait_ge(t_ready, u - 1)
                for c in range(2):
                    e = nc.scalar.activation(p[:, u % 2, c, 0:nk(t)], g.flat[:, 1024 * c:1024 * c + nk(t)], ACT.Exp,
                                             bias=mx[:, u % 2, 2 + c:3 + c], scale=scale, accum_out=sm[:, u % 2, c:c + 1])
                e.then_inc(e_done, 1)
                if u >= 1:
                    evac(u - 1)
            evac(len(units) - 1)


def head_sums(g, pe, src, ready, done, n_chunks=CA, first_bank=0):
    for c in range(n_chunks):
        pe.wait_ge(ready, c + 1)
        for bank, (a, b) in enumerate(((0, NS), (NS, NT))):
            mm = pe.matmul(g.ps[:, first_bank + 2 * c + bank, 0:b - a], g.bones, src(c)[:, a:b], start=True, stop=True)
        mm.then_inc(done, 1)


def subln_stage(g):
    nc = g.nc
    sq, sums, steps, roots = (g.sem(f"subln_{x}") for x in ("squared", "summed", "steps", "roots"))
    with ExitStack() as st, nc.Block() as block:
        s = g.sb(st, "s", [P, CB, NT])

        @block.scalar
        def _(act):
            for c in range(CB):
                nc.scalar.activation(s[:, c, :], g.outT[:, CA + c, :], ACT.Square).then_inc(sq, 1)
            for c in range(CB):
                act.wait_ge(steps, c + 1)
                nc.scalar.activation(s[:, c, :], s[:, c, :], ACT.Sqrt).then_inc(roots, 1)

        @block.tensor
        def _(pe):
            head_sums(g, pe, lambda c: s[:, c, :], sq, sums, n_chunks=CB)

        @block.vector
        def _(ve):
            k = Counter(ve, steps)
            for c in range(CB):
                ve.wait_ge(sums, c + 1)
                k.did(ve.tensor_scalar(s[:, c, :], g.flat[:, 1024 * c:1024 * c + NT], 1.0 / HD, SUB_EPS, ALU.mult, ALU.add))
            for c in range(CB):
                ve.wait_ge(roots, c + 1)
                k.then(ve.reciprocal(s[:, c, :], s[:, c, :]))
                k.did(ve.scalar_tensor_tensor(g.outT[:, CA + c, :], g.outT[:, CA + c, :], g.lam[:, 3:4], s[:, c, :],
                                              ALU.mult, ALU.mult))


def lru_stage(g, l):
    nc, d, v = g.nc, g.dram, g.v
    wl, zero, conv, gate_mm, gate_tk = (g.sem(f"lru_{x}") for x in ("w_loaded", "w_zero", "conv", "gates_summed", "gates_taken"))
    steps, agates, scans, out_st, gel = (g.sem(f"lru_{x}") for x in ("steps", "a_steps", "scans", "stored", "gelu"))
    SEQS = ((0, NS), (NS, NT))
    with ExitStack() as st, nc.Block() as block:
        w = g.sb(st, "lruw", [P, 2, 2, CC, P])
        xp = g.sb(st, "xpad", [P, CC, NT + 6])
        xc = g.sb(st, "xconv", [P, CC, NT])
        ga = g.sb(st, "ga", [P, NT])
        gi = g.sb(st, "gi", [P, NT])
        a = g.sb(st, "a", [P, NT])
        th = g.sb(st, "th", [P, NT])
        bt = g.sb(st, "bt", [P, NT])
        hs = g.sb(st, "hs", [P, CC, 2, NT])
        last = g.sb(st, "last", [P, 2, CC])

        @block.gpsimd
        def _(pool):
            pool.memset(w[:, :, :, :, :], 0.0).then_inc(zero, 1)

        @block.sync
        def _(sync):
            sync.wait_ge(zero, 1)
            for q in range(2):
                for half in range(2):
                    sync.dma_start(w[half * HD:(half + 1) * HD, q, :, :, half * HD:(half + 1) * HD],
                                   d["lru_w"][l, q, half]).then_inc(wl, 16)
            sync.wait_ge(steps, 3 * 2 * CC)
            sync.dma_start(d["new_lru"][l], last[:, :, :]).then_inc(out_st, 16)
            sync.wait_ge(out_st, 16)

        @block.tensor
        def _(pe):
            pe.wait_ge(wl, 64)
            pe.wait_ge(conv, CC)
            n = 0
            for c in range(CC):
                for dr in range(2):
                    for q in range(2):
                        if n >= 4:
                            pe.wait_ge(gate_tk, n - 3)
                        for bank, (x, y) in enumerate(SEQS):
                            mm = pe.matmul(g.ps[:, 2 * (n % 4) + bank, 0:y - x], w[:, q, dr, c, :], xc[:, c, x:y], start=True, stop=True)
                        mm.then_inc(gate_mm, 1)
                        n += 1

        @block.scalar
        def _(act):
            s = Counter(act, agates)
            for c in range(CC):
                nc.scalar.activation(g.outT[:, CA + CB + c, :], g.proj[:, G0 + c, :], ACT.Gelu).then_inc(gel, 1)
            n = 0
            for c in range(CC):
                for dr in range(2):
                    col = 2 * dr + c
                    i = 2 * c + dr
                    if i >= 1:
                        act.wait_ge(steps, 3 * i)
                    for q, dst, bias in ((0, ga, "ba"), (1, gi, "bx")):
                        act.wait_ge(gate_mm, n + 1)
                        nc.scalar.activation(dst[:, :], g.flat[:, 1024 * (n % 4):1024 * (n % 4) + NT], ACT.Sigmoid,
                                             bias=v(bias, col, col + 1)).then_inc(gate_tk, 1)
                        n += 1
                    act.wait_ge(gate_tk, n)
                    s.did(nc.scalar.activation(a[:, :], ga[:, :], ACT.Exp, scale=g.nsp[:, col:col + 1]))
                    s.then(nc.scalar.activation(th[:, :], ga[:, :], ACT.Tanh, scale=g.nsp[:, col:col + 1]))
                    act.wait_ge(steps, 3 * i + 2)
                    s.did(nc.scalar.activation(ga[:, :], ga[:, :], ACT.Sqrt))

        @block.vector
        def _(ve):
            k = Counter(ve, scans)
            s = Counter(ve, steps)
            cv = Counter(ve, g.sem("lru_conv_steps"))
            cv.then(ve.memset(xp[:, :, :], 0.0))
            for c in range(CC):
                cv.did(ve.tensor_copy(xp[:, c, 2:2 + NS], g.proj[:, X0 + c, 0:NS]))
                cv.did(ve.tensor_copy(xp[:, c, NS + 5:NS + 5 + NPR], g.proj[:, X0 + c, NS:NT]))
            cv.wait()
            for c in range(CC):
                for (x, y), at in zip(SEQS, (0, NS + 3)):
                    for j in range(4):
                        src = xp[:, c, at + j:at + j + y - x]
                        if j == 0:
                            i = ve.tensor_scalar(xc[:, c, x:y], src, v("convw", 2 * j + c, 2 * j + c + 1), v("convb", c, c + 1), ALU.mult, ALU.add)
                        else:
                            i = ve.scalar_tensor_tensor(xc[:, c, x:y], src, v("convw", 2 * j + c, 2 * j + c + 1), xc[:, c, x:y], ALU.mult, ALU.add)
                        if j < 3 or y == NS:
                            cv.then(i)
                        else:
                            i.then_inc(conv, 1)
            ve.wait_ge(conv, CC)
            for c in range(CC):
                for dr in range(2):
                    i = 2 * c + dr
                    col = 2 * dr + c
                    ve.wait_ge(agates, 3 * i + 2)
                    s.then(ve.tensor_tensor(bt[:, :], a[:, :], a[:, :], ALU.mult))
                    k.then(ve.scalar_tensor_tensor(bt[:, :], bt[:, :], 1.0, th[:, :], ALU.add, ALU.mult))
                    s.did(ve.tensor_scalar(ga[:, :], bt[:, :], -1.0, None, ALU.mult))
                    k.then(ve.tensor_tensor(gi[:, :], gi[:, :], xc[:, c, :], ALU.mult))
                    ve.wait_ge(agates, 3 * i + 3)
                    k.then(ve.tensor_tensor(bt[:, :], ga[:, :], gi[:, :], ALU.mult))
                    for j, (x, y) in enumerate(SEQS):
                        init = v("h0", col, col + 1) if j == 0 else 0.0
                        o, aa, bb = hs[:, c, dr, x:y], a[:, x:y], bt[:, x:y]
                        if dr:
                            o, aa, bb = o[:, ::-1], aa[:, ::-1], bb[:, ::-1]
                        k.did(ve.tensor_tensor_scan(o, aa, bb, init, ALU.mult, ALU.add))
                    k.wait()
                    e = NT - 1 if dr == 0 else NS
                    s.did(ve.tensor_copy(last[:, dr, c:c + 1], hs[:, c, dr, e:e + 1]))
                    s.wait()
                k.then(ve.tensor_tensor(hs[:, c, 0, :], hs[:, c, 0, :], hs[:, c, 1, :], ALU.add))
                ve.wait_ge(gel, c + 1)
                k.did(ve.tensor_tensor(g.outT[:, CA + CB + c, :], g.outT[:, CA + CB + c, :], hs[:, c, 0, :], ALU.mult))


def rwkv_prepare(g, l, keep):
    nc, d, v = g.nc, g.dram, g.v
    ar, gt, pc = keep
    loaded, first, zs, z_tk = (g.sem(f"rwkv_{x}") for x in ("lora_loaded", "lora_in", "lora_summed", "lora_taken"))
    sq, kks, roots = (g.sem(f"rwkv_{x}") for x in ("key_squared", "prep_steps", "key_roots"))
    logs, exps, kk_tk = (g.sem(f"rwkv_{x}") for x in ("logs_ready", "exps_ready", "key_sums_taken"))
    with ExitStack() as st, nc.Block() as block:
        wb = g.sb(st, "wB", [P, 2, CA * P])
        gb = g.sb(st, "gB", [P, CA * P])
        t1 = g.sb(st, "t1", [P, 2, NT])
        lw = g.sb(st, "lw", [P, 4, NT])
        aa = g.sb(st, "aa", [P, 4, NT])
        kk = g.sb(st, "kk", [P, CA, NT])
        e = g.sb(st, "e", [P, 2, 3, NT])
        sc = g.sb(st, "scan", [P, 2, NT])

        @block.sync
        def _(sync):
            sync.dma_start(wb[:, :, :], d["rwkv_B"][l]).then_inc(loaded, 16)
            sync.dma_start(gb[:, :], d["rwkv_gB"][l]).then_inc(loaded, 16)
            sync.dma_start(sc[:, :, :], d["consts"][:, CI["scanF"][0]:CI["scanF"][0] + 2 * NT]).then_inc(loaded, 16)

        @block.tensor
        def _(pe):
            pe.wait_ge(loaded, 48)
            n = 0

            def sums(lhs, rhs):
                nonlocal n
                if n >= 4:
                    pe.wait_ge(z_tk, n - 3)
                for bank, (x, y) in enumerate(((0, NS), (NS, NT))):
                    mm = pe.matmul(g.ps[:, 2 * (n % 4) + bank, 0:y - x], lhs, rhs[:, x:y], start=True, stop=True)
                mm.then_inc(zs, 1)
                n += 1

            pe.wait_ge(first, 2)
            for q in range(2):
                for dr in range(2):
                    rows = slice(dr * HD, (dr + 1) * HD)
                    for c in range(CA):
                        sums(wb[rows, q, c * P:(c + 1) * P], t1[rows, 0, :] if q == 0 else g.proj[rows, LA, :])
            for c in range(CA):
                sums(gb[:, c * P:(c + 1) * P], t1[:, 1, :])
            for c in range(CA):
                pe.wait_ge(sq, c + 1)
                sums(g.bones, e[:, c, 0, :])

        @block.scalar
        def _(act):
            nc.scalar.activation(t1[:, 0, :], g.proj[:, LW, :], ACT.Tanh).then_inc(first, 1)
            nc.scalar.activation(t1[:, 1, :], g.proj[:, LG, :], ACT.Sigmoid).then_inc(first, 1)
            n = 0
            for q, dst, bias in ((0, lw, "w0"), (1, aa, "a0")):
                for i in range(4):
                    act.wait_ge(zs, n + 1)
                    nc.scalar.activation(dst[:, i, :], g.flat[:, 1024 * (n % 4):1024 * (n % 4) + NT], ACT.Sigmoid,
                                         bias=v(bias, i, i + 1)).then_inc(z_tk, 1)
                    n += 1
            for c in range(CA):
                act.wait_ge(zs, n + 1)
                nc.scalar.activation(gt[:, c, :], g.flat[:, 1024 * (n % 4):1024 * (n % 4) + NT], ACT.Copy).then_inc(z_tk, 1)
                n += 1
            for c in range(CA):
                act.wait_ge(kk_tk, c + 1)
                nc.scalar.activation(e[:, c, 0, :], e[:, c, 1, :], ACT.Sqrt).then_inc(roots, 1)
            for i in range(4):
                act.wait_ge(logs, 2 * i + 2)
                nc.scalar.activation(e[:, i % 2, 2, :], e[:, i % 2, 0, :], ACT.Exp, scale=-1.0).then_inc(exps, 1)
                act.wait_ge(exps, 3 * i + 1)
                nc.scalar.activation(e[:, i % 2, 0, :], e[:, i % 2, 0, :], ACT.Exp).then_inc(exps, 1)
                nc.scalar.activation(e[:, i % 2, 1, :], e[:, i % 2, 1, :], ACT.Exp).then_inc(exps, 1)

        @block.vector
        def _(ve):
            k = Counter(ve, kks)
            ve.wait_ge(loaded, 48)
            for c in range(CA):
                k.then(ve.tensor_scalar(kk[:, c, :], g.proj[:, K0 + c, :], v("kk", c, c + 1), None, ALU.mult))
                ve.tensor_tensor(e[:, c, 0, :], kk[:, c, :], kk[:, c, :], ALU.mult).then_inc(sq, 1)
            for c in range(CA):
                n = 10 + c
                ve.wait_ge(zs, n + 1)
                ve.tensor_scalar(e[:, c, 1, :], g.flat[:, 1024 * (n % 4):1024 * (n % 4) + NT], 1e-12, None, ALU.max).then_inc(kk_tk, 1)
            for c in range(CA):
                ve.wait_ge(roots, c + 1)
                k.then(ve.reciprocal(e[:, c, 1, :], e[:, c, 0, :]))
                k.then(ve.tensor_tensor(kk[:, c, :], kk[:, c, :], e[:, c, 1, :], ALU.mult))
            k.then(ve.tensor_scalar(lw[:, :, :], lw[:, :, :], -DECAY_SCALE, None, ALU.mult))

            def log_sums(i):
                dr = i // 2
                o, m, x = e[:, i % 2, 0, :], sc[:, dr, :], lw[:, i, :]
                if dr:
                    o, m, x = o[:, ::-1], m[:, ::-1], x[:, ::-1]
                if i >= 2:
                    ve.wait_ge(kks, k.n)
                ve.tensor_tensor_scan(o, m, x, 0.0, ALU.mult, ALU.add).then_inc(logs, 1)
                ve.wait_ge(logs, 2 * i + 1)
                ve.tensor_tensor(e[:, i % 2, 1, :], e[:, i % 2, 0, :], lw[:, i, :], ALU.subtract).then_inc(logs, 1)

            def tiled(x):
                return x.rearrange("p (t n) -> p t n", n=P)

            log_sums(0)
            for i in range(4):
                dr, c = divmod(i, 2)
                if i < 3:
                    log_sums(i + 1)
                ve.wait_ge(exps, 3 * i + 3)
                ep, em, en = (e[:, i % 2, j, :] for j in range(3))
                k.did(ve.tensor_tensor(ar[:, dr, c, :, 1, :], tiled(g.proj[:, R0 + c, :]), tiled(ep), ALU.mult))
                k.did(ve.scalar_tensor_tensor(ar[:, dr, c, :, 0, :], tiled(kk[:, c, :]), -1.0, tiled(em), ALU.mult, ALU.mult))
                k.did(ve.tensor_copy(pc[:, dr, c, :], ep.rearrange("p (n t) -> p n t", t=CH)[:, :, 0 if dr else CH - 1]))
                b, kh = g.proj[:, Q0 + i, :], g.proj[:, B0 + i, :]
                k.then(ve.tensor_tensor(b, kk[:, c, :], aa[:, i, :], ALU.mult))
                k.did(ve.tensor_tensor(b, b, en, ALU.mult))
                k.then(ve.tensor_scalar(kh, aa[:, i, :], v("ka", c, c + 1), g.omka[:, c:c + 1], ALU.mult, ALU.add))
                k.then(ve.tensor_tensor(kh, kh, g.proj[:, K0 + c, :], ALU.mult))
                k.then(ve.tensor_tensor(kh, kh, en, ALU.mult))


HOPS = [("pairs", "V"), ("lower", "VA"), ("square1", "VA"), ("square2", "VA"), ("square3", "VA"), ("square4", "VA"),
        ("square5", "V"), ("inverse", "V")] + [(x + str(i), "V") for i in range(2) for x in ("rhs", "sa", "state")]


def rwkv_scan(g, l, keep):
    nc, d = g.nc, g.dram
    ar, gt, pc = keep
    ready = [g.sem(f"products_ready{i}") for i in range(2)]
    byv = [g.sem(f"by_vector{i}") for i in range(2)]
    bya = [g.sem(f"by_scalar{i}") for i in range(2)]
    loaded, zeroed, stored, own, final = (g.sem(f"scan_{x}") for x in ("loaded", "zeroed", "stored", "steps", "final_states"))
    with ExitStack() as st, nc.Block() as block:
        mask = g.sb(st, "mask", [P, 2, 2 * P])
        low = g.sb(st, "low", [P, 2, P])
        mb = g.sb(st, "mb", [P, 2, CA, 2, 2, P])
        mk = g.sb(st, "mk", [P, 2, CA, 2, 2, P])
        pw = g.sb(st, "pw", [P, 2, HA, P])
        pwt = g.sb(st, "pwt", [P, 2, HA, P])
        x = g.sb(st, "x", [P, 2, HA, P])
        bt = g.sb(st, "bt", [P, 2, 2, CA * P])
        sz = g.sb(st, "sz", [P, 2, CA, P])
        szt = g.sb(st, "szt", [P, 2, CA, P])
        rh = g.sb(st, "rh", [P, 2, CA * P])
        sa = g.sb(st, "sa", [P, 2, CA * P])

        def tile(step, dr):
            return TILES - 1 if step == TILES - 1 else (step if dr == 0 else NS // P - 1 - step)

        def half(i, dr):
            return i if dr == 0 else 1 - i

        @block.sync
        def _(sync):
            sync.dma_start(mask[:, :, :], d["consts"][:, CI["maskF"][0]:CI["maskF"][0] + 4 * P]).then_inc(loaded, 16)
            sync.dma_start(low[:, :, :], d["consts"][:, CI["lowF"][0]:CI["lowF"][0] + 2 * P]).then_inc(loaded, 16)
            sync.wait_ge(zeroed, 1)
            for h in range(2):
                rows = slice(h * HD, (h + 1) * HD)
                sync.dma_start(sz[rows, :, :, h * HD:(h + 1) * HD], d["state_rwkv"][l, h]).then_inc(loaded, 16)
            sync.wait_ge(final, 4)
            for h in range(2):
                rows = slice(h * HD, (h + 1) * HD)
                sync.dma_start(d["new_rwkv"][l, h], sz[rows, :, :, h * HD:(h + 1) * HD]).then_inc(stored, 16)
            sync.wait_ge(stored, 32)

        @block.tensor
        def _(pe):
            pe.wait_ge(loaded, 64)
            nv, na = [0, 0], [0, 0]

            def hop(name, dr, t):
                bh = lambda c: g.proj[:, Q0 + 2 * dr + c, t * P:(t + 1) * P]
                kh = lambda c: g.proj[:, B0 + 2 * dr + c, t * P:(t + 1) * P]
                A, B, C, O = 3 * dr, 3 * dr + 1, 3 * dr + 2, 6 + dr
                heads = [(c, h, slice(h * HD, (h + 1) * HD)) for c in range(CA) for h in range(2)]
                if name == "pairs":
                    for src, banks in ((bh, (A, B)), (kh, (C, O))):
                        for c, h, rows in heads:
                            mm = pe.matmul(g.ps[:, banks[h], c * 2 * P:(c + 1) * 2 * P], src(c)[rows, :],
                                           ar[rows, dr, c, t, :, :], start=True, stop=True)
                elif name == "lower":
                    for c, h, rows in heads:
                        pe.matmul(g.ps[:, (A, B)[h], c * P:(c + 1) * P], ar[rows, dr, c, t, 0, :], bh(c)[rows, :],
                                  start=True, stop=True)
                    for i, src in enumerate((bh, kh)):
                        for c in range(CA):
                            mm = pe.transpose(g.ps[:, C, (2 * i + c) * P:(2 * i + c + 1) * P], src(c), g.ident)
                elif name.startswith("square") or name == "inverse":
                    n = 6 if name == "inverse" else int(name[6:])
                    for h in range(HA):
                        cols = slice(h * P, (h + 1) * P)
                        p0 = mb[:, dr, h // 2, h % 2, 0, :] if n == 1 else pw[:, dr, h, :]
                        pt = pwt[:, dr, h, :]
                        if n >= 2:
                            mm = pe.matmul(g.ps[:, C, cols], pt, x[:, dr, h, :], start=True, stop=True)
                        if n <= 4:
                            mm = pe.matmul(g.ps[:, A, cols], pt, p0, start=True, stop=True)
                        if n <= 5:
                            mm = pe.matmul(g.ps[:, B, cols], p0, pt, start=True, stop=True)
                else:
                    i = int(name[-1])
                    hf = half(i, dr)
                    hs = slice(hf * HD, (hf + 1) * HD)
                    if name.startswith("rhs"):
                        for c in range(CA):
                            pe.matmul(g.ps[hs, A, c * P:(c + 1) * P], ar[:, dr, c, t, 0, hs], sz[:, dr, c, :],
                                      start=(c == 0), stop=False, skip_group_check=True)
                        for c, h, rows in heads:
                            at = c * P + h * HD
                            mm = pe.matmul(g.ps[hs, A, at:at + HD], mk[:, dr, c, h, 0, hs], g.vtok[:, t, at:at + HD],
                                           start=False, stop=(c == CA - 1 and h == 1), skip_group_check=True)
                    elif name.startswith("sa"):
                        for c, h, rows in heads:
                            at = c * P + h * HD
                            mm = pe.matmul(g.ps[hs, B, at:at + HD], x[:, dr, 2 * c + h, hs], rh[:, dr, at:at + HD],
                                           start=(at == 0), stop=(c == CA - 1 and h == 1), skip_group_check=True)
                    else:
                        for c in range(CA):
                            cols = slice(c * P, (c + 1) * P)
                            pe.matmul(g.ps[:, C, cols], bt[hs, dr, 0, cols], sa[hs, dr, cols],
                                      start=(c == 0), stop=False, skip_group_check=True)
                            pe.matmul(g.ps[:, C, cols], bt[hs, dr, 1, cols], g.vtok[hs, t, cols],
                                      start=False, stop=(c == CA - 1), skip_group_check=True)
                        for c in range(CA):
                            at = c * P + hf * HD
                            mm = pe.matmul(g.ps[:, O, at:at + HD], sz[:, dr, c, :], ar[:, dr, c, t, 1, hs],
                                           start=(i == 0 and c == 0), stop=False, skip_group_check=True)
                        if i == 1:
                            for c, h, rows in heads:
                                at = c * P + h * HD
                                for j, (lhs, m) in enumerate(((sa[:, dr, at:at + HD], mb), (g.vtok[:, t, at:at + HD], mk))):
                                    mm = pe.matmul(g.ps[rows, O, c * P:(c + 1) * P], lhs, m[:, dr, c, h, 1, :],
                                                   start=False, stop=(c == CA - 1 and j == 1), skip_group_check=True)
                mm.then_inc(ready[dr], 1)

            for step in range(TILES):
                for name, by in HOPS:
                    for dr in range(2):
                        if nv[dr]:
                            pe.wait_ge(byv[dr], nv[dr])
                        if na[dr]:
                            pe.wait_ge(bya[dr], na[dr])
                        hop(name, dr, tile(step, dr))
                        nv[dr] += "V" in by
                        na[dr] += "A" in by

        @block.scalar
        def _(act):
            k = 0
            for step in range(TILES):
                for name, by in HOPS:
                    k += 1
                    if "A" not in by:
                        continue
                    for dr in range(2):
                        act.wait_ge(ready[dr], k)
                        if name == "lower":
                            dst, src = bt[:, dr, :, :], g.ps[:, 3 * dr + 2, :]
                        else:
                            dst, src = pw[:, dr, :, :], g.ps[:, 3 * dr, :]
                        nc.scalar.activation(dst, src, ACT.Copy).then_inc(bya[dr], 1)

        @block.vector
        def _(ve):
            o = Counter(ve, own)
            ve.memset(sz[:, :, :, :], 0.0).then_inc(zeroed, 1)
            o.did(ve.memset(rh[:, :, :], 0.0))
            o.did(ve.memset(sa[:, :, :], 0.0))
            o.then(ve.memset(g.outT[:, 0:CA, :], 0.0))
            ve.wait_ge(loaded, 64)
            k = 0
            for step in range(TILES):
                for name, by in HOPS:
                    k += 1
                    for dr in range(2):
                        t = tile(step, dr)
                        A, B, C, O = 3 * dr, 3 * dr + 1, 3 * dr + 2, 6 + dr
                        ve.wait_ge(ready[dr], k)
                        if name == "pairs":
                            for dst, banks in ((mb, (A, B)), (mk, (C, O))):
                                for h in range(2):
                                    last = ve.tensor_tensor(dst[:, dr, :, h, :, :].rearrange("p c a t -> p c (a t)"),
                                                            g.ps[:, banks[h], :].rearrange("p (c n) -> p c n", c=CA),
                                                            mask[:, dr, :].unsqueeze(1).broadcast_to([P, CA, 2 * P]), ALU.mult)
                            if step == TILES - 1:
                                last = ve.memset(sz[:, dr, :, :], 0.0)
                        elif name == "lower":
                            for h in range(2):
                                ve.tensor_tensor(pwt[:, dr, h::2, :], g.ps[:, (A, B)[h], 0:2 * P].rearrange("p (c n) -> p c n", c=CA),
                                                 low[:, dr, :].unsqueeze(1).broadcast_to([P, CA, P]), ALU.mult)
                            last = ve.tensor_tensor(x[:, dr, :, :], mb[:, dr, :, :, 0, :].rearrange("p c h t -> p (c h) t"),
                                                    g.ident.unsqueeze(1).broadcast_to([P, HA, P]), ALU.add)
                        elif name.startswith("square") or name == "inverse":
                            if name != "square1":
                                last = ve.tensor_tensor(x[:, dr, :, :], x[:, dr, :, :],
                                                        g.ps[:, C, :].rearrange("p (h n) -> p h n", h=HA), ALU.add)
                            if name != "inverse":
                                last = ve.tensor_copy(pwt[:, dr, :, :], g.ps[:, B, :])
                        else:
                            i = int(name[-1])
                            hf = half(i, dr)
                            hs = slice(hf * HD, (hf + 1) * HD)
                            if name.startswith("rhs"):
                                last = ve.tensor_copy(rh[hs, dr, :], g.ps[hs, A, 0:CA * P])
                            elif name.startswith("sa"):
                                last = ve.tensor_copy(sa[hs, dr, :], g.ps[hs, B, 0:CA * P])
                            else:
                                o.then(ve.tensor_tensor(szt[:, dr, :, :], sz[:, dr, :, :],
                                                        g.ps[:, C, 0:CA * P].rearrange("p (c n) -> p c n", c=CA), ALU.add))
                                if i == 1:
                                    out = g.outT[:, 0:CA, t * P:(t + 1) * P]
                                    o.did(ve.tensor_tensor(out, out, g.ps[:, O, 0:CA * P].rearrange("p (c n) -> p c n", c=CA), ALU.add))
                                ch = 2 * t + hf
                                for c in range(CA):
                                    last = ve.scalar_tensor_tensor(sz[:, dr, c, :], szt[:, dr, c, :], pc[:, dr, c, ch:ch + 1],
                                                                   g.bones, ALU.mult, ALU.mult)
                                    if step == TILES - 1 and i == 1:
                                        last.then_inc(final, 1)
                                        last = None
                        if last is not None:
                            last.then_inc(byv[dr], 1)


def rwkv_finish(g, keep):
    nc, v = g.nc, g.v
    ar, gt, pc = keep
    sb_, ss, steps, sq, roots = (g.sem(f"rwkv_out_{x}") for x in ("bonus_in", "summed", "steps", "squared", "roots"))
    taken = g.sem("rwkv_out_taken")
    with ExitStack() as st, nc.Block() as block:
        bo = g.sb(st, "bo", [P, CA, NT])
        s2 = g.sb(st, "s2", [P, CA, NT])

        @block.tensor
        def _(pe):
            n = 0
            for src, sem in ((lambda c: bo[:, c, :], sb_), (lambda c: g.outT[:, c, :], None), (lambda c: s2[:, c, :], sq)):
                for c in range(CA):
                    if sem is not None:
                        pe.wait_ge(sem, c + 1)
                    if n >= 4:
                        pe.wait_ge(taken, n - 3)
                    for bank, (a, b) in enumerate(((0, NS), (NS, NT))):
                        mm = pe.matmul(g.ps[:, 2 * (n % 4) + bank, 0:b - a], g.bones, src(c)[:, a:b], start=True, stop=True)
                    mm.then_inc(ss, 1)
                    n += 1

        @block.scalar
        def _(act):
            for c in range(CA):
                act.wait_ge(taken, 3 + c)
                nc.scalar.activation(s2[:, c, :], g.outT[:, c, :], ACT.Square).then_inc(sq, 1)
            for c in range(CA):
                act.wait_ge(taken, 5 + c)
                nc.scalar.activation(s2[:, c, :], s2[:, c, :], ACT.Sqrt).then_inc(roots, 1)

        @block.vector
        def _(ve):
            k = Counter(ve, steps)
            flat = lambda n: g.flat[:, 1024 * (n % 4):1024 * (n % 4) + NT]
            for c in range(CA):
                ve.scalar_tensor_tensor(bo[:, c, :], g.proj[:, R0 + c, :], v("rk", c, c + 1), g.proj[:, K0 + c, :],
                                        ALU.mult, ALU.mult).then_inc(sb_, 1)
            for c in range(CA):
                ve.wait_ge(ss, c + 1)
                ve.tensor_tensor(bo[:, c, :], flat(c), g.proj[:, V0 + c, :], ALU.mult).then_inc(taken, 1)
            for c in range(CA):
                ve.wait_ge(ss, 3 + c)
                ve.scalar_tensor_tensor(g.outT[:, c, :], flat(2 + c), -1.0 / HD, g.outT[:, c, :], ALU.mult, ALU.add).then_inc(taken, 1)
            for c in range(CA):
                ve.wait_ge(ss, 5 + c)
                ve.tensor_scalar(s2[:, c, :], flat(4 + c), 1.0 / HD, GN_EPS, ALU.mult, ALU.add).then_inc(taken, 1)
            for c in range(CA):
                ve.wait_ge(roots, c + 1)
                k.then(ve.reciprocal(s2[:, c, :], s2[:, c, :]))
                k.then(ve.scalar_tensor_tensor(g.outT[:, c, :], g.outT[:, c, :], v("lng", c, c + 1), s2[:, c, :], ALU.mult, ALU.mult))
                k.then(ve.tensor_tensor(g.outT[:, c, :], g.outT[:, c, :], bo[:, c, :], ALU.add))
                k.did(ve.tensor_tensor(g.outT[:, c, :], g.outT[:, c, :], gt[:, c, :], ALU.mult))


def residual_take(g, part):
    def take(ve, oc, sums):
        for a, b in ((0, H2), (H2, NS), (NS, NT)):
            c, h = int(a >= NS), a // H2
            x = g.xT[:, bass.ds(oc, 1), a:b]
            i = ve.scalar_tensor_tensor(x, sums[:, h:h + 1, a - h * H2:b - h * H2], g.modT[:, bass.ds(part * KC + oc, 1), c], x,
                                        ALU.mult, ALU.add)
        return i
    return take


def select_stage(g, l, qT, sel):
    nc, d = g.nc, g.dram
    loaded, sc_ready, sc_taken, steps = (g.sem(f"sel_{x}") for x in ("keys_loaded", "scores_ready", "scores_taken", "steps"))
    dif, ex, out_ready, tr, tr_tk = (g.sem(f"sel_{x}") for x in ("differences", "exps", "selected", "transposed", "transposes_taken"))
    NC = 2 * PH
    with ExitStack() as st, nc.Block() as block:
        kt = g.sb(st, "kt", [P, NC, P])
        s = g.sb(st, "s", [P, NC, NKEY])
        s2 = g.sb(st, "s2", [P, NKEY])
        v16 = g.sb(st, "v16", [P, NC, TOPK])
        i16 = g.sb(st, "i16", [P, NC, TOPK], U32)
        if16 = g.sb(st, "if16", [P, NC, TOPK])
        cand = g.sb(st, "cand", [P, PH, TOPK * TOPK])
        c2 = g.sb(st, "c2", [P, TOPK * TOPK])
        top = g.sb(st, "top", [P, PH, TOPK])
        pos = g.sb(st, "pos", [P, PH, TOPK], U32)
        hi = g.sb(st, "hi", [P, 2, PH, TOPK], U32)
        hif = g.sb(st, "hif", [P, 2, PH, TOPK])
        oh = g.sb(st, "oh", [P, PH, TOPK, TOPK])
        res = g.sb(st, "res", [P, 3, PH, TOPK])
        sm = g.sb(st, "sm", [P, 2, PH])

        @block.sync
        def _(sync):
            sync.dma_start(kt[:, :, :], d["peer_keys"][l]).then_inc(loaded, 16)

        @block.tensor
        def _(pe):
            pe.wait_ge(loaded, 16)
            for t in range(TILES + 1):
                if t < TILES:
                    if t >= 1:
                        pe.wait_ge(sc_taken, t)
                    for i in range(NC):
                        mm = pe.matmul(g.flat[:, i * P:(i + 1) * P], qT[:, i, t * P:(t + 1) * P], kt[:, i, :], start=True, stop=True)
                    mm.then_inc(sc_ready, 1)
                if t >= 1:
                    pe.wait_ge(out_ready, t)
                    if t >= 2:
                        pe.wait_ge(tr_tk, t - 1)
                    for j in range(3):
                        mm = pe.transpose(g.ps[:, 4, j * P:(j + 1) * P], res[:, j, :, :].rearrange("p h k -> p (h k)"), g.ident)
                    mm.then_inc(tr, 1)

        @block.scalar
        def _(act):
            for t in range(TILES):
                act.wait_ge(sc_ready, t + 1)
                if t >= 1:
                    act.wait_ge(dif, t)
                nc.scalar.activation(s[:, :, :], g.flat[:, 0:NC * P], ACT.Copy).then_inc(sc_taken, 1)
                act.wait_ge(dif, t + 1)
                nc.scalar.activation(res[:, 2, :, :], res[:, 2, :, :], ACT.Exp).then_inc(ex, 1)
                act.wait_ge(tr, t + 1)
                nc.scalar.activation(sel[:, :, t * P:(t + 1) * P], g.ps[:, 4, 0:3 * P], ACT.Copy).then_inc(tr_tk, 1)

        @block.vector
        def _(ve):
            k = Counter(ve, steps)

            def top16(values, scratch, best, index):
                k.then(ve.max(best[:, 0:8], values))
                k.did(ve.max_index(index[:, 0:8], best[:, 0:8], values))
                k.then(ve.match_replace(scratch, best[:, 0:8], values, NEG))
                k.then(ve.max(best[:, 8:16], scratch))
                k.then(ve.max_index(index[:, 8:16], best[:, 8:16], scratch))

            iota16 = g.iota[:, 0:TOPK].unsqueeze(1).broadcast_to([P, PH * TOPK, TOPK])
            for t in range(TILES):
                ve.wait_ge(sc_taken, t + 1)
                for i in range(NC):
                    top16(s[:, i, :], s2[:, :], v16[:, i, :], i16[:, i, :])
                k.then(ve.tensor_copy(if16[:, :, :], i16[:, :, :]))
                both = v16[:, :, :].rearrange("p (h c) k -> p h c k", c=2)
                for h in range(PH):
                    k.did(ve.tensor_tensor(cand[:, h, :].rearrange("p (a b) -> p a b", b=TOPK),
                                           both[:, h, 0, :].unsqueeze(2).broadcast_to([P, TOPK, TOPK]),
                                           both[:, h, 1, :].unsqueeze(1).broadcast_to([P, TOPK, TOPK]), ALU.add))
                k.wait()
                for h in range(PH):
                    top16(cand[:, h, :], c2[:, :], top[:, h, :], pos[:, h, :])
                k.did(ve.tensor_scalar(hi[:, 0, :, :], pos[:, :, :], 4, None, ALU.logical_shift_right))
                k.then(ve.tensor_scalar(hi[:, 1, :, :], pos[:, :, :], TOPK - 1, None, ALU.bitwise_and))
                k.then(ve.tensor_copy(hif[:, :, :, :], hi[:, :, :, :]))
                if t >= 1:
                    ve.wait_ge(tr, t)
                ids = if16[:, :, :].rearrange("p (h c) k -> p h c k", c=2)
                for c in range(2):
                    rank = hif[:, c, :, :].rearrange("p h k -> p (h k)").unsqueeze(2).broadcast_to([P, PH * TOPK, TOPK])
                    flat = oh[:, :, :, :].rearrange("p h k m -> p (h k) m")
                    k.then(ve.tensor_tensor(flat, rank, iota16, ALU.is_equal))
                    k.then(ve.tensor_tensor(oh[:, :, :, :], oh[:, :, :, :],
                                            ids[:, :, c, :].unsqueeze(2).broadcast_to([P, PH, TOPK, TOPK]), ALU.mult))
                    k.then(ve.tensor_reduce(res[:, c, :, :], oh[:, :, :, :], AX.X, ALU.add))
                ve.tensor_tensor(res[:, 2, :, :], top[:, :, :], top[:, :, 0:1].broadcast_to([P, PH, TOPK]), ALU.subtract).then_inc(dif, 1)
                ve.wait_ge(ex, t + 1)
                k.then(ve.tensor_reduce(sm[:, 0, :], res[:, 2, :, :], AX.X, ALU.add))
                k.then(ve.reciprocal(sm[:, 1, :], sm[:, 0, :]))
                ve.tensor_tensor(res[:, 2, :, :], res[:, 2, :, :], sm[:, 1, :].unsqueeze(2).broadcast_to([P, PH, TOPK]),
                                 ALU.mult).then_inc(out_ready, 1)


GT_N = P
GB = 2
NG = NKEY // GB
H2 = NT // 2
OP = 8
OCT = 4


def gates_stage(g, l, sel):
    nc, d = g.nc, g.dram
    b_ready, a_ready, mm_ready, taken = (g.sem(f"gate_{x}") for x in ("b_onehots", "a_onehots", "products", "taken"))
    a_eq = g.sem("gate_a_equal")
    store = [g.sem(f"gate_stored{i}") for i in range(2)]
    with ExitStack() as st, nc.Block() as block:
        oa = g.sb(st, "oa", [P, 2, OCT, P])
        ob = g.sb(st, "ob", [P, 2, OCT, P])
        stage = g.sb(st, "stage", [P, 2, NKEY, GT_N])
        NO = GT_N // OCT
        iota = g.iota.unsqueeze(1).broadcast_to([P, OCT, P])

        def turns(eng, body):
            with eng.Fori(0, TILES // 2) as i:
                for q in range(2):
                    body(i * 2 + q, q, i)
            body(TILES - 1, 0, TILES // 2)

        @block.vector
        def _(ve):
            ve.sem_inc(mm_ready, 2)

            def tile(t, q, i):
                def col(j, o):
                    return sel[:, j, bass.ds(t * P + o * OCT, OCT)].unsqueeze(2).broadcast_to([P, OCT, P])

                for o in range(NO):
                    ve.wait_ge(mm_ready, t * NO + (o + 1))
                    ve.tensor_tensor(ob[:, o % 2, :, :], iota, col(1, o), ALU.is_equal).then_inc(b_ready, 1)
                    ve.tensor_tensor(oa[:, o % 2, :, :], iota, col(0, o), ALU.is_equal).then_inc(a_eq, 1)
                    ve.wait_ge(a_eq, t * NO + (o + 1))
                    ve.tensor_tensor(oa[:, o % 2, :, :], oa[:, o % 2, :, :], col(2, o), ALU.mult).then_inc(a_ready, 1)

            turns(ve, tile)

        @block.tensor
        def _(pe):
            def tile(t, q, i):
                for o in range(NO):
                    pe.wait_ge(a_ready, t * NO + (o + 1))
                    pe.wait_ge(b_ready, t * NO + (o + 1))
                    pe.wait_ge(taken, t * NO + (o + 1))
                    for n in range(OCT):
                        at = OCT * P * (o % OP) + n * P
                        mm = pe.matmul(g.flat[:, at:at + P], oa[:, o % 2, n, :], ob[:, o % 2, n, :], start=True, stop=True)
                    mm.then_inc(mm_ready, 1)

            turns(pe, tile)

        @block.scalar
        def _(act):
            act.sem_inc(taken, OP)
            act.sem_inc(store[0], 16)
            act.sem_inc(store[1], 16)

            def tile(t, q, i):
                act.wait_ge(store[q], i * 16 + 16)
                for o in range(NO):
                    act.wait_ge(mm_ready, t * NO + (o + 3))
                    at = OCT * P * (o % OP)
                    dst = stage[:, q, :, o * OCT:(o + 1) * OCT].rearrange("p b n -> p n b")
                    nc.scalar.activation(dst, g.flat[:, at:at + OCT * P].rearrange("p (n b) -> p n b", n=OCT), ACT.Copy).then_inc(taken, 1)

            turns(act, tile)

        @block.sync
        def _(sync):
            def tile(t, q, i):
                sync.wait_ge(taken, t * NO + (NO + OP))
                sync.dma_start(d["gates"][:, :, bass.ds(t, 1), :],
                               stage[:, q, :, :].rearrange("p (g b) n -> p g (b n)", b=GB).unsqueeze(2)).then_inc(store[q], 16)

            turns(sync, tile)
            sync.wait_ge(store[0], 16 * (TILES // 2 + 2))
            sync.wait_ge(store[1], 16 * (TILES // 2 + 1))


def experts_stage(g, l, acc):
    nc, d = g.nc, g.dram
    T = 2
    B = T * GB
    YN = 2 * TILES
    u_in = [g.sem(f"u_loaded{i}") for i in range(B)]
    v_in = [g.sem(f"v_loaded{i}") for i in range(B)]
    g_in = [g.sem(f"g_loaded{i}") for i in range(T)]
    u_hi, u_lo, v_hi, v_lo = (g.sem(f"exp_{x}") for x in ("u_high", "u_low", "v_high", "v_low"))
    h_ready, h_taken, weighed, w_hi, w_lo, y_ready, y_taken = (
        g.sem(f"exp_{x}") for x in ("h_ready", "h_taken", "weighed", "w_high", "w_low", "y_ready", "y_taken"))
    with ExitStack() as st, nc.Block() as block:
        u = g.sb(st, "u", [P, B, KC, P])
        v = g.sb(st, "v", [P, B, D])
        gw = g.sb(st, "gw", [P, T, TILES, GB, GT_N])
        hh = g.sb(st, "hh", [P, 2, NT])
        u2 = [g.sb(st, f"u{x}", [P, 2, KC, P], F32R) for x in ("hi", "lo")]
        v2 = [g.sb(st, f"v{x}", [P, B, D], F32R) for x in ("hi", "lo")]
        w2 = [g.sb(st, f"w{x}", [P, B, NT], F32R) for x in ("hi", "lo")]
        LAST = NG // T - 1

        def turns(eng, turn):
            with eng.Fori(0, LAST) as i:
                turn(i, False)
            turn(LAST, True)

        @block.sync
        def _(sync):
            sync.sem_inc(u_lo, B)
            sync.sem_inc(v_lo, B)
            sync.sem_inc(weighed, B)
            with sync.Fori(0, NG // T) as i:
                for j in range(B):
                    if j % GB == 0:
                        q = j // GB
                        sync.wait_ge(weighed, i * B + (q + 1) * GB)
                        sync.dma_start(gw[:, q, :, :, :].rearrange("p t b n -> p (t b n)"),
                                       d["gates"][:, bass.ds(i * T + q, 1), :, :].rearrange("p g t m -> p (g t m)")).then_inc(g_in[q], 16)
                    sync.wait_ge(u_lo, i * B + (j + 1))
                    sync.dma_start(u[:, j, :, :], d["peer_u"][l, i * B + j]).then_inc(u_in[j], 16)
                    sync.wait_ge(v_lo, i * B + (j + 1))
                    sync.dma_start(v[:, j, :], d["peer_v"][l, :, bass.ds((i * B + j) * D, D)]).then_inc(v_in[j], 16)

        @block.tensor
        def _(pe):
            def hidden(i, q):
                for j in range(q * GB, (q + 1) * GB):
                    pe.wait_ge(u_lo, i * B + (j + 1 + B))
                    pe.wait_ge(h_taken, i * B + (j + 1))
                    for h in range(2):
                        for kc in range(KC):
                            mm = split3(pe, g.ps[:, 2 * (j % 2) + h, 0:H2], [x[:, j % 2, kc, :] for x in u2],
                                        [x[:, kc, h * H2:(h + 1) * H2] for x in g.h2], start=(kc == 0), stop=(kc == KC - 1))
                    mm.then_inc(h_ready, 1)

            def output(i, q):
                pe.wait_ge(v_lo, i * B + ((q + 1) * GB + B))
                pe.wait_ge(w_lo, i * B + ((q + 1) * GB + 2))
                for n in range(YN):
                    t, half = divmod(n, 2)
                    m = q * YN + n
                    pe.wait_ge(y_taken, i * (T * YN) + (m + 1))
                    for b in range(GB):
                        j = q * GB + b
                        mm = split3(pe, g.ps[:, 4 + m % 4, :], [x[:, j, t * P:(t + 1) * P] for x in w2],
                                    [x[:, j, half * 512:(half + 1) * 512] for x in v2], start=(b == 0), stop=(b == GB - 1))
                    mm.then_inc(y_ready, 1)

            def turn(i, last):
                hidden(i, 1)
                output(i, 0)
                if not last:
                    hidden(i + 1, 0)
                output(i, 1)

            hidden(0, 0)
            turns(pe, turn)

        @block.scalar
        def _(act):
            act.sem_inc(h_taken, 2)
            act.sem_inc(h_ready, 2)
            act.sem_inc(y_ready, T * YN)

            def u_high(i, j):
                i, j = i + j // B, j % B
                act.wait_ge(u_in[j], i * 16 + 16)
                act.wait_ge(h_ready, i * B + (j + 1))
                nc.scalar.activation(u2[0][:, j % 2, :, :], u[:, j, :, :], ACT.Copy).then_inc(u_hi, 1)

            def v_high(i, q):
                i, q = i + q // T, q % T
                act.wait_ge(y_ready, i * (T * YN) + (q + 1) * YN)
                for j in range(q * GB, (q + 1) * GB):
                    act.wait_ge(v_in[j], i * 16 + 16)
                    nc.scalar.activation(v2[0][:, j, :], v[:, j, :], ACT.Copy).then_inc(v_hi, 1)

            def group(i, q, last, u_ahead=True):
                for b in range(GB):
                    j = q * GB + b
                    act.wait_ge(h_ready, i * B + (j + 1 + 2))
                    act.wait_ge(w_lo, i * B + (j + 1))
                    nc.scalar.activation(halves(hh[:, j % 2, :]), g.ps[:, 2 * (j % 2):2 * (j % 2) + 2, 0:H2], ACT.Gelu).then_inc(h_taken, 1)
                    if not (last and j + 2 >= B):
                        u_high(i, j + 2)
                    act.wait_ge(weighed, i * B + (j + 1 + B))
                    act.wait_ge(y_ready, i * (T * YN) + (q + 1) * YN)
                    nc.scalar.activation(w2[0][:, j, :], hh[:, j % 2, :], ACT.Copy).then_inc(w_hi, 1)

            def turn(i, last):
                group(i, 1, last)
                if not last:
                    v_high(i, 2)
                    group(i + 1, 0, False)
                    v_high(i, 3)

            u_high(0, 0)
            u_high(0, 1)
            v_high(0, 0)
            group(0, 0, False)
            v_high(0, 1)
            turns(act, turn)

        @block.vector
        def _(ve):
            ve.memset(acc[:, :, :], 0.0).then_inc(y_taken, 4)
            ve.wait_ge(y_taken, 4)
            ve.sem_inc(w_lo, 2)

            def u_low(i, j):
                i, j = i + j // B, j % B
                ve.wait_ge(u_hi, i * B + (j + 1))
                ve.tensor_tensor(u2[1][:, j % 2, :, :], u[:, j, :, :], u2[0][:, j % 2, :, :].bitcast(F32), ALU.subtract).then_inc(u_lo, 1)

            def v_low(i, q):
                i, q = i + q // T, q % T
                for j in range(q * GB, (q + 1) * GB):
                    ve.wait_ge(v_hi, i * B + (j + 1))
                    ve.tensor_tensor(v2[1][:, j, :], v[:, j, :], v2[0][:, j, :].bitcast(F32), ALU.subtract).then_inc(v_lo, 1)

            def group(i, q, last):
                ve.wait_ge(g_in[q], i * 16 + 16)
                for b in range(GB):
                    j = q * GB + b
                    ve.wait_ge(h_taken, i * B + (j + 1 + 2))
                    h = hh[:, j % 2, :].rearrange("p (t n) -> p t n", n=GT_N)
                    ve.tensor_tensor(h, gw[:, q, :, b, :], h, ALU.mult).then_inc(weighed, 1)
                    if not (last and j + 2 >= B):
                        u_low(i, j + 2)
                    ve.wait_ge(w_hi, i * B + (j + 1))
                    ve.tensor_tensor(w2[1][:, j, :], hh[:, j % 2, :], w2[0][:, j, :].bitcast(F32), ALU.subtract).then_inc(w_lo, 1)

            def take(i, q):
                for n in range(YN):
                    t, half = divmod(n, 2)
                    m = q * YN + n
                    ve.wait_ge(y_ready, i * (T * YN) + (m + 1 + T * YN))
                    a = acc[:, t, half * 512:(half + 1) * 512]
                    ve.tensor_tensor(a, a, g.ps[:, 4 + m % 4, :], ALU.add).then_inc(y_taken, 1)

            def turn(i, last):
                group(i, 1, last)
                take(i, 0)
                if not last:
                    v_low(i, 2)
                    group(i + 1, 0, False)
                take(i, 1)
                if not last:
                    v_low(i, 3)

            u_low(0, 0)
            u_low(0, 1)
            v_low(0, 0)
            group(0, 0, False)
            v_low(0, 1)
            turns(ve, turn)


def fold_stage(g, acc):
    nc = g.nc
    tr, tk = g.sem("fold_transposed"), g.sem("fold_taken")
    with nc.Block() as block:
        @block.tensor
        def _(pe):
            for t in range(TILES):
                if t >= 4:
                    pe.wait_ge(tk, t - 3)
                for kc in range(KC):
                    at = 1024 * (t % 4) + kc * P
                    mm = pe.transpose(g.flat[:, at:at + P], acc[:, t, kc * P:(kc + 1) * P], g.ident)
                mm.then_inc(tr, 1)

        @block.vector
        def _(ve):
            for t in range(TILES):
                ve.wait_ge(tr, t + 1)
                c = int(t == TILES - 1)
                for kc in range(KC):
                    at = 1024 * (t % 4) + kc * P
                    x = g.xT[:, kc, t * P:(t + 1) * P]
                    i = ve.scalar_tensor_tensor(x, g.flat[:, at:at + P], g.modT[:, 5 * KC + kc, c:c + 1], x, ALU.mult, ALU.add)
                i.then_inc(tk, 1)


def build(nc, dram, upto=99):
    ctx = ExitStack()
    with ctx:
        g = Program(nc, ctx, dram)
        g.ps = ctx.enter_context(nc.psum_tensor("ps", [P, 8, 512], F32))
        g.flat = g.ps[:, :, :].rearrange("p b n -> p (b n)")
        g.xT = g.sb(ctx, "xT", [P, KC, NT])
        g.keep = g.sb(ctx, "keep", [P, NKEEP])
        g.ident, g.ones, g.bones, g.iota = (g.keep[:, i * P:(i + 1) * P] for i in range(4))
        g.vec = g.sb(ctx, "vec", [P, NVEC])
        g.cond = g.sb(ctx, "cond", [P, KC, 2])
        g.scond = g.sb(ctx, "scond", [P, KC, 2])
        g.tiny = g.sb(ctx, "tiny", [P, 8 + DK])
        g.lam = g.sb(ctx, "lam", [P, 4])
        g.omka = g.sb(ctx, "omka", [P, 2])
        g.nsp = g.sb(ctx, "nsp", [P, 4])
        g.nsp2 = g.sb(ctx, "nsp2", [P, 4])
        g.modT = g.sb(ctx, "modT", [P, 6 * KC, 2])
        g.gain = g.sb(ctx, "gain", [P, 2, KC, 2])
        x_in = ctx.enter_context(nc.semaphore("x_loaded"))
        y_out = ctx.enter_context(nc.semaphore("y_stored"))

        with nc.Block() as block:
            @block.sync
            def _(sync):
                sync.dma_start(g.xT[:, :, :], dram["x"]).then_inc(x_in, 16)
                sync.wait_ge(x_in, 16)

        with nc.Fori(0, DEPTH) as l:
            g.begin()
            load_stage(g, l)
            mod_stage(g, l)
            with ExitStack() as s1:
                g.proj = g.sb(s1, "proj", [P, NPROJ, NT])
                g.vtok = g.sb(s1, "vtok", [P, TILES, VTOK])
                with ExitStack() as s2:
                    g.h2 = [g.sb(s2, f"h{x}", [P, KC, NT], F32R) for x in ("hi", "lo")]
                    norm_stage(g, "norm1", g.h2[0], lambda kc, c: g.gain[:, 0, kc, c:c + 1], lambda kc, c: g.modT[:, kc, c:c + 1],
                               low=g.h2[1])
                    proj_stage(g, l)
                g.outT = g.sb(s1, "outT", [P, KC, NT])
                with ExitStack() as s2:
                    g.kctx = g.sb(s2, "kctx", [P, CB, PAST])
                    g.vctx = g.sb(s2, "vctx", [P, PAST // P, 512])
                    rope_stage(g, l)
                    attention_stage(g, l)
                subln_stage(g)
                lru_stage(g, l)
                with ExitStack() as s2:
                    keep = (g.sb(s2, "ar", [P, 2, CA, TILES, 2, P]), g.sb(s2, "gt", [P, CA, NT]), g.sb(s2, "pc", [P, 2, CA, NT // CH]))
                    rwkv_prepare(g, l, keep)
                    rwkv_scan(g, l, keep)
                    rwkv_finish(g, keep)
                with ExitStack() as s2:
                    out2 = [g.sb(s2, f"out{x}", [P, KC, NT], F32R) for x in ("hi", "lo")]
                    split_stage(g, "out", g.outT, *out2)
                    gemm(g, "wout", lambda oc: dram["w_out"][l, oc], KC, 4, 2, out2, residual_take(g, 2))
            g.end()
            g.begin()
            with ExitStack() as s1:
                g.h2 = [g.sb(s1, f"h{x}", [P, KC, NT], F32R) for x in ("hi", "lo")]
                norm_stage(g, "norm2", g.h2[0], lambda kc, c: g.gain[:, 1, kc, c:c + 1], lambda kc, c: g.modT[:, 3 * KC + kc, c:c + 1],
                           low=g.h2[1])
                with ExitStack() as s2:
                    sel = g.sb(s2, "sel", [P, 3, NT])
                    with ExitStack() as s3:
                        qT = g.sb(s3, "qT", [P, 2 * PH, NT])
                        gemm(g, "query", lambda oc: dram["peer_wq"][l, oc], 2 * PH, 4, 2, g.h2,
                             lambda ve, oc, sums: ve.tensor_copy(qT[:, bass.ds(oc, 1), :].rearrange("p o (h n) -> p (o h) n", n=H2), sums))
                        select_stage(g, l, qT, sel)
                    gates_stage(g, l, sel)
                acc = g.sb(s1, "acc", [P, TILES, D])
                experts_stage(g, l, acc)
                fold_stage(g, acc)
            g.end()

        g.begin()
        with ExitStack() as s1:
            out = g.sb(s1, "out", [P, KC, NT])
            norm_stage(g, "final", out, lambda kc, c: g.v("final", kc, kc + 1), None)
            with nc.Block() as block:
                @block.sync
                def _(sync):
                    sync.dma_start(dram["y"], out[:, :, :]).then_inc(y_out, 16)
                    sync.wait_ge(y_out, 16)


def constants():
    i = np.arange(P)
    same = (i[:, None] // CH) == (i[None, :] // CH)
    s, t = i[:, None], i[None, :]
    perm = np.zeros((P, P))
    for m in range(0, P, 2):
        perm[m + 1, m] = -1.0
        perm[m, m + 1] = 1.0
    tok = np.arange(NS)
    row, col = (tok // GRID_W).astype(np.float32), (tok % GRID_W).astype(np.float32)
    pairs = DK // 4
    inv = (np.float32(10000.0) ** (-np.arange(pairs, dtype=np.float32) / np.float32(pairs))).astype(np.float32)
    ang = np.concatenate([row[:, None] * inv, col[:, None] * inv], axis=-1).astype(np.float32)
    pair = (i % DK) // 2
    n = np.arange(NT)
    parts = {
        "ident": np.eye(P), "ones": np.ones((P, P)), "bones": same, "iota": np.broadcast_to(i, (P, P)), "perm": perm,
        "maskF": np.concatenate([same & (s < t), same & (s <= t)], 1),
        "maskB": np.concatenate([same & (s > t), same & (s >= t)], 1),
        "lowF": same & (t < s), "lowB": same & (t > s),
        "scanF": np.broadcast_to(n % CH != 0, (P, NT)), "scanB": np.broadcast_to(n % CH != CH - 1, (P, NT)),
        "cos": np.cos(ang).T[pair], "sin": np.sin(ang).T[pair],
    }
    return np.concatenate([np.asarray(parts[k], np.float32) for k in CI], axis=1)


def kernel(**inputs):
    import concourse.bacc as bacc
    from concourse.bass_utils import run_bass_kernel_spmd

    w = {k: np.asarray(x) for k, x in inputs.items()}
    L = DEPTH

    def chunks(x):
        n = x.shape[-1] // P
        return x.reshape(L, x.shape[1] // P, P, n, P).transpose(0, 3, 2, 1, 4)

    def vec(x):
        return x.reshape(L, -1, P).transpose(0, 2, 1)

    wi = w["w_in"]
    va, vb = wi[:, :, 512:768], wi[:, :, 768 + 1024:768 + 1536]
    lora = [w[k].transpose(0, 2, 1, 3).reshape(L, D, P) for k in ("rwkv_wA", "rwkv_aA")]
    w_proj = np.concatenate([wi[:, :, 0:768 + 1024], wi[:, :, 768 + 1536:], *lora, w["rwkv_gA"]], axis=2)
    lam_init = np.array([0.8 - 0.6 * np.exp(-0.3 * l) for l in range(L)], np.float32)
    cols = {
        "mod_b": vec(w["mod_b"]), "n1": vec(w["norm1_g"]), "n2": vec(w["norm2_g"]),
        "w0": vec(w["rwkv_w0"].reshape(L, -1)), "a0": vec(w["rwkv_a0"].reshape(L, -1)),
        "kk": vec(w["rwkv_kk"]), "ka": vec(w["rwkv_ka"]), "rk": vec(w["rwkv_rk"].reshape(L, -1)),
        "lng": vec(w["rwkv_ln_g"]), "sub": np.concatenate([w["diff_subln_g"]] * 2, 1)[:, :, None],
        "convw": vec(w["lru_conv_w"].reshape(L, -1)), "convb": vec(w["lru_conv_b"]),
        "ba": vec(w["lru_ba"].reshape(L, -1)), "bx": vec(w["lru_bx"].reshape(L, -1)), "lam": vec(w["lru_lambda"].reshape(L, -1)),
        "lq": np.broadcast_to(np.concatenate([w[f"diff_{n}"] for n in ("lq1", "lk1", "lq2", "lk2")], 1)[:, None, :], (L, P, 4 * DK)),
        "laminit": np.broadcast_to(lam_init[:, None, None], (L, P, 1)),
        "final": np.broadcast_to(w["final_norm_g"].reshape(1, KC, P).transpose(0, 2, 1), (L, P, KC)),
        "h0": vec(w["state_lru"][0].reshape(L, -1)),
    }
    x = np.concatenate([w["x_sample"][0], w["x_prompt"][0]], 0)
    lru = np.stack([w["lru_wa"], w["lru_wx"]], 1).reshape(L, 2, 2, CC, 2, HD, HD)
    arrays = {
        "consts": constants(),
        "vecs": np.concatenate([cols[k] for k in VI], axis=2),
        "x": x.T.reshape(KC, P, NT).transpose(1, 0, 2),
        "cond": np.stack([w["c"][0], w["c_ctx"]], 1).reshape(KC, P, 2).transpose(1, 0, 2),
        "mod_w": chunks(w["mod_w"]),
        "w_proj": chunks(w_proj),
        "w_v": np.concatenate([va, vb], 2).reshape(L, KC, P, VTOK).transpose(0, 2, 1, 3),
        "w_out": chunks(w["w_out"]),
        "cache_k": w["cache_k"][0].transpose(0, 1, 3, 2).reshape(L, CB, P, PAST).transpose(0, 2, 1, 3),
        "cache_v": w["cache_v"][0].transpose(0, 2, 1, 3).reshape(L, PAST // P, P, HB * HD).transpose(0, 2, 1, 3),
        "state_rwkv": w["state_rwkv"][0].reshape(L, 2, CA, 2, HD, HD).transpose(0, 3, 5, 1, 2, 4),
        "rwkv_B": np.stack([w["rwkv_wB"].reshape(L, P, CA * P), w["rwkv_aB"].reshape(L, P, CA * P)], 2),
        "rwkv_gB": w["rwkv_gB"],
        "lru_w": lru.transpose(0, 1, 4, 5, 2, 3, 6),
        "peer_wq": chunks(w["peer_wq"]),
        "peer_keys": w["peer_keys"].reshape(L, 2 * PH, NKEY, P).transpose(0, 3, 1, 2),
        "peer_u": w["peer_u"].reshape(L, NKEY, NKEY, KC, P).transpose(0, 2, 4, 3, 1),
        "peer_v": w["peer_v"].reshape(L, NKEY, NKEY * D),
    }
    arrays = {k: np.ascontiguousarray(a) for k, a in arrays.items()}
    nc = bacc.Bacc("TRN2", target_bir_lowering=False, num_devices=1)
    dram = {k: nc.dram_tensor(k, a.shape, F32, kind="ExternalInput").ap() for k, a in arrays.items()}
    outs = {
        "y": (P, KC, NT), "new_k": (L, P, CB, NPR), "new_v": (L, P, 512),
        "new_rwkv": (L, 2, HD, 2, CA, HD), "new_lru": (L, P, 2, CC),
    }
    for k, s in outs.items():
        dram[k] = nc.dram_tensor(k, s, F32, kind="ExternalOutput").ap()
    dram["gates"] = nc.dram_tensor("gates", (P, NG, NT // GT_N, GB * GT_N), F32, kind="Internal").ap()
    build(nc, dram)
    r = run_bass_kernel_spmd(nc, [arrays], core_ids=[0]).results[0]
    y = r["y"].transpose(2, 1, 0).reshape(NT, D)
    return (
        y[None, NS:], y[None, :NS],
        r["new_k"].transpose(0, 2, 1, 3).reshape(L, HB, HD, NPR).transpose(0, 1, 3, 2)[None],
        r["new_v"].reshape(L, NPR, HB, HD).transpose(0, 2, 1, 3)[None],
        r["new_rwkv"].transpose(0, 3, 4, 1, 5, 2).reshape(L, 2, HA, HD, HD)[None],
        r["new_lru"].transpose(0, 2, 3, 1).reshape(L, 2, CC * P)[None],
    )
```

```python
from contextlib import ExitStack

import numpy as np

import concourse.bass as bass
from concourse import mybir

F32 = mybir.dt.float32
U32 = mybir.dt.uint32
F32R = mybir.dt.float32r
BF16 = mybir.dt.bfloat16
ALU = mybir.AluOpType
ACT = mybir.ActivationFunctionType
AX = mybir.AxisListType

P = 128
D = 1024
DEPTH = 2
NS = 512
NPR = 128
NT = NS + NPR
TILES = NT // P
PAST = 256
GRID_W = 64
KC = D // P
HD = 64
CA = 2
HA = 4
HB = 8
CB = 4
DK = 32
CC = 2
DECAY_SCALE = 0.606531
CH = 64
PH = 8
TOPK = 16
NKEY = 128
LRU_C = 8.0
RMS_EPS = 1e-6
SUB_EPS = 1e-5
GN_EPS = 64e-5
NEG = -3.0e38

R0, K0, V0, Q0, B0, X0, G0, LW, LA, LG = 0, 2, 4, 6, 10, 14, 16, 18, 19, 20
NPROJ = 21
BH0, KH0 = X0, LW
VTOK = 768

CI = {}
_at = 0
for _n, _w in (("ident", P), ("ones", P), ("bones", P), ("iota", P), ("perm", P), ("maskF", 2 * P), ("maskB", 2 * P),
               ("lowF", P), ("lowB", P), ("scanF", NT), ("scanB", NT), ("cos", NS), ("sin", NS)):
    CI[_n] = (_at, _w)
    _at += _w
NCONST = _at
NKEEP = 4 * P

VI = {}
_at = 0
for _n, _w in (("mod_b", 48), ("n1", 8), ("n2", 8), ("w0", 4), ("a0", 4), ("kk", 2), ("ka", 2), ("rk", 2),
               ("lng", 2), ("sub", 1), ("convw", 8), ("convb", 2), ("ba", 4), ("bx", 4), ("lam", 4),
               ("lq", 4 * DK), ("laminit", 1), ("final", 8), ("h0", 4)):
    VI[_n] = (_at, _w)
    _at += _w
NVEC = _at


class Counter:

    def __init__(self, eng, sem):
        self.eng, self.sem, self.n = eng, sem, 0

    def did(self, inst):
        inst.then_inc(self.sem, 1)
        self.n += 1

    def wait(self):
        self.eng.wait_ge(self.sem, self.n)

    def then(self, inst):
        self.did(inst)
        self.wait()


class Program:
    def __init__(self, nc, ctx, dram):
        self.nc, self.ctx, self.dram = nc, ctx, dram
        self.sems = []
        self.n = 0

    def sem(self, name):
        s = self.phase.enter_context(self.nc.semaphore(name))
        self.sems.append(s)
        return s

    def begin(self):
        self.phase, self.sems = ExitStack(), []

    def end(self):
        nums = sorted(s.num for s in self.sems)
        runs = [n for n in nums if n - 1 not in nums]
        with self.nc.Block() as block:
            @block.gpsimd
            def _(pool):
                for a in runs:
                    b = a
                    while b in nums:
                        b += 1
                    pool.sem_clear(range(a, b))
        self.phase.close()

    def sb(self, st, name, shape, dt=F32):
        self.n += 1
        return st.enter_context(self.nc.sbuf_tensor(f"{name}_{self.n}", shape, dt))


def load_stage(g, l):
    nc, d = g.nc, g.dram
    loaded, done, ex = g.sem("vectors_loaded"), g.sem("lambda_steps"), g.sem("lambda_exps")
    sp, lam_exp = g.sem("softplus_steps"), g.sem("lru_lambda_exp")
    vec = g.vec

    def v(name, a=0, b=None):
        at, w = VI[name]
        return vec[:, at + a:at + (w if b is None else b)]

    g.v = v
    with nc.Block() as block:
        @block.sync
        def _(sync):
            sync.dma_start(vec[:, :], d["vecs"][l]).then_inc(loaded, 16)

        @block.vector
        def _(ve):
            c = Counter(ve, done)
            ve.wait_ge(loaded, 16)
            lq = v("lq").rearrange("p (a k) -> p a k", a=4)
            for i in range(2):
                c.then(ve.tensor_tensor(g.tiny[:, 8:8 + DK], lq[:, 2 * i, :], lq[:, 2 * i + 1, :], ALU.mult))
                c.then(ve.tensor_reduce(g.tiny[:, i:i + 1], g.tiny[:, 8:8 + DK], AX.X, ALU.add))
            ve.wait_ge(ex, 1)
            c.then(ve.tensor_tensor(g.lam[:, 0:1], g.tiny[:, 2:3], g.tiny[:, 3:4], ALU.subtract))
            c.then(ve.tensor_tensor(g.lam[:, 0:1], g.lam[:, 0:1], v("laminit"), ALU.add))
            c.then(ve.tensor_scalar(g.lam[:, 1:2], g.lam[:, 0:1], -1.0, None, ALU.mult))
            c.then(ve.tensor_scalar(g.lam[:, 2:3], v("laminit"), -1.0, 1.0, ALU.mult, ALU.add))
            c.then(ve.tensor_tensor(g.lam[:, 3:4], g.lam[:, 2:3], v("sub"), ALU.mult))
            c.then(ve.tensor_scalar(g.omka[:, :], v("ka"), -1.0, 1.0, ALU.mult, ALU.add))
            ve.wait_ge(sp, 1)
            c.then(ve.tensor_scalar(g.nsp[:, :], g.nsp[:, :], -LRU_C, None, ALU.mult))

        @block.scalar
        def _(act):
            c = Counter(act, sp)
            act.wait_ge(loaded, 16)
            act.wait_ge(done, 4)
            nc.scalar.activation(g.tiny[:, 2:4], g.tiny[:, 0:2], ACT.Exp).then_inc(ex, 1)
            nc.scalar.activation(g.nsp2[:, :], v("lam"), ACT.Exp, scale=-1.0).then_inc(lam_exp, 1)
            act.wait_ge(lam_exp, 1)
            c.did(nc.scalar.activation(g.nsp[:, :], g.nsp2[:, :], ACT.Ln, bias=1.0))


def split3(pe, out, lhs, rhs, start=True, stop=True):
    pe.matmul(out, lhs[1], rhs[0], start=start, stop=False)
    pe.matmul(out, lhs[0], rhs[1], start=False, stop=False)
    return pe.matmul(out, lhs[0], rhs[0], start=False, stop=stop)


def halves(ap):
    return ap.rearrange("p (h n) -> p h n", n=H2)


def gemm(g, name, weights, n_out, R, SR, rhs, take):
    nc = g.nc
    w_in = [g.sem(f"{name}_w_loaded{i}") for i in range(R)]
    w_hi, w_lo, ready, taken = (g.sem(f"{name}_{x}") for x in ("w_high", "w_low", "sums_ready", "sums_taken"))
    with ExitStack() as st, nc.Block() as block:
        raw = g.sb(st, f"{name}_raw", [P, R, KC, P])
        hi = g.sb(st, f"{name}_hi", [P, SR, KC, P], F32R)
        lo = g.sb(st, f"{name}_lo", [P, SR, KC, P], F32R)

        @block.sync
        def _(sync):
            sync.sem_inc(w_lo, R)
            with sync.Fori(0, n_out // R) as i:
                for j in range(R):
                    sync.wait_ge(w_lo, i * R + (j + 1))
                    sync.dma_start(raw[:, j, :, :], weights(i * R + j)).then_inc(w_in[j], 16)

        @block.scalar
        def _(act):
            act.sem_inc(ready, SR)
            with act.Fori(0, n_out // R) as i:
                for j in range(R):
                    act.wait_ge(w_in[j], i * 16 + 16)
                    act.wait_ge(ready, i * R + (j + 1))
                    nc.scalar.activation(hi[:, j % SR, :, :], raw[:, j, :, :], ACT.Copy).then_inc(w_hi, 1)

        @block.tensor
        def _(pe):
            with pe.Fori(0, n_out // R) as i:
                for j in range(R):
                    pe.wait_ge(w_lo, i * R + (j + 1 + R))
                    pe.wait_ge(taken, i * R + (j + 1))
                    w = (hi[:, j % SR, :, :], lo[:, j % SR, :, :])
                    for h in range(2):
                        cols = slice(h * H2, (h + 1) * H2)
                        for kc in range(KC):
                            mm = split3(pe, g.ps[:, 2 * j + h, 0:H2], [x[:, kc, :] for x in w], [x[:, kc, cols] for x in rhs],
                                        start=(kc == 0), stop=(kc == KC - 1))
                    mm.then_inc(ready, 1)

        @block.vector
        def _(ve):
            ve.sem_inc(taken, R)

            def low(i, j):
                ve.wait_ge(w_hi, i * R + (j + 1))
                s = (j % R) % SR
                ve.tensor_tensor(lo[:, s, :, :], raw[:, j % R, :, :], hi[:, s, :, :].bitcast(F32), ALU.subtract).then_inc(w_lo, 1)

            def turn(i, last):
                for j in range(R):
                    if not (last and j == R - 1):
                        low(i, j + 1)
                    ve.wait_ge(ready, i * R + (j + 1 + SR))
                    take(ve, i * R + j, g.ps[:, 2 * j:2 * j + 2, 0:H2]).then_inc(taken, 1)

            low(0, 0)
            with ve.Fori(0, n_out // R - 1) as i:
                turn(i, False)
            turn(n_out // R - 1, True)


MP = 512
NM = 6 * D // MP


class Modulation:

    def __init__(self, g, st, weights):
        self.g, self.weights = g, weights
        self.ring = g.sb(st, "mod_ring", [P, 2, KC, MP])
        self.rows = g.sb(st, "mod_rows", [2, 2, MP])
        self.w_in = [g.sem(f"mod_w_loaded{i}") for i in range(2)]
        self.summed, self.row, self.turned, self.taken = (g.sem(f"mod_{x}") for x in ("summed", "row_taken", "transposed", "columns_taken"))

    def load(self, sync):
        for i in range(NM):
            if i >= 2:
                sync.wait_ge(self.summed, i - 1)
            sync.dma_start(self.ring[:, i % 2, :, :], self.weights(i)).then_inc(self.w_in[i % 2], 16)

    def sums(self, pe, i):
        pe.wait_ge(self.w_in[i % 2], 16 * (i // 2 + 1))
        if i >= 2:
            pe.wait_ge(self.row, i - 1)
        for kc in range(KC):
            mm = pe.matmul(self.g.ps[0:2, 5 + i % 2, :], self.g.scond[:, kc, :], self.ring[:, i % 2, kc, :],
                           start=(kc == 0), stop=(kc == KC - 1))
        mm.then_inc(self.summed, 1)

    def turn(self, pe, i):
        pe.wait_ge(self.row, i + 1)
        if i >= 1:
            pe.wait_ge(self.taken, i)
        for c in range(MP // P):
            mm = pe.transpose(self.g.ps[:, 7, 2 * c:2 * c + 2], self.rows[:, i % 2, c * P:(c + 1) * P], self.g.ident[0:2, 0:2])
        mm.then_inc(self.turned, 1)

    def take_row(self, act, i):
        act.wait_ge(self.summed, i + 1)
        if i >= 2:
            act.wait_ge(self.turned, i - 1)
        self.g.nc.scalar.activation(self.rows[:, i % 2, :], self.g.ps[0:2, 5 + i % 2, :], ACT.Copy).then_inc(self.row, 1)

    def take_columns(self, act, i):
        n = MP // P
        act.wait_ge(self.turned, i + 1)
        self.g.nc.scalar.activation(self.g.modN[:, i * n:(i + 1) * n, :], self.g.ps[:, 7, 0:2 * n], ACT.Copy).then_inc(self.taken, 1)

    def on_tensor(self, pe, first, last):
        for i in range(first, last + 1):
            if i < last:
                self.sums(pe, i)
            if i > first:
                self.turn(pe, i - 1)

    def on_scalar(self, act, first, last):
        for i in range(first, last + 1):
            if i < last:
                self.take_row(act, i)
            if i > first:
                self.take_columns(act, i - 1)


def first_mod_stage(g):
    nc, d = g.nc, g.dram
    loaded, silu = g.sem("cond_loaded"), g.sem("cond_silu")
    with ExitStack() as st, nc.Block() as block:
        mod = Modulation(g, st, lambda i: d["mod_w"][DEPTH - 1, i])

        @block.sync
        def _(sync):
            sync.dma_start(g.keep[:, :], d["consts"][:, 0:NKEEP]).then_inc(loaded, 16)
            sync.dma_start(g.cond[:, :, :], d["cond"]).then_inc(loaded, 16)
            sync.dma_start(g.xT[:, :, :], d["x"]).then_inc(loaded, 16)
            mod.load(sync)
            sync.wait_ge(loaded, 48)

        @block.scalar
        def _(act):
            act.wait_ge(loaded, 48)
            nc.scalar.activation(g.scond[:, :, :], g.cond[:, :, :], ACT.Silu).then_inc(silu, 1)
            mod.on_scalar(act, 0, NM)

        @block.tensor
        def _(pe):
            pe.wait_ge(silu, 1)
            mod.on_tensor(pe, 0, NM)


def mod_stage(g):
    nc, v = g.nc, g.v
    steps = g.sem("mod_steps")
    with nc.Block() as block:
        @block.vector
        def _(ve):
            c = Counter(ve, steps)
            c.then(ve.tensor_tensor(g.modT[:, :, :], g.modN[:, :, :],
                                    v("mod_b").unsqueeze(2).broadcast_to([P, 6 * KC, 2]), ALU.add))
            for i, (name, part) in enumerate((("n1", 1), ("n2", 4))):
                c.then(ve.tensor_scalar(g.gain[:, i, :, :], g.modT[:, part * KC:(part + 1) * KC, :], 1.0, None, ALU.add))
                c.then(ve.tensor_tensor(g.gain[:, i, :, :], g.gain[:, i, :, :],
                                        v(name).unsqueeze(2).broadcast_to([P, KC, 2]), ALU.mult))


def norm_stage(g, name, out, gain, shift, low=None):
    nc = g.nc
    sq_ready, sum_ready, r_ready, steps = (g.sem(f"{name}_{x}") for x in ("squared", "summed", "root", "steps"))
    scaled, normed, lowed = g.sem(f"{name}_scaled"), g.sem(f"{name}_normed"), g.sem(f"{name}_low")
    with ExitStack() as st, nc.Block() as block:
        sq = g.sb(st, "sq", [P, 2, NT])
        rs = g.sb(st, "rs", [P, 2, NT])
        t = g.sb(st, "t", [P, 3, NT])
        raw = (lambda kc: out[:, kc, :]) if low is None else (lambda kc: t[:, kc % 3, :])

        @block.scalar
        def _(act):
            for kc in range(KC):
                if kc >= 2:
                    act.wait_ge(sum_ready, kc - 1)
                nc.scalar.activation(sq[:, kc % 2, :], g.xT[:, kc, :], ACT.Square).then_inc(sq_ready, 1)
            act.wait_ge(steps, 1)
            nc.scalar.activation(rs[:, 1, :], rs[:, 0, :], ACT.Sqrt).then_inc(r_ready, 1)
            for kc in range(KC):
                act.wait_ge(scaled, kc + 1)
                for c, (a, b) in enumerate(((0, NS), (NS, NT))):
                    last = nc.scalar.activation(raw(kc)[:, a:b], raw(kc)[:, a:b], ACT.Identity,
                                                scale=gain(kc, c), bias=shift(kc, c) if shift else 0.0)
                last.then_inc(normed, 1)
                if low is not None:
                    act.wait_ge(normed, 2 * kc + 1)
                    nc.scalar.activation(out[:, kc, :], raw(kc), ACT.Copy).then_inc(normed, 1)

        @block.tensor
        def _(pe):
            for kc in range(KC):
                pe.wait_ge(sq_ready, kc + 1)
                for bank, (a, b) in enumerate(((0, NS), (NS, NT))):
                    mm = pe.matmul(g.ps[:, bank, 0:b - a], g.ones, sq[:, kc % 2, a:b], start=(kc == 0), stop=(kc == KC - 1))
                mm.then_inc(sum_ready, 1)

        @block.vector
        def _(ve):
            c = Counter(ve, steps)
            ve.wait_ge(sum_ready, KC)
            c.did(ve.tensor_scalar(rs[:, 0, :], g.flat[:, 0:NT], 1.0 / D, RMS_EPS, ALU.mult, ALU.add))
            ve.wait_ge(r_ready, 1)
            c.then(ve.reciprocal(rs[:, 0, :], rs[:, 1, :]))

            def lower(kc):
                ve.wait_ge(normed, 2 * kc + 2)
                ve.tensor_tensor(low[:, kc, :], raw(kc), out[:, kc, :].bitcast(F32), ALU.subtract).then_inc(lowed, 1)

            for kc in range(KC):
                if low is not None and kc >= 3:
                    ve.wait_ge(lowed, kc - 2)
                ve.tensor_tensor(raw(kc), g.xT[:, kc, :], rs[:, 0, :], ALU.mult).then_inc(scaled, 1)
                if low is not None and kc >= 1:
                    lower(kc - 1)
            if low is not None:
                lower(KC - 1)


def split_stage(g, name, src, hi, lo):
    nc = g.nc
    high = g.sem(f"{name}_high")
    with nc.Block() as block:
        @block.scalar
        def _(act):
            for kc in range(KC):
                nc.scalar.activation(hi[:, kc, :], src[:, kc, :], ACT.Copy).then_inc(high, 1)

        @block.vector
        def _(ve):
            for kc in range(KC):
                ve.wait_ge(high, kc + 1)
                ve.tensor_tensor(lo[:, kc, :], src[:, kc, :], hi[:, kc, :].bitcast(F32), ALU.subtract)


VP = 256


def proj_stage(g, l):
    nc, d = g.nc, g.dram
    gemm(g, "proj", lambda oc: d["w_proj"][l, oc], NPROJ, 3, 3, g.h2,
         lambda ve, oc, sums: ve.tensor_copy(g.proj[:, bass.ds(oc, 1), :].rearrange("p o (h n) -> p (o h) n", n=H2), sums))
    w_in, w_hi, w_lo, ready, taken = (g.sem(f"vtok_{x}") for x in ("w_loaded", "w_high", "w_low", "ready", "taken"))
    NP = VTOK // VP
    with ExitStack() as st, nc.Block() as block:
        raw = g.sb(st, "wv", [P, KC, VP])
        hi = g.sb(st, "wvh", [P, 2, KC, VP], F32R)
        lo = g.sb(st, "wvl", [P, 2, KC, VP], F32R)

        @block.sync
        def _(sync):
            for c in range(NP):
                if c:
                    sync.wait_ge(w_lo, c)
                sync.dma_start(raw[:, :, :], d["w_v"][l, :, :, c * VP:(c + 1) * VP]).then_inc(w_in, 16)

        @block.scalar
        def _(act):
            for c in range(NP):
                act.wait_ge(w_in, 16 * (c + 1))
                if c >= 2:
                    act.wait_ge(ready, TILES * (c - 1))
                nc.scalar.activation(hi[:, c % 2, :, :], raw[:, :, :], ACT.Copy).then_inc(w_hi, 1)

        @block.tensor
        def _(pe):
            for c in range(NP):
                pe.wait_ge(w_lo, c + 1)
                for t in range(TILES):
                    n = c * TILES + t
                    if n >= 8:
                        pe.wait_ge(taken, n - 7)
                    for kc in range(KC):
                        mm = split3(pe, g.ps[:, n % 8, 0:VP], [x[:, kc, t * P:(t + 1) * P] for x in g.h2],
                                    [x[:, c % 2, kc, :] for x in (hi, lo)], start=(kc == 0), stop=(kc == KC - 1))
                    mm.then_inc(ready, 1)

        @block.vector
        def _(ve):
            def low(c):
                ve.wait_ge(w_hi, c + 1)
                ve.tensor_tensor(lo[:, c % 2, :, :], raw[:, :, :], hi[:, c % 2, :, :].bitcast(F32), ALU.subtract).then_inc(w_lo, 1)

            low(0)
            low(1)
            for c in range(NP):
                for t in range(TILES):
                    n = c * TILES + t
                    ve.wait_ge(ready, n + 1)
                    ve.tensor_copy(g.vtok[:, t, c * VP:(c + 1) * VP], g.ps[:, n % 8, 0:VP]).then_inc(taken, 1)
                if c + 2 < NP:
                    low(c + 2)


def rope_stage(g, l):
    nc, d = g.nc, g.dram
    loaded, out_done = g.sem("rope_consts_loaded"), g.sem("cache_stored")
    rot, cosd, sind = g.sem("rotated"), g.sem("cos_done"), g.sem("sin_done")
    added = g.sem("rope_added")
    with ExitStack() as st, nc.Block() as block:
        cs = g.sb(st, "ropecs", [P, 2, NS])
        perm = g.sb(st, "perm", [P, P])
        tmp = g.sb(st, "ropetmp", [P, 2, 2, NS])
        at = CI["cos"][0]

        @block.sync
        def _(sync):
            sync.dma_start(cs[:, :, :], d["consts"][:, at:at + 2 * NS]).then_inc(loaded, 16)
            sync.dma_start(perm[:, :], d["consts"][:, CI["perm"][0]:CI["perm"][0] + P]).then_inc(loaded, 16)
            sync.dma_start(g.kctx[:, :, :], d["cache_k"][l]).then_inc(loaded, 16)
            sync.dma_start(g.vctx[:, :, :], d["cache_v"][l]).then_inc(loaded, 16)
            sync.dma_start(d["new_k"][l], g.proj[:, B0:B0 + CB, NS:NT]).then_inc(out_done, 16)
            sync.dma_start(d["new_v"][l], g.vtok[:, TILES - 1, 256:VTOK]).then_inc(out_done, 16)
            sync.wait_ge(out_done, 32)
            sync.wait_ge(loaded, 64)

        @block.tensor
        def _(pe):
            pe.wait_ge(loaded, 64)
            for c in range(8):
                if c >= 2:
                    pe.wait_ge(sind, c - 1)
                pe.matmul(g.ps[:, c % 2, :], perm[:, :], g.proj[:, Q0 + c, 0:NS], start=True, stop=True).then_inc(rot, 1)

        @block.gpsimd
        def _(pool):
            pool.wait_ge(loaded, 64)
            for c in range(8):
                if c >= 2:
                    pool.wait_ge(added, c - 1)
                pool.tensor_tensor(tmp[:, 0, c % 2, :], g.proj[:, Q0 + c, 0:NS], cs[:, 0, :], ALU.mult).then_inc(cosd, 1)

        @block.vector
        def _(ve):
            for c in range(8):
                ve.wait_ge(rot, c + 1)
                ve.tensor_tensor(tmp[:, 1, c % 2, :], g.ps[:, c % 2, :], cs[:, 1, :], ALU.mult).then_inc(sind, 1)
                ve.wait_ge(sind, c + 1)
                ve.wait_ge(cosd, c + 1)
                ve.tensor_tensor(g.proj[:, Q0 + c, 0:NS], tmp[:, 0, c % 2, :], tmp[:, 1, c % 2, :], ALU.add).then_inc(added, 1)


def head_sums(g, pe, src, ready, done, n_chunks=CA, first_bank=0):
    for c in range(n_chunks):
        pe.wait_ge(ready, c + 1)
        for bank, (a, b) in enumerate(((0, NS), (NS, NT))):
            mm = pe.matmul(g.ps[:, first_bank + 2 * c + bank, 0:b - a], g.bones, src(c)[:, a:b], start=True, stop=True)
        mm.then_inc(done, 1)


def subln_stage(g):
    nc = g.nc
    sq, sums, steps, roots = (g.sem(f"subln_{x}") for x in ("squared", "summed", "steps", "roots"))
    with ExitStack() as st, nc.Block() as block:
        s = g.sb(st, "s", [P, CB, NT])

        @block.scalar
        def _(act):
            for c in range(CB):
                nc.scalar.activation(s[:, c, :], g.outT[:, CA + c, :], ACT.Square).then_inc(sq, 1)
            for c in range(CB):
                act.wait_ge(steps, c + 1)
                nc.scalar.activation(s[:, c, :], s[:, c, :], ACT.Sqrt).then_inc(roots, 1)

        @block.tensor
        def _(pe):
            head_sums(g, pe, lambda c: s[:, c, :], sq, sums, n_chunks=CB)

        @block.vector
        def _(ve):
            k = Counter(ve, steps)
            for c in range(CB):
                ve.wait_ge(sums, c + 1)
                k.did(ve.tensor_scalar(s[:, c, :], g.flat[:, 1024 * c:1024 * c + NT], 1.0 / HD, SUB_EPS, ALU.mult, ALU.add))
            for c in range(CB):
                ve.wait_ge(roots, c + 1)
                k.then(ve.reciprocal(s[:, c, :], s[:, c, :]))
                k.did(ve.scalar_tensor_tensor(g.outT[:, CA + c, :], g.outT[:, CA + c, :], g.lam[:, 3:4], s[:, c, :],
                                              ALU.mult, ALU.mult))


def lru_stage(g, l):
    nc, d, v = g.nc, g.dram, g.v
    wl, zero, conv, gate_mm, gate_tk = (g.sem(f"lru_{x}") for x in ("w_loaded", "w_zero", "conv", "gates_summed", "gates_taken"))
    steps, agates, scans, out_st, gel = (g.sem(f"lru_{x}") for x in ("steps", "a_steps", "scans", "stored", "gelu"))
    SEQS = ((0, NS), (NS, NT))
    with ExitStack() as st, nc.Block() as block:
        w = g.sb(st, "lruw", [P, 2, 2, CC, P])
        xp = g.sb(st, "xpad", [P, CC, NT + 6])
        xc = g.sb(st, "xconv", [P, CC, NT])
        ga = g.sb(st, "ga", [P, NT])
        gi = g.sb(st, "gi", [P, NT])
        a = g.sb(st, "a", [P, NT])
        th = g.sb(st, "th", [P, NT])
        bt = g.sb(st, "bt", [P, NT])
        hs = g.sb(st, "hs", [P, CC, 2, NT])
        last = g.sb(st, "last", [P, 2, CC])

        @block.gpsimd
        def _(pool):
            pool.memset(w[:, :, :, :, :], 0.0).then_inc(zero, 1)

        @block.sync
        def _(sync):
            sync.wait_ge(zero, 1)
            for q in range(2):
                for half in range(2):
                    sync.dma_start(w[half * HD:(half + 1) * HD, q, :, :, half * HD:(half + 1) * HD],
                                   d["lru_w"][l, q, half]).then_inc(wl, 16)
            sync.wait_ge(steps, 3 * 2 * CC)
            sync.dma_start(d["new_lru"][l], last[:, :, :]).then_inc(out_st, 16)
            sync.wait_ge(out_st, 16)

        @block.tensor
        def _(pe):
            pe.wait_ge(wl, 64)
            pe.wait_ge(conv, CC)
            n = 0
            for c in range(CC):
                for dr in range(2):
                    for q in range(2):
                        if n >= 4:
                            pe.wait_ge(gate_tk, n - 3)
                        for bank, (x, y) in enumerate(SEQS):
                            mm = pe.matmul(g.ps[:, 2 * (n % 4) + bank, 0:y - x], w[:, q, dr, c, :], xc[:, c, x:y], start=True, stop=True)
                        mm.then_inc(gate_mm, 1)
                        n += 1

        @block.scalar
        def _(act):
            s = Counter(act, agates)
            for c in range(CC):
                nc.scalar.activation(g.outT[:, CA + CB + c, :], g.proj[:, G0 + c, :], ACT.Gelu).then_inc(gel, 1)
            n = 0
            for c in range(CC):
                for dr in range(2):
                    col = 2 * dr + c
                    i = 2 * c + dr
                    if i >= 1:
                        act.wait_ge(steps, 3 * i)
                    for q, dst, bias in ((0, ga, "ba"), (1, gi, "bx")):
                        act.wait_ge(gate_mm, n + 1)
                        nc.scalar.activation(dst[:, :], g.flat[:, 1024 * (n % 4):1024 * (n % 4) + NT], ACT.Sigmoid,
                                             bias=v(bias, col, col + 1)).then_inc(gate_tk, 1)
                        n += 1
                    act.wait_ge(gate_tk, n)
                    s.did(nc.scalar.activation(a[:, :], ga[:, :], ACT.Exp, scale=g.nsp[:, col:col + 1]))
                    s.then(nc.scalar.activation(th[:, :], ga[:, :], ACT.Tanh, scale=g.nsp[:, col:col + 1]))
                    act.wait_ge(steps, 3 * i + 2)
                    s.did(nc.scalar.activation(ga[:, :], ga[:, :], ACT.Sqrt))

        @block.vector
        def _(ve):
            k = Counter(ve, scans)
            s = Counter(ve, steps)
            cv = Counter(ve, g.sem("lru_conv_steps"))
            cv.then(ve.memset(xp[:, :, :], 0.0))
            for c in range(CC):
                cv.did(ve.tensor_copy(xp[:, c, 2:2 + NS], g.proj[:, X0 + c, 0:NS]))
                cv.did(ve.tensor_copy(xp[:, c, NS + 5:NS + 5 + NPR], g.proj[:, X0 + c, NS:NT]))
            cv.wait()
            for c in range(CC):
                for (x, y), at in zip(SEQS, (0, NS + 3)):
                    for j in range(4):
                        src = xp[:, c, at + j:at + j + y - x]
                        if j == 0:
                            i = ve.tensor_scalar(xc[:, c, x:y], src, v("convw", 2 * j + c, 2 * j + c + 1), v("convb", c, c + 1), ALU.mult, ALU.add)
                        else:
                            i = ve.scalar_tensor_tensor(xc[:, c, x:y], src, v("convw", 2 * j + c, 2 * j + c + 1), xc[:, c, x:y], ALU.mult, ALU.add)
                        if j < 3 or y == NS:
                            cv.then(i)
                        else:
                            i.then_inc(conv, 1)
            ve.wait_ge(conv, CC)
            for c in range(CC):
                for dr in range(2):
                    i = 2 * c + dr
                    col = 2 * dr + c
                    ve.wait_ge(agates, 3 * i + 2)
                    s.then(ve.tensor_tensor(bt[:, :], a[:, :], a[:, :], ALU.mult))
                    k.then(ve.scalar_tensor_tensor(bt[:, :], bt[:, :], 1.0, th[:, :], ALU.add, ALU.mult))
                    s.did(ve.tensor_scalar(ga[:, :], bt[:, :], -1.0, None, ALU.mult))
                    k.then(ve.tensor_tensor(gi[:, :], gi[:, :], xc[:, c, :], ALU.mult))
                    ve.wait_ge(agates, 3 * i + 3)
                    k.then(ve.tensor_tensor(bt[:, :], ga[:, :], gi[:, :], ALU.mult))
                    for j, (x, y) in enumerate(SEQS):
                        init = v("h0", col, col + 1) if j == 0 else 0.0
                        o, aa, bb = hs[:, c, dr, x:y], a[:, x:y], bt[:, x:y]
                        if dr:
                            o, aa, bb = o[:, ::-1], aa[:, ::-1], bb[:, ::-1]
                        k.did(ve.tensor_tensor_scan(o, aa, bb, init, ALU.mult, ALU.add))
                    k.wait()
                    e = NT - 1 if dr == 0 else NS
                    s.did(ve.tensor_copy(last[:, dr, c:c + 1], hs[:, c, dr, e:e + 1]))
                    s.wait()
                k.then(ve.tensor_tensor(hs[:, c, 0, :], hs[:, c, 0, :], hs[:, c, 1, :], ALU.add))
                ve.wait_ge(gel, c + 1)
                k.did(ve.tensor_tensor(g.outT[:, CA + CB + c, :], g.outT[:, CA + CB + c, :], hs[:, c, 0, :], ALU.mult))


def rwkv_prepare(g, l, keep):
    nc, d, v = g.nc, g.dram, g.v
    ar, gt, pc = keep
    loaded, first, zs, z_tk = (g.sem(f"rwkv_{x}") for x in ("lora_loaded", "lora_in", "lora_summed", "lora_taken"))
    sq, kks, roots = (g.sem(f"rwkv_{x}") for x in ("key_squared", "prep_steps", "key_roots"))
    logs, exps, kk_tk = (g.sem(f"rwkv_{x}") for x in ("logs_ready", "exps_ready", "key_sums_taken"))
    with ExitStack() as st, nc.Block() as block:
        wb = g.sb(st, "wB", [P, 2, CA * P])
        gb = g.sb(st, "gB", [P, CA * P])
        t1 = g.sb(st, "t1", [P, 2, NT])
        lw = g.sb(st, "lw", [P, 4, NT])
        aa = g.sb(st, "aa", [P, 4, NT])
        kk = g.sb(st, "kk", [P, CA, NT])
        e = g.sb(st, "e", [P, 2, 3, NT])
        sc = g.sb(st, "scan", [P, 2, NT])

        @block.sync
        def _(sync):
            sync.dma_start(wb[:, :, :], d["rwkv_B"][l]).then_inc(loaded, 16)
            sync.dma_start(gb[:, :], d["rwkv_gB"][l]).then_inc(loaded, 16)
            sync.dma_start(sc[:, :, :], d["consts"][:, CI["scanF"][0]:CI["scanF"][0] + 2 * NT]).then_inc(loaded, 16)

        @block.tensor
        def _(pe):
            pe.wait_ge(loaded, 48)
            n = 0

            def sums(lhs, rhs):
                nonlocal n
                if n >= 4:
                    pe.wait_ge(z_tk, n - 3)
                for bank, (x, y) in enumerate(((0, NS), (NS, NT))):
                    mm = pe.matmul(g.ps[:, 2 * (n % 4) + bank, 0:y - x], lhs, rhs[:, x:y], start=True, stop=True)
                mm.then_inc(zs, 1)
                n += 1

            pe.wait_ge(first, 2)
            for q in range(2):
                for dr in range(2):
                    rows = slice(dr * HD, (dr + 1) * HD)
                    for c in range(CA):
                        sums(wb[rows, q, c * P:(c + 1) * P], t1[rows, 0, :] if q == 0 else g.proj[rows, LA, :])
            for c in range(CA):
                sums(gb[:, c * P:(c + 1) * P], t1[:, 1, :])
            for c in range(CA):
                pe.wait_ge(sq, c + 1)
                sums(g.bones, e[:, c, 0, :])

        @block.scalar
        def _(act):
            nc.scalar.activation(t1[:, 0, :], g.proj[:, LW, :], ACT.Tanh).then_inc(first, 1)
            nc.scalar.activation(t1[:, 1, :], g.proj[:, LG, :], ACT.Sigmoid).then_inc(first, 1)
            n = 0
            for q, dst, bias in ((0, lw, "w0"), (1, aa, "a0")):
                for i in range(4):
                    act.wait_ge(zs, n + 1)
                    nc.scalar.activation(dst[:, i, :], g.flat[:, 1024 * (n % 4):1024 * (n % 4) + NT], ACT.Sigmoid,
                                         bias=v(bias, i, i + 1)).then_inc(z_tk, 1)
                    n += 1
            for c in range(CA):
                act.wait_ge(zs, n + 1)
                nc.scalar.activation(gt[:, c, :], g.flat[:, 1024 * (n % 4):1024 * (n % 4) + NT], ACT.Copy).then_inc(z_tk, 1)
                n += 1
            for c in range(CA):
                act.wait_ge(kk_tk, c + 1)
                nc.scalar.activation(e[:, c, 0, :], e[:, c, 1, :], ACT.Sqrt).then_inc(roots, 1)
            for i in range(4):
                act.wait_ge(logs, 2 * i + 2)
                nc.scalar.activation(e[:, i % 2, 2, :], e[:, i % 2, 0, :], ACT.Exp, scale=-1.0).then_inc(exps, 1)
                act.wait_ge(exps, 3 * i + 1)
                nc.scalar.activation(e[:, i % 2, 0, :], e[:, i % 2, 0, :], ACT.Exp).then_inc(exps, 1)
                nc.scalar.activation(e[:, i % 2, 1, :], e[:, i % 2, 1, :], ACT.Exp).then_inc(exps, 1)

        @block.vector
        def _(ve):
            k = Counter(ve, kks)
            ve.wait_ge(loaded, 48)
            for c in range(CA):
                k.then(ve.tensor_scalar(kk[:, c, :], g.proj[:, K0 + c, :], v("kk", c, c + 1), None, ALU.mult))
                ve.tensor_tensor(e[:, c, 0, :], kk[:, c, :], kk[:, c, :], ALU.mult).then_inc(sq, 1)
            for c in range(CA):
                n = 10 + c
                ve.wait_ge(zs, n + 1)
                ve.tensor_scalar(e[:, c, 1, :], g.flat[:, 1024 * (n % 4):1024 * (n % 4) + NT], 1e-12, None, ALU.max).then_inc(kk_tk, 1)
            for c in range(CA):
                ve.wait_ge(roots, c + 1)
                k.then(ve.reciprocal(e[:, c, 1, :], e[:, c, 0, :]))
                k.then(ve.tensor_tensor(kk[:, c, :], kk[:, c, :], e[:, c, 1, :], ALU.mult))
            k.then(ve.tensor_scalar(lw[:, :, :], lw[:, :, :], -DECAY_SCALE, None, ALU.mult))

            def log_sums(i):
                dr = i // 2
                o, m, x = e[:, i % 2, 0, :], sc[:, dr, :], lw[:, i, :]
                if dr:
                    o, m, x = o[:, ::-1], m[:, ::-1], x[:, ::-1]
                if i >= 2:
                    ve.wait_ge(kks, k.n)
                ve.tensor_tensor_scan(o, m, x, 0.0, ALU.mult, ALU.add).then_inc(logs, 1)
                ve.wait_ge(logs, 2 * i + 1)
                ve.tensor_tensor(e[:, i % 2, 1, :], e[:, i % 2, 0, :], lw[:, i, :], ALU.subtract).then_inc(logs, 1)

            def tiled(x):
                return x.rearrange("p (t n) -> p t n", n=P)

            log_sums(0)
            for i in range(4):
                dr, c = divmod(i, 2)
                if i < 3:
                    log_sums(i + 1)
                ve.wait_ge(exps, 3 * i + 3)
                ep, em, en = (e[:, i % 2, j, :] for j in range(3))
                k.did(ve.tensor_tensor(ar[:, dr, c, :, 1, :], tiled(g.proj[:, R0 + c, :]), tiled(ep), ALU.mult))
                k.did(ve.scalar_tensor_tensor(ar[:, dr, c, :, 0, :], tiled(kk[:, c, :]), -1.0, tiled(em), ALU.mult, ALU.mult))
                k.did(ve.tensor_copy(pc[:, dr, c, :], ep.rearrange("p (n t) -> p n t", t=CH)[:, :, 0 if dr else CH - 1]))
                b, kh = g.proj[:, BH0 + i, :], g.proj[:, KH0 + i, :]
                k.then(ve.tensor_tensor(b, kk[:, c, :], aa[:, i, :], ALU.mult))
                k.did(ve.tensor_tensor(b, b, en, ALU.mult))
                k.then(ve.tensor_scalar(kh, aa[:, i, :], v("ka", c, c + 1), g.omka[:, c:c + 1], ALU.mult, ALU.add))
                k.then(ve.tensor_tensor(kh, kh, g.proj[:, K0 + c, :], ALU.mult))
                k.then(ve.tensor_tensor(kh, kh, en, ALU.mult))


HOPS = [("pairs", "V"), ("lower", "VA"), ("square1", "VA"), ("square2", "VA"), ("square3", "VA"), ("square4", "VA"),
        ("square5", "V"), ("inverse", "V")] + [(x + str(i), "V") for i in range(2) for x in ("rhs", "sa", "state")]
SLOTS = [(step, dr, name, by) for step in range(TILES) for dr in range(2) for name, by in HOPS]
UNITS = [(h, t) for t in range(TILES) for h in range(HB)]


def attention_parts(slot):
    u, part = divmod(slot, 3)
    if part < 2:
        parts = [("values", u - 2, None)] if part == 1 else []
        parts += [("scores", u, part)]
    else:
        parts = [("combine", u, None), ("transpose", u - 1, None)]
    return [p for p in parts if 0 <= p[1] < len(UNITS)]


def pair(slot):
    return 4 + 2 * (slot % 2)


assert len(SLOTS) >= 3 * (len(UNITS) + 2)


def mix_stage(g, l, keep):
    nc, d = g.nc, g.dram
    ar, gt, pc = keep
    ready, byv, bya = g.sem("products_ready"), g.sem("by_vector"), g.sem("by_scalar")
    loaded, zeroed, stored, own, final = (g.sem(f"scan_{x}") for x in ("loaded", "zeroed", "stored", "steps", "final_states"))
    scale = DK ** -0.5
    s_ready, m_ready, e_done = g.sem("scores_ready"), g.sem("row_max_ready"), g.sem("exps_ready")
    comb, t_ready = g.sem("probs_combined"), g.sem("probs_transposed")
    pt_ready, o_ready, o_taken = g.sem("probsT_ready"), g.sem("attn_out_ready"), g.sem("attn_out_taken")
    A, B, C, O = 0, 1, 2, 3
    with ExitStack() as st, nc.Block() as block:
        mask = g.sb(st, "mask", [P, 2, 2 * P])
        low = g.sb(st, "low", [P, 2, P])
        mb = g.sb(st, "mb", [P, CA, 2, 2, P])
        mk = g.sb(st, "mk", [P, CA, 2, 2, P])
        pw = g.sb(st, "pw", [P, HA, P])
        pwt = g.sb(st, "pwt", [P, HA, P])
        x = g.sb(st, "x", [P, HA, P])
        bt = g.sb(st, "bt", [P, 2, CA * P])
        sz = g.sb(st, "sz", [P, 2, CA, P])
        szt = g.sb(st, "szt", [P, CA, P])
        rh = g.sb(st, "rh", [P, CA * P])
        sa = g.sb(st, "sa", [P, CA * P])
        p = g.sb(st, "p", [P, 2, 2, NS + PAST])
        pt = g.sb(st, "pt", [P, 2, NS + PAST])
        mx = g.sb(st, "mx", [P, 2, 4])
        sm = g.sb(st, "sm", [P, 2, 4])
        heads = [(c, h, slice(h * HD, (h + 1) * HD)) for c in range(CA) for h in range(2)]

        def tile(step, dr):
            return TILES - 1 if step == TILES - 1 else (step if dr == 0 else NS // P - 1 - step)

        def half(i, dr):
            return i if dr == 0 else 1 - i

        def nk(t):
            return P if t == TILES - 1 else NS + PAST

        @block.sync
        def _(sync):
            sync.dma_start(mask[:, :, :], d["consts"][:, CI["maskF"][0]:CI["maskF"][0] + 4 * P]).then_inc(loaded, 16)
            sync.dma_start(low[:, :, :], d["consts"][:, CI["lowF"][0]:CI["lowF"][0] + 2 * P]).then_inc(loaded, 16)
            sync.wait_ge(zeroed, 1)
            for h in range(2):
                rows = slice(h * HD, (h + 1) * HD)
                sync.dma_start(sz[rows, :, :, h * HD:(h + 1) * HD], d["state_rwkv"][l, h]).then_inc(loaded, 16)
            sync.wait_ge(final, 4)
            for h in range(2):
                rows = slice(h * HD, (h + 1) * HD)
                sync.dma_start(d["new_rwkv"][l, h], sz[rows, :, :, h * HD:(h + 1) * HD]).then_inc(stored, 16)
            sync.wait_ge(stored, 32)

        @block.tensor
        def _(pe):
            def hop(name, dr, t):
                bh = lambda c: g.proj[:, BH0 + 2 * dr + c, t * P:(t + 1) * P]
                kh = lambda c: g.proj[:, KH0 + 2 * dr + c, t * P:(t + 1) * P]
                if name == "pairs":
                    for src, banks in ((bh, (A, B)), (kh, (C, O))):
                        for c, h, rows in heads:
                            mm = pe.matmul(g.ps[:, banks[h], c * 2 * P:(c + 1) * 2 * P], src(c)[rows, :],
                                           ar[rows, dr, c, t, :, :], start=True, stop=True)
                elif name == "lower":
                    for c, h, rows in heads:
                        pe.matmul(g.ps[:, (A, B)[h], c * P:(c + 1) * P], ar[rows, dr, c, t, 0, :], bh(c)[rows, :],
                                  start=True, stop=True)
                    for i, src in enumerate((bh, kh)):
                        for c in range(CA):
                            mm = pe.transpose(g.ps[:, C, (2 * i + c) * P:(2 * i + c + 1) * P], src(c), g.ident)
                elif name.startswith("square") or name == "inverse":
                    n = 6 if name == "inverse" else int(name[6:])
                    for h in range(HA):
                        cols = slice(h * P, (h + 1) * P)
                        p0 = mb[:, h // 2, h % 2, 0, :] if n == 1 else pw[:, h, :]
                        p1 = pwt[:, h, :]
                        if n >= 2:
                            mm = pe.matmul(g.ps[:, C, cols], p1, x[:, h, :], start=True, stop=True)
                        if n <= 4:
                            mm = pe.matmul(g.ps[:, A, cols], p1, p0, start=True, stop=True)
                        if n <= 5:
                            mm = pe.matmul(g.ps[:, B, cols], p0, p1, start=True, stop=True)
                else:
                    i = int(name[-1])
                    hf = half(i, dr)
                    hs = slice(hf * HD, (hf + 1) * HD)
                    if name.startswith("rhs"):
                        for c in range(CA):
                            pe.matmul(g.ps[hs, A, c * P:(c + 1) * P], ar[:, dr, c, t, 0, hs], sz[:, dr, c, :],
                                      start=(c == 0), stop=False, skip_group_check=True)
                        for c, h, rows in heads:
                            at = c * P + h * HD
                            mm = pe.matmul(g.ps[hs, A, at:at + HD], mk[:, c, h, 0, hs], g.vtok[:, t, at:at + HD],
                                           start=False, stop=(c == CA - 1 and h == 1), skip_group_check=True)
                    elif name.startswith("sa"):
                        for c, h, rows in heads:
                            at = c * P + h * HD
                            mm = pe.matmul(g.ps[hs, B, at:at + HD], x[:, 2 * c + h, hs], rh[:, at:at + HD],
                                           start=(at == 0), stop=(c == CA - 1 and h == 1), skip_group_check=True)
                    else:
                        for c in range(CA):
                            cols = slice(c * P, (c + 1) * P)
                            pe.matmul(g.ps[:, C, cols], bt[hs, 0, cols], sa[hs, cols],
                                      start=(c == 0), stop=False, skip_group_check=True)
                            pe.matmul(g.ps[:, C, cols], bt[hs, 1, cols], g.vtok[hs, t, cols],
                                      start=False, stop=(c == CA - 1), skip_group_check=True)
                        for c in range(CA):
                            at = c * P + hf * HD
                            mm = pe.matmul(g.ps[:, O, at:at + HD], sz[:, dr, c, :], ar[:, dr, c, t, 1, hs],
                                           start=(i == 0 and c == 0), stop=False, skip_group_check=True)
                        if i == 1:
                            for c, h, rows in heads:
                                at = c * P + h * HD
                                for j, (lhs, m) in enumerate(((sa[:, at:at + HD], mb), (g.vtok[:, t, at:at + HD], mk))):
                                    mm = pe.matmul(g.ps[rows, O, c * P:(c + 1) * P], lhs, m[:, c, h, 1, :],
                                                   start=False, stop=(c == CA - 1 and j == 1), skip_group_check=True)
                mm.then_inc(ready, 1)

            def scores(u, c, S):
                h, t = UNITS[u]
                base = (h % 2) * HD + c * DK
                rows = slice(base, base + DK)
                q = g.proj[rows, Q0 + h // 2, t * P:(t + 1) * P]
                if t == TILES - 1:
                    mm = pe.matmul(g.ps[:, S, 0:P], q, g.proj[rows, B0 + h // 2, NS:NT], start=True, stop=True)
                else:
                    pe.matmul(g.ps[:, S, :], q, g.proj[rows, B0 + h // 2, 0:NS], start=True, stop=True)
                    mm = pe.matmul(g.ps[:, S + 1, 0:PAST], q, g.kctx[rows, h // 2, :], start=True, stop=True)
                mm.then_inc(s_ready, 1)

            def transpose(u, T):
                _, t = UNITS[u]
                pe.wait_ge(comb, u + 1)
                for k in range(nk(t) // P):
                    mm = pe.transpose(g.ps[:, T + k // 4, (k % 4) * P:(k % 4 + 1) * P], p[:, u % 2, 0, k * P:(k + 1) * P], g.ident)
                mm.then_inc(t_ready, 1)

            def values(u, S):
                h, t = UNITS[u]
                col = slice(256 + h * HD, 256 + (h + 1) * HD)
                pe.wait_ge(pt_ready, u + 1)
                base = (h % 2) * HD
                if t == TILES - 1:
                    vs = [g.vtok[:, t, col]]
                else:
                    vs = [g.vtok[:, k, col] for k in range(NS // P)] + [g.vctx[:, k, h * HD:(h + 1) * HD] for k in range(PAST // P)]
                for k, vk in enumerate(vs):
                    mm = pe.matmul(g.ps[base:base + HD, S + 1, (2 + u % 2) * P:(3 + u % 2) * P], vk, pt[:, u % 2, k * P:(k + 1) * P],
                                   start=(k == 0), stop=(k == len(vs) - 1), skip_group_check=True)
                mm.then_inc(o_ready, 1)

            pe.wait_ge(loaded, 64)
            nv = na = 0
            for slot, (step, dr, name, by) in enumerate(SLOTS):
                if nv:
                    pe.wait_ge(byv, nv)
                if na:
                    pe.wait_ge(bya, na)
                hop(name, dr, tile(step, dr))
                nv += "V" in by
                na += "A" in by
                for what, u, c in (attention_parts(slot - 2) if slot >= 2 else []):
                    if what == "scores":
                        pe.wait_ge(e_done, 2 * u + c + 1)
                    elif what == "transpose":
                        pe.wait_ge(pt_ready, u + 1)
                    elif what == "values":
                        pe.wait_ge(o_taken, u + 1)
                for what, u, c in attention_parts(slot):
                    if what == "scores":
                        scores(u, c, pair(slot))
                    elif what == "transpose":
                        transpose(u, pair(slot))
                    elif what == "values":
                        values(u, pair(slot))

        @block.scalar
        def _(act):
            for slot, (step, dr, name, by) in enumerate(SLOTS):
                if "A" in by:
                    act.wait_ge(ready, slot + 1)
                    if name == "lower":
                        dst, src = bt[:, :, :], g.ps[:, C, :]
                    else:
                        dst, src = pw[:, :, :], g.ps[:, A, :]
                    nc.scalar.activation(dst, src, ACT.Copy).then_inc(bya, 1)
                for what, u, c in attention_parts(slot):
                    _, t = UNITS[u]
                    if what == "scores":
                        act.wait_ge(m_ready, 2 * u + c + 1)
                        if u >= 2 and c == 0:
                            act.wait_ge(t_ready, u - 1)
                        nc.scalar.activation(p[:, u % 2, c, 0:nk(t)], g.flat[:, pair(slot) * 512:pair(slot) * 512 + nk(t)], ACT.Exp,
                                             bias=mx[:, u % 2, 2 + c:3 + c], scale=scale, accum_out=sm[:, u % 2, c:c + 1]).then_inc(e_done, 1)
                    elif what == "transpose":
                        act.wait_ge(t_ready, u + 1)
                        if u >= 2:
                            act.wait_ge(o_ready, u - 1)
                        nc.scalar.activation(pt[:, u % 2, 0:nk(t)], g.flat[:, pair(slot) * 512:pair(slot) * 512 + nk(t)], ACT.Copy).then_inc(pt_ready, 1)

        @block.vector
        def _(ve):
            o = Counter(ve, own)

            def take(step, dr, name):
                t = tile(step, dr)
                if name == "pairs":
                    for dst, banks in ((mb, (A, B)), (mk, (C, O))):
                        for h in range(2):
                            last = ve.tensor_tensor(dst[:, :, h, :, :].rearrange("p c a t -> p c (a t)"),
                                                    g.ps[:, banks[h], :].rearrange("p (c n) -> p c n", c=CA),
                                                    mask[:, dr, :].unsqueeze(1).broadcast_to([P, CA, 2 * P]), ALU.mult)
                    if step == TILES - 1:
                        last = ve.memset(sz[:, dr, :, :], 0.0)
                elif name == "lower":
                    for h in range(2):
                        ve.tensor_tensor(pwt[:, h::2, :], g.ps[:, (A, B)[h], 0:2 * P].rearrange("p (c n) -> p c n", c=CA),
                                         low[:, dr, :].unsqueeze(1).broadcast_to([P, CA, P]), ALU.mult)
                    last = ve.tensor_tensor(x[:, :, :], mb[:, :, :, 0, :].rearrange("p c h t -> p (c h) t"),
                                            g.ident.unsqueeze(1).broadcast_to([P, HA, P]), ALU.add)
                elif name.startswith("square") or name == "inverse":
                    if name != "inverse":
                        last = ve.tensor_copy(pwt[:, :, :], g.ps[:, B, :])
                    if name != "square1":
                        last = ve.tensor_tensor(x[:, :, :], x[:, :, :], g.ps[:, C, :].rearrange("p (h n) -> p h n", h=HA), ALU.add)
                else:
                    i = int(name[-1])
                    hf = half(i, dr)
                    hs = slice(hf * HD, (hf + 1) * HD)
                    if name.startswith("rhs"):
                        last = ve.tensor_copy(rh[hs, :], g.ps[hs, A, 0:CA * P])
                    elif name.startswith("sa"):
                        last = ve.tensor_copy(sa[hs, :], g.ps[hs, B, 0:CA * P])
                    else:
                        o.did(ve.tensor_tensor(szt[:, :, :], sz[:, dr, :, :],
                                               g.ps[:, C, 0:CA * P].rearrange("p (c n) -> p c n", c=CA), ALU.add))
                        if i == 1:
                            out = g.outT[:, 0:CA, t * P:(t + 1) * P]
                            o.did(ve.tensor_tensor(out, out, g.ps[:, O, 0:CA * P].rearrange("p (c n) -> p c n", c=CA), ALU.add))
                        o.wait()
                        ch = 2 * t + hf
                        for c in range(CA):
                            last = ve.scalar_tensor_tensor(sz[:, dr, c, :], szt[:, c, :], pc[:, dr, c, ch:ch + 1],
                                                           g.bones, ALU.mult, ALU.mult)
                return last

            def row_max(u, c, S):
                _, t = UNITS[u]
                ve.wait_ge(s_ready, 2 * u + c + 1)
                o.then(ve.tensor_reduce(mx[:, u % 2, c:c + 1], g.flat[:, S * 512:S * 512 + nk(t)], AX.X, ALU.max, negate=True))
                ve.tensor_scalar(mx[:, u % 2, 2 + c:3 + c], mx[:, u % 2, c:c + 1], scale, None, ALU.mult).then_inc(m_ready, 1)

            def combine(u):
                n = nk(UNITS[u][1])
                ve.wait_ge(e_done, 2 * u + 2)
                o.then(ve.reciprocal(sm[:, u % 2, 2:4], sm[:, u % 2, 0:2]))
                o.then(ve.tensor_scalar(p[:, u % 2, 1, 0:n], p[:, u % 2, 1, 0:n], sm[:, u % 2, 3:4], g.lam[:, 1:2], ALU.mult, ALU.mult))
                ve.scalar_tensor_tensor(p[:, u % 2, 0, 0:n], p[:, u % 2, 0, 0:n], sm[:, u % 2, 2:3], p[:, u % 2, 1, 0:n],
                                        ALU.mult, ALU.add).then_inc(comb, 1)

            def out(u, S):
                h, t = UNITS[u]
                base = (h % 2) * HD
                ve.wait_ge(o_ready, u + 1)
                if u + 2 < len(UNITS):
                    ve.wait_ge(s_ready, 2 * (u + 2) + 2)
                ve.tensor_copy(g.outT[base:base + HD, CA + h // 2, t * P:(t + 1) * P],
                               g.ps[base:base + HD, S + 1, (2 + u % 2) * P:(3 + u % 2) * P]).then_inc(o_taken, 1)

            ve.memset(sz[:, :, :, :], 0.0).then_inc(zeroed, 1)
            o.did(ve.memset(rh[:, :], 0.0))
            o.did(ve.memset(sa[:, :], 0.0))
            o.then(ve.memset(g.outT[:, 0:CA, :], 0.0))
            ve.wait_ge(loaded, 64)
            for slot, (step, dr, name, by) in enumerate(SLOTS):
                ve.wait_ge(ready, slot + 1)
                last = take(step, dr, name)
                last.then_inc(byv, 1)
                if step == TILES - 1 and name == "state1":
                    ve.wait_ge(byv, slot + 1)
                    ve.sem_inc(final, 2)
                for what, u, c in attention_parts(slot):
                    if what == "scores":
                        row_max(u, c, pair(slot))
                    elif what == "combine":
                        combine(u)
                    elif what == "values":
                        out(u, pair(slot))


def rwkv_finish(g, keep):
    nc, v = g.nc, g.v
    ar, gt, pc = keep
    sb_, ss, steps, sq, roots = (g.sem(f"rwkv_out_{x}") for x in ("bonus_in", "summed", "steps", "squared", "roots"))
    taken = g.sem("rwkv_out_taken")
    with ExitStack() as st, nc.Block() as block:
        bo = g.sb(st, "bo", [P, CA, NT])
        s2 = g.sb(st, "s2", [P, CA, NT])

        @block.tensor
        def _(pe):
            n = 0
            for src, sem in ((lambda c: bo[:, c, :], sb_), (lambda c: g.outT[:, c, :], None), (lambda c: s2[:, c, :], sq)):
                for c in range(CA):
                    if sem is not None:
                        pe.wait_ge(sem, c + 1)
                    if n >= 4:
                        pe.wait_ge(taken, n - 3)
                    for bank, (a, b) in enumerate(((0, NS), (NS, NT))):
                        mm = pe.matmul(g.ps[:, 2 * (n % 4) + bank, 0:b - a], g.bones, src(c)[:, a:b], start=True, stop=True)
                    mm.then_inc(ss, 1)
                    n += 1

        @block.scalar
        def _(act):
            for c in range(CA):
                act.wait_ge(taken, 3 + c)
                nc.scalar.activation(s2[:, c, :], g.outT[:, c, :], ACT.Square).then_inc(sq, 1)
            for c in range(CA):
                act.wait_ge(taken, 5 + c)
                nc.scalar.activation(s2[:, c, :], s2[:, c, :], ACT.Sqrt).then_inc(roots, 1)

        @block.vector
        def _(ve):
            k = Counter(ve, steps)
            flat = lambda n: g.flat[:, 1024 * (n % 4):1024 * (n % 4) + NT]
            for c in range(CA):
                ve.scalar_tensor_tensor(bo[:, c, :], g.proj[:, R0 + c, :], v("rk", c, c + 1), g.proj[:, K0 + c, :],
                                        ALU.mult, ALU.mult).then_inc(sb_, 1)
            for c in range(CA):
                ve.wait_ge(ss, c + 1)
                ve.tensor_tensor(bo[:, c, :], flat(c), g.proj[:, V0 + c, :], ALU.mult).then_inc(taken, 1)
            for c in range(CA):
                ve.wait_ge(ss, 3 + c)
                ve.scalar_tensor_tensor(g.outT[:, c, :], flat(2 + c), -1.0 / HD, g.outT[:, c, :], ALU.mult, ALU.add).then_inc(taken, 1)
            for c in range(CA):
                ve.wait_ge(ss, 5 + c)
                ve.tensor_scalar(s2[:, c, :], flat(4 + c), 1.0 / HD, GN_EPS, ALU.mult, ALU.add).then_inc(taken, 1)
            for c in range(CA):
                ve.wait_ge(roots, c + 1)
                k.then(ve.reciprocal(s2[:, c, :], s2[:, c, :]))
                k.then(ve.scalar_tensor_tensor(g.outT[:, c, :], g.outT[:, c, :], v("lng", c, c + 1), s2[:, c, :], ALU.mult, ALU.mult))
                k.then(ve.tensor_tensor(g.outT[:, c, :], g.outT[:, c, :], bo[:, c, :], ALU.add))
                k.did(ve.tensor_tensor(g.outT[:, c, :], g.outT[:, c, :], gt[:, c, :], ALU.mult))


def residual_take(g, part):
    def take(ve, oc, sums):
        for a, b in ((0, H2), (H2, NS), (NS, NT)):
            c, h = int(a >= NS), a // H2
            x = g.xT[:, bass.ds(oc, 1), a:b]
            i = ve.scalar_tensor_tensor(x, sums[:, h:h + 1, a - h * H2:b - h * H2], g.modT[:, bass.ds(part * KC + oc, 1), c], x,
                                        ALU.mult, ALU.add)
        return i
    return take


def select_stage(g, l, qT, sel):
    nc, d = g.nc, g.dram
    loaded, sc_ready, sc_taken, steps = (g.sem(f"sel_{x}") for x in ("keys_loaded", "scores_ready", "scores_taken", "steps"))
    dif, ex, out_ready, tr, tr_tk = (g.sem(f"sel_{x}") for x in ("differences", "exps", "selected", "transposed", "transposes_taken"))
    lists = g.sem("sel_lists_done")
    NC = 2 * PH
    TAIL = P - TOPK // 2
    MT = -(-NM // (TILES - 1))
    with ExitStack() as st, nc.Block() as block:
        mod = Modulation(g, st, lambda i: d["mod_w"][l, i])
        kt = g.sb(st, "kt", [P, NC, P])
        s = g.sb(st, "s", [P, NC, NKEY])
        s2 = g.sb(st, "s2", [P, NC, NKEY])
        v16 = g.sb(st, "v16", [P, NC, TOPK])
        i16 = g.sb(st, "i16", [P, NC, TOPK], U32)
        if16 = g.sb(st, "if16", [P, NC, TOPK])
        top = g.sb(st, "top", [P, PH, TOPK])
        pos = g.sb(st, "pos", [P, PH, TOPK], U32)
        hi = g.sb(st, "hi", [P, 2, PH, TOPK], U32)
        hif = g.sb(st, "hif", [P, 2, PH, TOPK])
        late = g.sb(st, "late", [P, 3, PH, TOPK])
        oh = g.sb(st, "oh", [P, 2, PH, TOPK, TOPK])
        cand, c2 = s2[:, 0:PH, :], s2[:, PH:NC, :]
        res = g.sb(st, "res", [P, 3, PH, TOPK])
        sm = g.sb(st, "sm", [P, 2, PH])

        def pieces(t):
            return min(t * MT, NM), min((t + 1) * MT, NM)

        @block.sync
        def _(sync):
            sync.dma_start(kt[:, :, :], d["peer_keys"][l]).then_inc(loaded, 16)
            mod.load(sync)

        @block.tensor
        def _(pe):
            pe.wait_ge(loaded, 16)
            for t in range(TILES + 1):
                if t < TILES:
                    if t >= 1:
                        pe.wait_ge(sc_taken, t)
                    for i in range(NC):
                        mm = pe.matmul(g.flat[:, i * P:(i + 1) * P], qT[:, i, t * P:(t + 1) * P], kt[:, i, :], start=True, stop=True)
                    mm.then_inc(sc_ready, 1)
                if t >= 1:
                    pe.wait_ge(out_ready, t)
                    if t >= 2:
                        pe.wait_ge(tr_tk, t - 1)
                    for j in range(3):
                        mm = pe.transpose(g.ps[:, 4, j * P:(j + 1) * P], res[:, j, :, :].rearrange("p h k -> p (h k)"), g.ident)
                    mm.then_inc(tr, 1)
                mod.on_tensor(pe, *pieces(t))

        @block.scalar
        def _(act):
            def scores(t):
                act.wait_ge(sc_ready, t + 1)
                if t >= 1:
                    act.wait_ge(lists, t)
                nc.scalar.activation(s[:, :, :], g.flat[:, 0:NC * P], ACT.Copy).then_inc(sc_taken, 1)

            scores(0)
            for t in range(TILES):
                mod.on_scalar(act, *pieces(t))
                if t + 1 < TILES:
                    scores(t + 1)
                act.wait_ge(dif, t + 1)
                nc.scalar.activation(res[:, 2, :, :], res[:, 2, :, :], ACT.Exp).then_inc(ex, 1)
                act.wait_ge(tr, t + 1)
                nc.scalar.activation(sel[:, :, t * P:(t + 1) * P], g.ps[:, 4, 0:3 * P], ACT.Copy).then_inc(tr_tk, 1)

        @block.vector
        def _(ve):
            k = Counter(ve, steps)

            def top16(n, values, scratch, best, index):
                for i in range(n):
                    k.did(ve.max(best[:, i, 0:8], values[:, i, :]))
                k.wait()
                for i in range(n):
                    k.did(ve.match_replace(scratch[:, i, :], best[:, i, 0:8], values[:, i, :], NEG))
                    k.did(ve.max_index(index[:, i, 0:8], best[:, i, 0:8], values[:, i, :]))
                k.wait()
                for i in range(n):
                    k.did(ve.max(best[:, i, 8:16], scratch[:, i, :]))
                k.wait()
                for i in range(n):
                    k.did(ve.max_index(index[:, i, 8:16], best[:, i, 8:16], scratch[:, i, :]))
                k.wait()

            both = v16[:, :, :].rearrange("p (h c) k -> p h c k", c=2)
            ids = if16[:, :, :].rearrange("p (h c) k -> p h c k", c=2)
            iota16 = g.iota[:, 0:TOPK].unsqueeze(1).broadcast_to([P, PH * TOPK, TOPK])
            for t in range(TILES):
                ve.wait_ge(sc_taken, t + 1)
                top16(NC, s, s2, v16, i16)
                ve.sem_inc(lists, 1)
                for out, a, b in ((slice(0, 7 * TOPK), slice(0, 7), slice(0, TOPK)),
                                  (slice(7 * TOPK, TAIL), slice(7, 8), slice(0, P - TAIL)),
                                  (slice(TAIL, P), slice(8, TOPK), slice(0, 1))):
                    dims = [P, PH, a.stop - a.start, b.stop - b.start]
                    k.did(ve.tensor_tensor(cand[:, :, out].rearrange("p h (a b) -> p h a b", b=dims[3]),
                                           both[:, :, 0, a].unsqueeze(3).broadcast_to(dims),
                                           both[:, :, 1, b].unsqueeze(2).broadcast_to(dims), ALU.add))
                k.did(ve.tensor_copy(if16[:, :, :], i16[:, :, :]))
                k.wait()
                top16(PH, cand, c2, top, pos)
                k.did(ve.tensor_scalar(hi[:, 0, :, :], pos[:, :, :], 4, None, ALU.logical_shift_right))
                k.did(ve.tensor_scalar(hi[:, 1, :, :], pos[:, :, :], TOPK - 1, None, ALU.bitwise_and))
                k.did(ve.tensor_copy(late[:, 0, :, :], pos[:, :, :]))
                if t >= 1:
                    ve.wait_ge(tr, t)
                ve.tensor_tensor(res[:, 2, :, :], top[:, :, :], top[:, :, 0:1].broadcast_to([P, PH, TOPK]), ALU.subtract).then_inc(dif, 1)
                k.wait()
                k.did(ve.tensor_copy(hif[:, :, :, :], hi[:, :, :, :]))
                k.did(ve.tensor_scalar(late[:, 1, :, :], late[:, 0, :, :], float(TAIL), None, ALU.is_ge))
                k.wait()
                k.did(ve.tensor_tensor(late[:, 0, :, :], late[:, 1, :, :], hif[:, 1, :, :], ALU.mult))
                k.did(ve.scalar_tensor_tensor(late[:, 2, :, :], hif[:, 1, :, :], -7.0, late[:, 1, :, :], ALU.add, ALU.mult))
                k.wait()
                k.did(ve.tensor_tensor(hif[:, 0, :, :], hif[:, 0, :, :], late[:, 2, :, :], ALU.add))
                k.did(ve.tensor_tensor(hif[:, 1, :, :], hif[:, 1, :, :], late[:, 0, :, :], ALU.subtract))
                k.wait()
                for c in range(2):
                    rank = hif[:, c, :, :].rearrange("p h k -> p (h k)").unsqueeze(2).broadcast_to([P, PH * TOPK, TOPK])
                    k.did(ve.tensor_tensor(oh[:, c, :, :, :].rearrange("p h k m -> p (h k) m"), rank, iota16, ALU.is_equal))
                k.wait()
                for c in range(2):
                    k.did(ve.tensor_tensor(oh[:, c, :, :, :], oh[:, c, :, :, :],
                                           ids[:, :, c, :].unsqueeze(2).broadcast_to([P, PH, TOPK, TOPK]), ALU.mult))
                ve.wait_ge(ex, t + 1)
                k.did(ve.tensor_reduce(sm[:, 0, :], res[:, 2, :, :], AX.X, ALU.add))
                k.wait()
                k.did(ve.tensor_reduce(res[:, 0:2, :, :], oh[:, :, :, :, :], AX.X, ALU.add))
                k.then(ve.reciprocal(sm[:, 1, :], sm[:, 0, :]))
                ve.tensor_tensor(res[:, 2, :, :], res[:, 2, :, :], sm[:, 1, :].unsqueeze(2).broadcast_to([P, PH, TOPK]),
                                 ALU.mult).then_inc(out_ready, 1)


GT_N = 64
TG = NT // GT_N
GB = 2
NG = NKEY // GB
H2 = NT // 2
OCT = 16
OP = 8 * 512 // (OCT * P)
PARTS = 3


def gates_stage(g, l, sel):
    nc, d = g.nc, g.dram
    b_ready, a_ready, mm_ready, taken = (g.sem(f"gate_{x}") for x in ("b_onehots", "a_onehots", "products", "taken"))
    a_eq, steps = g.sem("gate_a_equal"), g.sem("gate_steps")
    store = [g.sem(f"gate_stored{i}") for i in range(2)]
    with ExitStack() as st, nc.Block() as block:
        iota = g.sb(st, "iota_tokens", [P, NKEY, OCT], BF16)
        s16 = g.sb(st, "sel16", [P, 2 + PARTS, NT], BF16)
        rest = g.sb(st, "rest", [P, 2, NT])
        ea = g.sb(st, "ea", [P, 2, NKEY, OCT], BF16)
        oa = g.sb(st, "oa", [P, 2, PARTS, NKEY, OCT], BF16)
        ob = g.sb(st, "ob", [P, 2, NKEY, OCT], BF16)
        stage = g.sb(st, "stage", [P, 2, NKEY, GT_N])
        NO = GT_N // OCT

        def turns(eng, body):
            with eng.Fori(0, TG // 2) as i:
                for q in range(2):
                    body(i * 2 + q, q, i)

        @block.vector
        def _(ve):
            k = Counter(ve, steps)
            k.did(ve.tensor_copy(iota[:, :, :], g.iota.unsqueeze(2).broadcast_to([P, NKEY, OCT])))
            k.did(ve.tensor_copy(s16[:, 0:3, :], sel[:, :, :]))
            k.wait()
            for i in range(1, PARTS):
                last = sel[:, 2, :] if i == 1 else rest[:, 0, :]
                k.then(ve.tensor_tensor(rest[:, i - 1, :], last, s16[:, 1 + i, :], ALU.subtract))
                k.then(ve.tensor_copy(s16[:, 2 + i, :], rest[:, i - 1, :]))
            ve.sem_inc(mm_ready, 2)

            def tile(t, q, i):
                def col(j, o):
                    return s16[:, j, bass.ds(t * GT_N + o * OCT, OCT)].unsqueeze(1).broadcast_to([P, NKEY, OCT])

                for o in range(NO):
                    ve.wait_ge(mm_ready, t * NO + (o + 1))
                    ve.tensor_tensor(ea[:, o % 2, :, :], iota[:, :, :], col(0, o), ALU.is_equal).then_inc(a_eq, 1)
                    ve.tensor_tensor(ob[:, o % 2, :, :], iota[:, :, :], col(1, o), ALU.is_equal).then_inc(b_ready, 1)
                    ve.wait_ge(a_eq, t * NO + (o + 1))
                    for part in range(PARTS):
                        last = ve.tensor_tensor(oa[:, o % 2, part, :, :], ea[:, o % 2, :, :], col(2 + part, o), ALU.mult)
                    last.then_inc(a_ready, 1)

            turns(ve, tile)

        @block.tensor
        def _(pe):
            def tile(t, q, i):
                for o in range(NO):
                    pe.wait_ge(a_ready, t * NO + (o + 1))
                    pe.wait_ge(b_ready, t * NO + (o + 1))
                    pe.wait_ge(taken, t * NO + (o + 1))
                    for n in range(OCT):
                        at = OCT * P * (o % OP) + n * P
                        for part in reversed(range(PARTS)):
                            mm = pe.matmul(g.flat[:, at:at + P], oa[:, o % 2, part, :, n], ob[:, o % 2, :, n],
                                           start=(part == PARTS - 1), stop=(part == 0))
                    mm.then_inc(mm_ready, 1)

            turns(pe, tile)

        @block.scalar
        def _(act):
            act.sem_inc(taken, OP)
            act.sem_inc(store[0], 16)
            act.sem_inc(store[1], 16)

            def tile(t, q, i):
                act.wait_ge(store[q], i * 16 + 16)
                for o in range(NO):
                    act.wait_ge(mm_ready, t * NO + (o + 3))
                    at = OCT * P * (o % OP)
                    nc.scalar.activation(stage[:, q, :, o * OCT:(o + 1) * OCT],
                                         g.flat[:, at:at + OCT * P].rearrange("p (n b) -> p b n", n=OCT), ACT.Copy).then_inc(taken, 1)

            turns(act, tile)

        @block.sync
        def _(sync):
            def tile(t, q, i):
                sync.wait_ge(taken, t * NO + (NO + OP))
                sync.dma_start(d["gates"][:, :, bass.ds(t, 1), :],
                               stage[:, q, :, :].rearrange("p (g b) n -> p g (b n)", b=GB).unsqueeze(2)).then_inc(store[q], 16)

            turns(sync, tile)
            sync.wait_ge(store[0], 16 * (TG // 2 + 1))
            sync.wait_ge(store[1], 16 * (TG // 2 + 1))


def experts_stage(g, l, acc):
    nc, d = g.nc, g.dram
    T = 2
    B = T * GB
    YN = 2 * TILES
    u_in = [g.sem(f"u_loaded{i}") for i in range(B)]
    v_in = [g.sem(f"v_loaded{i}") for i in range(B)]
    g_in = [g.sem(f"g_loaded{i}") for i in range(T)]
    u_hi, u_lo, v_hi, v_lo = (g.sem(f"exp_{x}") for x in ("u_high", "u_low", "v_high", "v_low"))
    h_ready, h_taken, weighed, w_hi, w_lo, y_ready, y_taken = (
        g.sem(f"exp_{x}") for x in ("h_ready", "h_taken", "weighed", "w_high", "w_low", "y_ready", "y_taken"))
    with ExitStack() as st, nc.Block() as block:
        u = g.sb(st, "u", [P, B, KC, P])
        v = g.sb(st, "v", [P, B, D])
        gw = g.sb(st, "gw", [P, T, TG, GB, GT_N])
        hh = g.sb(st, "hh", [P, 2, NT])
        u2 = [g.sb(st, f"u{x}", [P, 2, KC, P], F32R) for x in ("hi", "lo")]
        v2 = [g.sb(st, f"v{x}", [P, B, D], F32R) for x in ("hi", "lo")]
        w2 = [g.sb(st, f"w{x}", [P, B, NT], F32R) for x in ("hi", "lo")]
        LAST = NG // T - 1

        def turns(eng, turn):
            with eng.Fori(0, LAST) as i:
                turn(i, False)
            turn(LAST, True)

        @block.sync
        def _(sync):
            sync.sem_inc(u_lo, B)
            sync.sem_inc(v_lo, B)
            sync.sem_inc(weighed, B)
            with sync.Fori(0, NG // T) as i:
                for j in range(B):
                    if j % GB == 0:
                        q = j // GB
                        sync.wait_ge(weighed, i * B + (q + 1) * GB)
                        sync.dma_start(gw[:, q, :, :, :].rearrange("p t b n -> p (t b n)"),
                                       d["gates"][:, bass.ds(i * T + q, 1), :, :].rearrange("p g t m -> p (g t m)")).then_inc(g_in[q], 16)
                    sync.wait_ge(u_lo, i * B + (j + 1))
                    sync.dma_start(u[:, j, :, :], d["peer_u"][l, i * B + j]).then_inc(u_in[j], 16)
                    sync.wait_ge(v_lo, i * B + (j + 1))
                    sync.dma_start(v[:, j, :], d["peer_v"][l, :, bass.ds((i * B + j) * D, D)]).then_inc(v_in[j], 16)

        @block.tensor
        def _(pe):
            def hidden(i, q):
                for j in range(q * GB, (q + 1) * GB):
                    pe.wait_ge(u_lo, i * B + (j + 1 + B))
                    pe.wait_ge(h_taken, i * B + (j + 1))
                    for h in range(2):
                        for kc in range(KC):
                            mm = split3(pe, g.ps[:, 2 * (j % 2) + h, 0:H2], [x[:, j % 2, kc, :] for x in u2],
                                        [x[:, kc, h * H2:(h + 1) * H2] for x in g.h2], start=(kc == 0), stop=(kc == KC - 1))
                    mm.then_inc(h_ready, 1)

            def output(i, q):
                pe.wait_ge(v_lo, i * B + ((q + 1) * GB + B))
                pe.wait_ge(w_lo, i * B + ((q + 1) * GB + 2))
                for n in range(YN):
                    t, half = divmod(n, 2)
                    m = q * YN + n
                    pe.wait_ge(y_taken, i * (T * YN) + (m + 1))
                    for b in range(GB):
                        j = q * GB + b
                        mm = split3(pe, g.ps[:, 4 + m % 4, :], [x[:, j, t * P:(t + 1) * P] for x in w2],
                                    [x[:, j, half * 512:(half + 1) * 512] for x in v2], start=(b == 0), stop=(b == GB - 1))
                    mm.then_inc(y_ready, 1)

            def turn(i, last):
                hidden(i, 1)
                output(i, 0)
                if not last:
                    hidden(i + 1, 0)
                output(i, 1)

            hidden(0, 0)
            turns(pe, turn)

        @block.scalar
        def _(act):
            act.sem_inc(h_taken, 2)
            act.sem_inc(h_ready, 2)
            act.sem_inc(y_ready, T * YN)

            def u_high(i, j):
                i, j = i + j // B, j % B
                act.wait_ge(u_in[j], i * 16 + 16)
                act.wait_ge(h_ready, i * B + (j + 1))
                nc.scalar.activation(u2[0][:, j % 2, :, :], u[:, j, :, :], ACT.Copy).then_inc(u_hi, 1)

            def v_high(i, q):
                i, q = i + q // T, q % T
                act.wait_ge(y_ready, i * (T * YN) + (q + 1) * YN)
                for j in range(q * GB, (q + 1) * GB):
                    act.wait_ge(v_in[j], i * 16 + 16)
                    nc.scalar.activation(v2[0][:, j, :], v[:, j, :], ACT.Copy).then_inc(v_hi, 1)

            def group(i, q, last, u_ahead=True):
                for b in range(GB):
                    j = q * GB + b
                    act.wait_ge(h_ready, i * B + (j + 1 + 2))
                    act.wait_ge(w_lo, i * B + (j + 1))
                    nc.scalar.activation(halves(hh[:, j % 2, :]), g.ps[:, 2 * (j % 2):2 * (j % 2) + 2, 0:H2], ACT.Gelu).then_inc(h_taken, 1)
                    if not (last and j + 2 >= B):
                        u_high(i, j + 2)
                    act.wait_ge(weighed, i * B + (j + 1 + B))
                    act.wait_ge(y_ready, i * (T * YN) + (q + 1) * YN)
                    nc.scalar.activation(w2[0][:, j, :], hh[:, j % 2, :], ACT.Copy).then_inc(w_hi, 1)

            def turn(i, last):
                group(i, 1, last)
                if not last:
                    v_high(i, 2)
                    group(i + 1, 0, False)
                    v_high(i, 3)

            u_high(0, 0)
            u_high(0, 1)
            v_high(0, 0)
            group(0, 0, False)
            v_high(0, 1)
            turns(act, turn)

        @block.vector
        def _(ve):
            ve.memset(acc[:, :, :], 0.0).then_inc(y_taken, 4)
            ve.wait_ge(y_taken, 4)
            ve.sem_inc(w_lo, 2)

            def u_low(i, j):
                i, j = i + j // B, j % B
                ve.wait_ge(u_hi, i * B + (j + 1))
                ve.tensor_tensor(u2[1][:, j % 2, :, :], u[:, j, :, :], u2[0][:, j % 2, :, :].bitcast(F32), ALU.subtract).then_inc(u_lo, 1)

            def v_low(i, q):
                i, q = i + q // T, q % T
                for j in range(q * GB, (q + 1) * GB):
                    ve.wait_ge(v_hi, i * B + (j + 1))
                    ve.tensor_tensor(v2[1][:, j, :], v[:, j, :], v2[0][:, j, :].bitcast(F32), ALU.subtract).then_inc(v_lo, 1)

            def group(i, q, last):
                ve.wait_ge(g_in[q], i * 16 + 16)
                for b in range(GB):
                    j = q * GB + b
                    ve.wait_ge(h_taken, i * B + (j + 1 + 2))
                    h = hh[:, j % 2, :].rearrange("p (t n) -> p t n", n=GT_N)
                    ve.tensor_tensor(h, gw[:, q, :, b, :], h, ALU.mult).then_inc(weighed, 1)
                    if not (last and j + 2 >= B):
                        u_low(i, j + 2)
                    ve.wait_ge(w_hi, i * B + (j + 1))
                    ve.tensor_tensor(w2[1][:, j, :], hh[:, j % 2, :], w2[0][:, j, :].bitcast(F32), ALU.subtract).then_inc(w_lo, 1)

            def take(i, q):
                for n in range(YN):
                    t, half = divmod(n, 2)
                    m = q * YN + n
                    ve.wait_ge(y_ready, i * (T * YN) + (m + 1 + T * YN))
                    a = acc[:, t, half * 512:(half + 1) * 512]
                    ve.tensor_tensor(a, a, g.ps[:, 4 + m % 4, :], ALU.add).then_inc(y_taken, 1)

            def turn(i, last):
                group(i, 1, last)
                take(i, 0)
                if not last:
                    v_low(i, 2)
                    group(i + 1, 0, False)
                take(i, 1)
                if not last:
                    v_low(i, 3)

            u_low(0, 0)
            u_low(0, 1)
            v_low(0, 0)
            group(0, 0, False)
            v_low(0, 1)
            turns(ve, turn)


def fold_stage(g, acc):
    nc = g.nc
    tr, tk = g.sem("fold_transposed"), g.sem("fold_taken")
    with nc.Block() as block:
        @block.tensor
        def _(pe):
            for t in range(TILES):
                if t >= 4:
                    pe.wait_ge(tk, t - 3)
                for kc in range(KC):
                    at = 1024 * (t % 4) + kc * P
                    mm = pe.transpose(g.flat[:, at:at + P], acc[:, t, kc * P:(kc + 1) * P], g.ident)
                mm.then_inc(tr, 1)

        @block.vector
        def _(ve):
            for t in range(TILES):
                ve.wait_ge(tr, t + 1)
                c = int(t == TILES - 1)
                for kc in range(KC):
                    at = 1024 * (t % 4) + kc * P
                    x = g.xT[:, kc, t * P:(t + 1) * P]
                    i = ve.scalar_tensor_tensor(x, g.flat[:, at:at + P], g.modT[:, 5 * KC + kc, c:c + 1], x, ALU.mult, ALU.add)
                i.then_inc(tk, 1)


def build(nc, dram, upto=99):
    ctx = ExitStack()
    with ctx:
        g = Program(nc, ctx, dram)
        g.ps = ctx.enter_context(nc.psum_tensor("ps", [P, 8, 512], F32))
        g.flat = g.ps[:, :, :].rearrange("p b n -> p (b n)")
        g.xT = g.sb(ctx, "xT", [P, KC, NT])
        g.keep = g.sb(ctx, "keep", [P, NKEEP])
        g.ident, g.ones, g.bones, g.iota = (g.keep[:, i * P:(i + 1) * P] for i in range(4))
        g.vec = g.sb(ctx, "vec", [P, NVEC])
        g.cond = g.sb(ctx, "cond", [P, KC, 2])
        g.scond = g.sb(ctx, "scond", [P, KC, 2])
        g.tiny = g.sb(ctx, "tiny", [P, 8 + DK])
        g.lam = g.sb(ctx, "lam", [P, 4])
        g.omka = g.sb(ctx, "omka", [P, 2])
        g.nsp = g.sb(ctx, "nsp", [P, 4])
        g.nsp2 = g.sb(ctx, "nsp2", [P, 4])
        g.modT = g.sb(ctx, "modT", [P, 6 * KC, 2])
        g.modN = g.sb(ctx, "modN", [P, 6 * KC, 2])
        g.gain = g.sb(ctx, "gain", [P, 2, KC, 2])
        y_out = ctx.enter_context(nc.semaphore("y_stored"))

        g.begin()
        first_mod_stage(g)
        g.end()

        with nc.Fori(0, DEPTH) as l:
            g.begin()
            load_stage(g, l)
            mod_stage(g)
            with ExitStack() as s1:
                g.proj = g.sb(s1, "proj", [P, NPROJ + 1, NT])
                g.vtok = g.sb(s1, "vtok", [P, TILES, VTOK])
                with ExitStack() as s2:
                    g.h2 = [g.sb(s2, f"h{x}", [P, KC, NT], F32R) for x in ("hi", "lo")]
                    norm_stage(g, "norm1", g.h2[0], lambda kc, c: g.gain[:, 0, kc, c:c + 1], lambda kc, c: g.modT[:, kc, c:c + 1],
                               low=g.h2[1])
                    proj_stage(g, l)
                g.outT = g.sb(s1, "outT", [P, KC, NT])
                with ExitStack() as s2:
                    g.kctx = g.sb(s2, "kctx", [P, CB, PAST])
                    g.vctx = g.sb(s2, "vctx", [P, PAST // P, 512])
                    keep = (g.sb(s2, "ar", [P, 2, CA, TILES, 2, P]), g.sb(s2, "gt", [P, CA, NT]), g.sb(s2, "pc", [P, 2, CA, NT // CH]))
                    rope_stage(g, l)
                    lru_stage(g, l)
                    rwkv_prepare(g, l, keep)
                    mix_stage(g, l, keep)
                    subln_stage(g)
                    rwkv_finish(g, keep)
                with ExitStack() as s2:
                    out2 = [g.sb(s2, f"out{x}", [P, KC, NT], F32R) for x in ("hi", "lo")]
                    split_stage(g, "out", g.outT, *out2)
                    gemm(g, "wout", lambda oc: dram["w_out"][l, oc], KC, 4, 2, out2, residual_take(g, 2))
            g.end()
            g.begin()
            with ExitStack() as s1:
                g.h2 = [g.sb(s1, f"h{x}", [P, KC, NT], F32R) for x in ("hi", "lo")]
                norm_stage(g, "norm2", g.h2[0], lambda kc, c: g.gain[:, 1, kc, c:c + 1], lambda kc, c: g.modT[:, 3 * KC + kc, c:c + 1],
                           low=g.h2[1])
                with ExitStack() as s2:
                    sel = g.sb(s2, "sel", [P, 3, NT])
                    with ExitStack() as s3:
                        qT = g.sb(s3, "qT", [P, 2 * PH, NT])
                        gemm(g, "query", lambda oc: dram["peer_wq"][l, oc], 2 * PH, 4, 2, g.h2,
                             lambda ve, oc, sums: ve.tensor_copy(qT[:, bass.ds(oc, 1), :].rearrange("p o (h n) -> p (o h) n", n=H2), sums))
                        select_stage(g, l, qT, sel)
                    gates_stage(g, l, sel)
                acc = g.sb(s1, "acc", [P, TILES, D])
                experts_stage(g, l, acc)
                fold_stage(g, acc)
            g.end()

        g.begin()
        with ExitStack() as s1:
            out = g.sb(s1, "out", [P, KC, NT])
            norm_stage(g, "final", out, lambda kc, c: g.v("final", kc, kc + 1), None)
            with nc.Block() as block:
                @block.sync
                def _(sync):
                    sync.dma_start(dram["y"], out[:, :, :]).then_inc(y_out, 16)
                    sync.wait_ge(y_out, 16)


def constants():
    i = np.arange(P)
    same = (i[:, None] // CH) == (i[None, :] // CH)
    s, t = i[:, None], i[None, :]
    perm = np.zeros((P, P))
    for m in range(0, P, 2):
        perm[m + 1, m] = -1.0
        perm[m, m + 1] = 1.0
    tok = np.arange(NS)
    row, col = (tok // GRID_W).astype(np.float32), (tok % GRID_W).astype(np.float32)
    pairs = DK // 4
    inv = (np.float32(10000.0) ** (-np.arange(pairs, dtype=np.float32) / np.float32(pairs))).astype(np.float32)
    ang = np.concatenate([row[:, None] * inv, col[:, None] * inv], axis=-1).astype(np.float32)
    pair = (i % DK) // 2
    n = np.arange(NT)
    parts = {
        "ident": np.eye(P), "ones": np.ones((P, P)), "bones": same, "iota": np.broadcast_to(i, (P, P)), "perm": perm,
        "maskF": np.concatenate([same & (s < t), same & (s <= t)], 1),
        "maskB": np.concatenate([same & (s > t), same & (s >= t)], 1),
        "lowF": same & (t < s), "lowB": same & (t > s),
        "scanF": np.broadcast_to(n % CH != 0, (P, NT)), "scanB": np.broadcast_to(n % CH != CH - 1, (P, NT)),
        "cos": np.cos(ang).T[pair], "sin": np.sin(ang).T[pair],
    }
    return np.concatenate([np.asarray(parts[k], np.float32) for k in CI], axis=1)


def kernel(**inputs):
    import concourse.bacc as bacc
    from concourse.bass_utils import run_bass_kernel_spmd

    w = {k: np.asarray(x) for k, x in inputs.items()}
    L = DEPTH

    def chunks(x):
        n = x.shape[-1] // P
        return x.reshape(L, x.shape[1] // P, P, n, P).transpose(0, 3, 2, 1, 4)

    def vec(x):
        return x.reshape(L, -1, P).transpose(0, 2, 1)

    wi = w["w_in"]
    va, vb = wi[:, :, 512:768], wi[:, :, 768 + 1024:768 + 1536]
    lora = [w[k].transpose(0, 2, 1, 3).reshape(L, D, P) for k in ("rwkv_wA", "rwkv_aA")]
    w_proj = np.concatenate([wi[:, :, 0:768 + 1024], wi[:, :, 768 + 1536:], *lora, w["rwkv_gA"]], axis=2)
    lam_init = np.array([0.8 - 0.6 * np.exp(-0.3 * l) for l in range(L)], np.float32)
    cols = {
        "mod_b": vec(w["mod_b"]), "n1": vec(w["norm1_g"]), "n2": vec(w["norm2_g"]),
        "w0": vec(w["rwkv_w0"].reshape(L, -1)), "a0": vec(w["rwkv_a0"].reshape(L, -1)),
        "kk": vec(w["rwkv_kk"]), "ka": vec(w["rwkv_ka"]), "rk": vec(w["rwkv_rk"].reshape(L, -1)),
        "lng": vec(w["rwkv_ln_g"]), "sub": np.concatenate([w["diff_subln_g"]] * 2, 1)[:, :, None],
        "convw": vec(w["lru_conv_w"].reshape(L, -1)), "convb": vec(w["lru_conv_b"]),
        "ba": vec(w["lru_ba"].reshape(L, -1)), "bx": vec(w["lru_bx"].reshape(L, -1)), "lam": vec(w["lru_lambda"].reshape(L, -1)),
        "lq": np.broadcast_to(np.concatenate([w[f"diff_{n}"] for n in ("lq1", "lk1", "lq2", "lk2")], 1)[:, None, :], (L, P, 4 * DK)),
        "laminit": np.broadcast_to(lam_init[:, None, None], (L, P, 1)),
        "final": np.broadcast_to(w["final_norm_g"].reshape(1, KC, P).transpose(0, 2, 1), (L, P, KC)),
        "h0": vec(w["state_lru"][0].reshape(L, -1)),
    }
    x = np.concatenate([w["x_sample"][0], w["x_prompt"][0]], 0)
    lru = np.stack([w["lru_wa"], w["lru_wx"]], 1).reshape(L, 2, 2, CC, 2, HD, HD)
    arrays = {
        "consts": constants(),
        "vecs": np.concatenate([cols[k] for k in VI], axis=2),
        "x": x.T.reshape(KC, P, NT).transpose(1, 0, 2),
        "cond": np.stack([w["c"][0], w["c_ctx"]], 1).reshape(KC, P, 2).transpose(1, 0, 2),
        "mod_w": np.roll(w["mod_w"], -1, axis=0).reshape(L, KC, P, NM, MP).transpose(0, 3, 2, 1, 4),
        "w_proj": chunks(w_proj),
        "w_v": np.concatenate([va, vb], 2).reshape(L, KC, P, VTOK).transpose(0, 2, 1, 3),
        "w_out": chunks(w["w_out"]),
        "cache_k": w["cache_k"][0].transpose(0, 1, 3, 2).reshape(L, CB, P, PAST).transpose(0, 2, 1, 3),
        "cache_v": w["cache_v"][0].transpose(0, 2, 1, 3).reshape(L, PAST // P, P, HB * HD).transpose(0, 2, 1, 3),
        "state_rwkv": w["state_rwkv"][0].reshape(L, 2, CA, 2, HD, HD).transpose(0, 3, 5, 1, 2, 4),
        "rwkv_B": np.stack([w["rwkv_wB"].reshape(L, P, CA * P), w["rwkv_aB"].reshape(L, P, CA * P)], 2),
        "rwkv_gB": w["rwkv_gB"],
        "lru_w": lru.transpose(0, 1, 4, 5, 2, 3, 6),
        "peer_wq": chunks(w["peer_wq"]),
        "peer_keys": w["peer_keys"].reshape(L, 2 * PH, NKEY, P).transpose(0, 3, 1, 2),
        "peer_u": w["peer_u"].reshape(L, NKEY, NKEY, KC, P).transpose(0, 2, 4, 3, 1),
        "peer_v": w["peer_v"].reshape(L, NKEY, NKEY * D),
    }
    arrays = {k: np.ascontiguousarray(a) for k, a in arrays.items()}
    nc = bacc.Bacc("TRN2", target_bir_lowering=False, num_devices=1)
    dram = {k: nc.dram_tensor(k, a.shape, F32, kind="ExternalInput").ap() for k, a in arrays.items()}
    outs = {
        "y": (P, KC, NT), "new_k": (L, P, CB, NPR), "new_v": (L, P, 512),
        "new_rwkv": (L, 2, HD, 2, CA, HD), "new_lru": (L, P, 2, CC),
    }
    for k, s in outs.items():
        dram[k] = nc.dram_tensor(k, s, F32, kind="ExternalOutput").ap()
    dram["gates"] = nc.dram_tensor("gates", (P, NG, NT // GT_N, GB * GT_N), F32, kind="Internal").ap()
    build(nc, dram)
    r = run_bass_kernel_spmd(nc, [arrays], core_ids=[0]).results[0]
    y = r["y"].transpose(2, 1, 0).reshape(NT, D)
    return (
        y[None, NS:], y[None, :NS],
        r["new_k"].transpose(0, 2, 1, 3).reshape(L, HB, HD, NPR).transpose(0, 1, 3, 2)[None],
        r["new_v"].reshape(L, NPR, HB, HD).transpose(0, 2, 1, 3)[None],
        r["new_rwkv"].transpose(0, 3, 4, 1, 5, 2).reshape(L, 2, HA, HD, HD)[None],
        r["new_lru"].transpose(0, 2, 3, 1).reshape(L, 2, CC * P)[None],
    )
```
